# Optimizing a Trainium2 kernel written in Bass

```python
import math
import jax
import jax.numpy as jnp
from jax import lax
import numpy as np
import jax, jax.numpy as jnp

D_MODEL = 1024
BATCH = 1
SEQ = 256
DEPTH = 1

HEAD_DIM = 64
MIX_WIDTH = D_MODEL
A_WIDTH = MIX_WIDTH // 2
B_WIDTH = MIX_WIDTH - A_WIDTH
A_HEADS = A_WIDTH // HEAD_DIM
B_HEADS = B_WIDTH // (2 * HEAD_DIM)
DIL_PATTERNS = ((128, 1), (512, 4), (2048, 16))
BAND_BLOCK = 128
Q_BLOCK = 128
N_EXPERTS = 32
TOP_K = 4
D_FF = D_MODEL
SWIGLU_LIMIT = 7.0
SWIGLU_ALPHA = 1.702
MOE_BLOCK = 128
RMS_EPS = 1e-6
ATTN_SCALE = HEAD_DIM ** -0.5
IN_SIZES = (A_WIDTH, A_WIDTH, A_WIDTH, B_WIDTH, B_WIDTH, B_WIDTH)
IN_WIDTH = sum(IN_SIZES)
IN_SPLITS = tuple(int(v) for v in np.cumsum(IN_SIZES)[:-1])


def rms_norm(x, g):
    xf = x.astype(jnp.float32)
    y = xf * lax.rsqrt(jnp.mean(xf * xf, axis=-1, keepdims=True) + RMS_EPS)
    return (y * g.astype(jnp.float32)).astype(x.dtype)

def alibi_slopes(n):
    return 2.0 ** (-8.0 * jnp.arange(1, n + 1, dtype=jnp.float32) / n)

def dilated_band_attention(q, k, v, slopes, window, dil):
    bsz, nh, n_tok, hd = q.shape
    L = n_tok // dil
    w_sub = window // dil
    nb = -(-L // BAND_BLOCK)
    Lp = nb * BAND_BLOCK

    def to_sub(t):
        t = jnp.swapaxes(t.reshape(bsz, nh, L, dil, hd), 2, 3)
        return jnp.pad(t, ((0, 0), (0, 0), (0, 0), (0, Lp - L), (0, 0)))

    def key_band(t):
        t = jnp.pad(to_sub(t), ((0, 0), (0, 0), (0, 0), (BAND_BLOCK, 0), (0, 0)))
        t = t.reshape(bsz, nh, dil, nb + 1, BAND_BLOCK, hd)
        return jnp.concatenate([t[:, :, :, :-1], t[:, :, :, 1:]], axis=4)

    qs = to_sub(q).reshape(bsz, nh, dil, nb, BAND_BLOCK, hd)
    ks, vs = key_band(k), key_band(v)
    iq = jnp.arange(BAND_BLOCK)[:, None]
    ik = jnp.arange(2 * BAND_BLOCK)[None, :]
    delta = iq - ik + BAND_BLOCK
    k_sub = (jnp.arange(nb)[:, None] * BAND_BLOCK - BAND_BLOCK
             + jnp.arange(2 * BAND_BLOCK)[None, :])
    valid = ((delta >= 0) & (delta <= w_sub))[None] & (k_sub >= 0)[:, None, :]
    bias = -slopes[:, None, None] * (delta * dil).astype(jnp.float32)[None]
    s = jnp.einsum('bhrnqd,bhrnkd->bhrnqk', qs, ks).astype(jnp.float32) * ATTN_SCALE
    s = s + bias[None, :, None, None]
    s = jnp.where(valid[None, None, None], s, -jnp.inf)
    m = jnp.max(s, axis=-1, keepdims=True)
    e = jnp.exp(s - m)
    den = jnp.sum(e, axis=-1, keepdims=True)
    o = jnp.einsum('bhrnqk,bhrnkd->bhrnqd', (e / den).astype(v.dtype), vs)
    lse = (m + jnp.log(den))[..., 0]

    def from_sub(t):
        tail = t.shape[5:]
        t = t.reshape((bsz, nh, dil, Lp) + tail)[:, :, :, :L]
        t = jnp.swapaxes(t, 2, 3)
        return t.reshape((bsz, nh, n_tok) + tail)

    return from_sub(o), from_sub(lse)

def dilated_mixture_attention(q, k, v, slopes):
    outs, lses = [], []
    for window, dil in DIL_PATTERNS:
        o, lse = dilated_band_attention(q, k, v, slopes, window, dil)
        outs.append(o)
        lses.append(lse)
    w = jax.nn.softmax(jnp.stack(lses, axis=0), axis=0)
    return jnp.einsum('pbhs,pbhsd->bhsd', w.astype(q.dtype), jnp.stack(outs, axis=0))

def differential_attention(q, k, v, slopes, lam):
    bsz, nh, n_tok, _, hd = q.shape
    nqb = n_tok // Q_BLOCK
    qb = jnp.moveaxis(q.reshape(bsz, nh, nqb, Q_BLOCK, 2, hd), 2, 0)
    k_pos = jnp.arange(n_tok)

    def block(args):
        q_blk, start = args
        dist = (start + jnp.arange(Q_BLOCK))[:, None] - k_pos[None, :]
        sc = jnp.einsum('bhqcd,bhkcd->bhcqk', q_blk, k).astype(jnp.float32) * ATTN_SCALE
        sc = sc - slopes[None, :, None, None, None] * dist.astype(jnp.float32)
        sc = jnp.where(dist >= 0, sc, -jnp.inf)
        p = jax.nn.softmax(sc, axis=-1)
        a = p[:, :, 0] - lam * p[:, :, 1]
        return jnp.einsum('bhqk,bhkd->bhqd', a.astype(v.dtype), v)

    o = lax.map(block, (qb, jnp.arange(nqb) * Q_BLOCK))
    return jnp.moveaxis(o, 0, 2).reshape(bsz, nh, n_tok, 2 * hd)

def moe_ffn(h, w_router, b_router, w_gate_up, b_gate_up, w_down, b_down):
    n, d = h.shape
    logits = (h @ w_router).astype(jnp.float32) + b_router.astype(jnp.float32)
    top_val, top_idx = lax.top_k(logits, TOP_K)
    gates = jax.nn.softmax(top_val, axis=-1)
    n_assign = n * TOP_K
    flat_e = top_idx.reshape(-1)
    order = jnp.argsort(flat_e)
    e_sorted = flat_e[order]
    tok_sorted = order // TOP_K
    gate_sorted = gates.reshape(-1)[order]
    counts = jnp.zeros((N_EXPERTS,), jnp.int32).at[flat_e].add(1)
    padded = (counts + MOE_BLOCK - 1) // MOE_BLOCK * MOE_BLOCK
    pad_end = jnp.cumsum(padded)
    pad_start = pad_end - padded
    grp_start = jnp.cumsum(counts) - counts
    dest = pad_start[e_sorted] + jnp.arange(n_assign) - grp_start[e_sorted]
    n_blocks = -(-(n_assign + N_EXPERTS * (MOE_BLOCK - 1)) // MOE_BLOCK)
    buf_tok = jnp.zeros((n_blocks * MOE_BLOCK,), jnp.int32).at[dest].set(tok_sorted)
    block_e = jnp.minimum(jnp.searchsorted(pad_end, jnp.arange(n_blocks) * MOE_BLOCK, side='right'),
                          N_EXPERTS - 1)
    xb = h[buf_tok].reshape(n_blocks, MOE_BLOCK, d)

    def expert_block(args):
        xe, e = args
        gu = xe @ w_gate_up[e] + b_gate_up[e]
        g = jnp.minimum(gu[:, :D_FF], SWIGLU_LIMIT)
        u = jnp.clip(gu[:, D_FF:], -SWIGLU_LIMIT, SWIGLU_LIMIT)
        act = (u + 1.0) * (g * jax.nn.sigmoid(SWIGLU_ALPHA * g))
        return act @ w_down[e] + b_down[e]

    yb = lax.map(expert_block, (xb, block_e)).reshape(-1, d)
    y = yb[dest] * gate_sorted[:, None].astype(yb.dtype)
    return jax.ops.segment_sum(y, tok_sorted, num_segments=n)

def hybrid_layer(x, c, w_ada, b_ada, norm1_g, w_in, a_q_norm_g, a_k_norm_g, b_q_norm_g,
                 b_k_norm_g, lambda_q1, lambda_k1, lambda_q2, lambda_k2, diff_norm_g, w_out,
                 norm2_g, w_router, b_router, w_gate_up, b_gate_up, w_down, b_down, lambda_init):
    bsz, n_tok, d = x.shape
    mod = jax.nn.silu(c) @ w_ada + b_ada
    shift1, scale1, gate1, shift2, scale2, gate2 = jnp.split(mod[:, None, :], 6, axis=-1)

    h = rms_norm(x, norm1_g) * (1.0 + scale1) + shift1
    proj = h @ w_in
    aq, ak, av, bq, bk, bv = jnp.split(proj, IN_SPLITS, axis=-1)

    def heads_a(t):
        return jnp.swapaxes(t.reshape(bsz, n_tok, A_HEADS, HEAD_DIM), 1, 2)

    aq = rms_norm(heads_a(aq), a_q_norm_g)
    ak = rms_norm(heads_a(ak), a_k_norm_g)
    o_a = dilated_mixture_attention(aq, ak, heads_a(av), alibi_slopes(A_HEADS))
    o_a = jnp.swapaxes(o_a, 1, 2).reshape(bsz, n_tok, A_WIDTH)

    def heads_b(t):
        return jnp.swapaxes(t.reshape(bsz, n_tok, B_HEADS, 2, HEAD_DIM), 1, 2)

    bq = rms_norm(heads_b(bq), b_q_norm_g)
    bk = rms_norm(heads_b(bk), b_k_norm_g)
    bv = jnp.swapaxes(bv.reshape(bsz, n_tok, B_HEADS, 2 * HEAD_DIM), 1, 2)
    lam = (jnp.exp(jnp.sum(lambda_q1.astype(jnp.float32) * lambda_k1.astype(jnp.float32)))
           - jnp.exp(jnp.sum(lambda_q2.astype(jnp.float32) * lambda_k2.astype(jnp.float32)))
           + lambda_init)
    o_b = differential_attention(bq, bk, bv, alibi_slopes(B_HEADS), lam)
    o_b = rms_norm(o_b, diff_norm_g) * (1.0 - lambda_init)
    o_b = jnp.swapaxes(o_b, 1, 2).reshape(bsz, n_tok, B_WIDTH)

    mixed = jnp.concatenate([o_a, o_b], axis=-1) @ w_out
    x = x + gate1 * mixed

    h2 = rms_norm(x, norm2_g) * (1.0 + scale2) + shift2
    y = moe_ffn(h2.reshape(bsz * n_tok, d), w_router, b_router, w_gate_up, b_gate_up,
                w_down, b_down).reshape(bsz, n_tok, d)
    return x + gate2 * y

def first_inputs(seed: int = 0) -> dict:
    key = jax.random.key(seed)
    ks = jax.random.split(key, 24)

    def nrm(k, shape, scale):
        return jax.random.normal(k, shape, jnp.float32) * scale

    def gain(k, shape):
        return 1.0 + nrm(k, shape, 0.05)

    L = DEPTH
    return {
        'x': nrm(ks[0], (BATCH, SEQ, D_MODEL), 1.0),
        'c': nrm(ks[1], (BATCH, D_MODEL), 1.0),
        'w_ada': nrm(ks[2], (L, D_MODEL, 6 * D_MODEL), 0.5 * D_MODEL ** -0.5),
        'b_ada': nrm(ks[3], (L, 6 * D_MODEL), 0.02),
        'norm1_g': gain(ks[4], (L, D_MODEL)),
        'w_in': nrm(ks[5], (L, D_MODEL, IN_WIDTH), D_MODEL ** -0.5),
        'a_q_norm_g': gain(ks[6], (L, HEAD_DIM)),
        'a_k_norm_g': gain(ks[7], (L, HEAD_DIM)),
        'b_q_norm_g': gain(ks[8], (L, HEAD_DIM)),
        'b_k_norm_g': gain(ks[9], (L, HEAD_DIM)),
        'lambda_q1': nrm(ks[10], (L, HEAD_DIM), 0.1),
        'lambda_k1': nrm(ks[11], (L, HEAD_DIM), 0.1),
        'lambda_q2': nrm(ks[12], (L, HEAD_DIM), 0.1),
        'lambda_k2': nrm(ks[13], (L, HEAD_DIM), 0.1),
        'diff_norm_g': gain(ks[14], (L, 2 * HEAD_DIM)),
        'w_out': nrm(ks[15], (L, MIX_WIDTH, D_MODEL), MIX_WIDTH ** -0.5),
        'norm2_g': gain(ks[16], (L, D_MODEL)),
        'w_router': nrm(ks[17], (L, D_MODEL, N_EXPERTS), D_MODEL ** -0.5),
        'b_router': nrm(ks[18], (L, N_EXPERTS), 0.01),
        'w_gate_up': nrm(ks[19], (L, N_EXPERTS, D_MODEL, 2 * D_FF), D_MODEL ** -0.5),
        'b_gate_up': nrm(ks[20], (L, N_EXPERTS, 2 * D_FF), 0.01),
        'w_down': nrm(ks[21], (L, N_EXPERTS, D_FF, D_MODEL), D_FF ** -0.5),
        'b_down': nrm(ks[22], (L, N_EXPERTS, D_MODEL), 0.01),
    }

def first_block(x, c, w_ada, b_ada, norm1_g, w_in, a_q_norm_g, a_k_norm_g, b_q_norm_g, b_k_norm_g,
              lambda_q1, lambda_k1, lambda_q2, lambda_k2, diff_norm_g, w_out, norm2_g, w_router,
              b_router, w_gate_up, b_gate_up, w_down, b_down):
    for l in range(DEPTH):
        lambda_init = 0.8 - 0.6 * math.exp(-0.3 * l)
        x = hybrid_layer(x, c, w_ada[l], b_ada[l], norm1_g[l], w_in[l], a_q_norm_g[l],
                         a_k_norm_g[l], b_q_norm_g[l], b_k_norm_g[l], lambda_q1[l], lambda_k1[l],
                         lambda_q2[l], lambda_k2[l], diff_norm_g[l], w_out[l], norm2_g[l],
                         w_router[l], b_router[l], w_gate_up[l], b_gate_up[l], w_down[l],
                         b_down[l], lambda_init)
    return x


DEPTH_2 = 2

GRID_W = 64
CTX_LEN = 256
N_Q_HEADS = 8
N_KV_HEADS = 2
GQA_GROUP = N_Q_HEADS // N_KV_HEADS
HEAD_DIM_2 = 128
ATTN_WIDTH = N_Q_HEADS * HEAD_DIM_2
KV_WIDTH = N_KV_HEADS * HEAD_DIM_2
ROPE_THETA = 10000.0
ROPE_FREQS = HEAD_DIM_2 // 4
ATTN_SCALE_2 = 1.0 / math.sqrt(HEAD_DIM_2)
GMLP_WIDTH = D_MODEL
GMLP_GROUPS = 4
GMLP_GROUP_DIM = GMLP_WIDTH // GMLP_GROUPS
CHUNK = 128
CONV_WIDTH = D_MODEL
CONV_KERNEL = 31
CONV_PAD = CONV_KERNEL // 2
N_BRANCHES = 3
D_FF_2 = 4 * D_MODEL
EPS = 1e-6
Q_OFF = 0
K_OFF = Q_OFF + ATTN_WIDTH
V_OFF = K_OFF + KV_WIDTH
GU_OFF = V_OFF + KV_WIDTH
GV_OFF = GU_OFF + GMLP_WIDTH
CG_OFF = GV_OFF + GMLP_WIDTH
GATE_OFF = CG_OFF + 2 * CONV_WIDTH
IN_COLS = GATE_OFF + N_BRANCHES * D_MODEL


def rms_norm_2(x, g):
    xf = x.astype(jnp.float32)
    y = xf * lax.rsqrt(jnp.mean(xf * xf, axis=-1, keepdims=True) + EPS)
    return (y * g.astype(jnp.float32)).astype(x.dtype)

def layer_norm(x, g, b):
    xf = x.astype(jnp.float32)
    mu = jnp.mean(xf, axis=-1, keepdims=True)
    var = jnp.mean(jnp.square(xf - mu), axis=-1, keepdims=True)
    y = (xf - mu) * lax.rsqrt(var + EPS)
    return (y * g.astype(jnp.float32) + b.astype(jnp.float32)).astype(x.dtype)

def modulate(h, shift, scale):
    return h * (1.0 + scale) + shift

def axial_rope_tables(n_rows):
    row = jnp.repeat(jnp.arange(n_rows), GRID_W).astype(jnp.float32)
    col = jnp.tile(jnp.arange(GRID_W), n_rows).astype(jnp.float32)
    inv = ROPE_THETA ** (-jnp.arange(ROPE_FREQS, dtype=jnp.float32) / ROPE_FREQS)
    ang = jnp.concatenate([row[:, None] * inv, col[:, None] * inv], axis=-1)
    return jnp.cos(ang), jnp.sin(ang)

def apply_rope(x, cos, sin):
    half = HEAD_DIM_2 // 2
    x1, x2 = x[..., :half], x[..., half:]
    c = cos[None, :, None, :].astype(x.dtype)
    s = sin[None, :, None, :].astype(x.dtype)
    return jnp.concatenate([x1 * c - x2 * s, x2 * c + x1 * s], axis=-1)

def q_heads(p, q_norm_g):
    B, L, _ = p.shape
    return rms_norm_2(p[..., Q_OFF:K_OFF].reshape(B, L, N_Q_HEADS, HEAD_DIM_2), q_norm_g)

def kv_heads(pkv, k_norm_g):
    B, L, _ = pkv.shape
    k = rms_norm_2(pkv[..., :KV_WIDTH].reshape(B, L, N_KV_HEADS, HEAD_DIM_2), k_norm_g)
    v = pkv[..., KV_WIDTH:].reshape(B, L, N_KV_HEADS, HEAD_DIM_2)
    return k, v

def gqa_attend(q, k, v):
    s = jnp.einsum('bqhgd,bkhd->bhgqk', q, k).astype(jnp.float32) * ATTN_SCALE_2
    p = jax.nn.softmax(s, axis=-1).astype(v.dtype)
    return jnp.einsum('bhgqk,bkhd->bqhgd', p, v)

def latent_attention(q, k_all, v_all):
    B, S = q.shape[0], q.shape[1]
    nb = S // Q_BLOCK
    qb = q.reshape(B, nb, Q_BLOCK, N_KV_HEADS, GQA_GROUP, HEAD_DIM_2).transpose(1, 0, 2, 3, 4, 5)
    ob = lax.map(lambda qi: gqa_attend(qi, k_all, v_all), qb)
    return ob.transpose(1, 0, 2, 3, 4, 5).reshape(B, S, ATTN_WIDTH)

def chunk_spatial_gate(u, v, ws, bs):
    B, L, _ = v.shape
    nc = L // CHUNK
    vg = v.reshape(B, nc, CHUNK, GMLP_GROUPS, GMLP_GROUP_DIM)
    sv = jnp.einsum('gpq,bnqgc->bnpgc', ws, vg) + bs.T[None, None, :, :, None]
    return u * sv.reshape(B, L, GMLP_WIDTH)

def conformer_conv(a, conv_w, conv_b, norm_g, norm_b, w_o):
    gl = a[..., :CONV_WIDTH] * jax.nn.sigmoid(a[..., CONV_WIDTH:])
    y = lax.conv_general_dilated(gl, conv_w[:, None, :], window_strides=(1,),
                                 padding=[(CONV_PAD, CONV_PAD)],
                                 dimension_numbers=('NWC', 'WIO', 'NWC'),
                                 feature_group_count=CONV_WIDTH) + conv_b
    y = jax.nn.silu(layer_norm(y, norm_g, norm_b))
    return y @ w_o

def mixer_merge(p, attn, w_attn_o, gmlp_norm_g, gmlp_ws, gmlp_bs, w_gmlp_o,
                conv_w, conv_b, conv_norm_g, conv_norm_b, w_conv_o, w_out):
    a_out = attn @ w_attn_o
    gu = jax.nn.gelu(p[..., GU_OFF:GV_OFF])
    gv = rms_norm_2(jax.nn.gelu(p[..., GV_OFF:CG_OFF]), gmlp_norm_g)
    g_out = chunk_spatial_gate(gu, gv, gmlp_ws, gmlp_bs) @ w_gmlp_o
    c_out = conformer_conv(p[..., CG_OFF:GATE_OFF], conv_w, conv_b, conv_norm_g, conv_norm_b, w_conv_o)
    gates = jax.nn.sigmoid(p[..., GATE_OFF:])
    ga = gates[..., :D_MODEL]
    gg = gates[..., D_MODEL:2 * D_MODEL]
    gc = gates[..., 2 * D_MODEL:]
    return (ga * a_out + gg * g_out + gc * c_out) @ w_out

def sq_relu_mlp(h, w1, w2):
    return jnp.square(jax.nn.relu(h @ w1)) @ w2

def second_inputs(seed: int = 0) -> dict:
    key = jax.random.key(seed)
    ks = jax.random.split(key, 32)
    f32 = jnp.float32

    def nrm(k, shape, scale):
        return jax.random.normal(k, shape, f32) * scale

    def gain(k, shape):
        return 1.0 + 0.1 * jax.random.normal(k, shape, f32)

    L = DEPTH_2
    return {
        'x': nrm(ks[0], (BATCH, SEQ, D_MODEL), 1.0),
        'c': nrm(ks[1], (BATCH, D_MODEL), 1.0),
        'ctx': nrm(ks[2], (BATCH, CTX_LEN, D_MODEL), 1.0),
        'c_ctx': nrm(ks[3], (D_MODEL,), 1.0),
        'ada_w': nrm(ks[4], (L, D_MODEL, 6 * D_MODEL), 0.5 * D_MODEL ** -0.5),
        'ada_b': nrm(ks[5], (L, 6 * D_MODEL), 0.02),
        'mix_pre_g': gain(ks[6], (L, D_MODEL)),
        'mix_post_g': gain(ks[7], (L, D_MODEL)),
        'w_in': nrm(ks[8], (L, D_MODEL, IN_COLS), D_MODEL ** -0.5),
        'q_norm_g': gain(ks[9], (L, HEAD_DIM_2)),
        'k_norm_g': gain(ks[10], (L, HEAD_DIM_2)),
        'w_attn_o': nrm(ks[11], (L, ATTN_WIDTH, D_MODEL), ATTN_WIDTH ** -0.5),
        'gmlp_norm_g': gain(ks[12], (L, GMLP_WIDTH)),
        'gmlp_ws': nrm(ks[13], (L, GMLP_GROUPS, CHUNK, CHUNK), CHUNK ** -0.5),
        'gmlp_bs': gain(ks[14], (L, GMLP_GROUPS, CHUNK)),
        'w_gmlp_o': nrm(ks[15], (L, GMLP_WIDTH, D_MODEL), GMLP_WIDTH ** -0.5),
        'conv_w': nrm(ks[16], (L, CONV_KERNEL, CONV_WIDTH), CONV_KERNEL ** -0.5),
        'conv_b': nrm(ks[17], (L, CONV_WIDTH), 0.02),
        'conv_norm_g': gain(ks[18], (L, CONV_WIDTH)),
        'conv_norm_b': nrm(ks[19], (L, CONV_WIDTH), 0.02),
        'w_conv_o': nrm(ks[20], (L, CONV_WIDTH, D_MODEL), CONV_WIDTH ** -0.5),
        'w_out': nrm(ks[21], (L, D_MODEL, D_MODEL), D_MODEL ** -0.5),
        'ffn_pre_g': gain(ks[22], (L, D_MODEL)),
        'ffn_post_g': gain(ks[23], (L, D_MODEL)),
        'w_ff1': nrm(ks[24], (L, D_MODEL, D_FF_2), D_MODEL ** -0.5),
        'w_ff2': nrm(ks[25], (L, D_FF_2, D_MODEL), D_FF_2 ** -0.5),
    }

def second_block(x, c, ctx, c_ctx, ada_w, ada_b, mix_pre_g, mix_post_g, w_in, q_norm_g, k_norm_g,
              w_attn_o, gmlp_norm_g, gmlp_ws, gmlp_bs, w_gmlp_o, conv_w, conv_b, conv_norm_g,
              conv_norm_b, w_conv_o, w_out, ffn_pre_g, ffn_post_g, w_ff1, w_ff2):
    B, S, _ = x.shape
    n_ctx = ctx.shape[1]
    ROWS = S // GRID_W
    cos, sin = axial_rope_tables(ROWS)
    xc = ctx
    for l in range(DEPTH_2):
        last = l == DEPTH_2 - 1
        mod = (jax.nn.silu(c) @ ada_w[l] + ada_b[l])[:, None, :]
        sh1, sc1, g1, sh2, sc2, g2 = jnp.split(mod, 6, axis=-1)
        modc = jax.nn.silu(c_ctx) @ ada_w[l] + ada_b[l]
        shc1, scc1, gc1, shc2, scc2, gc2 = jnp.split(modc, 6, axis=-1)

        h = modulate(rms_norm_2(x, mix_pre_g[l]), sh1, sc1)
        hc = modulate(rms_norm_2(xc, mix_pre_g[l]), shc1, scc1)
        p = h @ w_in[l]
        q = apply_rope(q_heads(p, q_norm_g[l]), cos, sin)
        k, v = kv_heads(p[..., K_OFF:GU_OFF], k_norm_g[l])
        k = apply_rope(k, cos, sin)
        if last:
            kc, vc = kv_heads(hc @ w_in[l][:, K_OFF:GU_OFF], k_norm_g[l])
        else:
            pc = hc @ w_in[l]
            qc = q_heads(pc, q_norm_g[l])
            kc, vc = kv_heads(pc[..., K_OFF:GU_OFF], k_norm_g[l])
        k_all = jnp.concatenate([kc, k], axis=1)
        v_all = jnp.concatenate([vc, v], axis=1)
        attn = latent_attention(q.reshape(B, S, N_KV_HEADS, GQA_GROUP, HEAD_DIM_2), k_all, v_all)
        y = mixer_merge(p, attn, w_attn_o[l], gmlp_norm_g[l], gmlp_ws[l], gmlp_bs[l], w_gmlp_o[l],
                        conv_w[l], conv_b[l], conv_norm_g[l], conv_norm_b[l], w_conv_o[l], w_out[l])
        x = x + g1 * rms_norm_2(y, mix_post_g[l])

        h2 = modulate(rms_norm_2(x, ffn_pre_g[l]), sh2, sc2)
        x = x + g2 * rms_norm_2(sq_relu_mlp(h2, w_ff1[l], w_ff2[l]), ffn_post_g[l])

        if not last:
            attn_c = gqa_attend(qc.reshape(B, n_ctx, N_KV_HEADS, GQA_GROUP, HEAD_DIM_2), kc, vc)
            yc = mixer_merge(pc, attn_c.reshape(B, n_ctx, ATTN_WIDTH), w_attn_o[l], gmlp_norm_g[l],
                             gmlp_ws[l], gmlp_bs[l], w_gmlp_o[l], conv_w[l], conv_b[l],
                             conv_norm_g[l], conv_norm_b[l], w_conv_o[l], w_out[l])
            xc = xc + gc1 * rms_norm_2(yc, mix_post_g[l])
            hc2 = modulate(rms_norm_2(xc, ffn_pre_g[l]), shc2, scc2)
            xc = xc + gc2 * rms_norm_2(sq_relu_mlp(hc2, w_ff1[l], w_ff2[l]), ffn_post_g[l])
    return x


def setup_inputs(seed=0):
    out = dict(first_inputs(seed))
    for name, value in second_inputs(seed + 1).items():
        if name != "x":
            out[name + "_2"] = value
    return out


def reference(
    x, c, w_ada, b_ada, norm1_g, w_in, a_q_norm_g, a_k_norm_g, b_q_norm_g, b_k_norm_g,
    lambda_q1, lambda_k1, lambda_q2, lambda_k2, diff_norm_g, w_out, norm2_g, w_router, b_router,
    w_gate_up, b_gate_up, w_down, b_down, c_2, ctx_2, c_ctx_2, ada_w_2, ada_b_2, mix_pre_g_2,
    mix_post_g_2, w_in_2, q_norm_g_2, k_norm_g_2, w_attn_o_2, gmlp_norm_g_2, gmlp_ws_2,
    gmlp_bs_2, w_gmlp_o_2, conv_w_2, conv_b_2, conv_norm_g_2, conv_norm_b_2, w_conv_o_2,
    w_out_2, ffn_pre_g_2, ffn_post_g_2, w_ff1_2, w_ff2_2,
):
    x = first_block(
        x, c, w_ada, b_ada, norm1_g, w_in, a_q_norm_g, a_k_norm_g, b_q_norm_g, b_k_norm_g,
        lambda_q1, lambda_k1, lambda_q2, lambda_k2, diff_norm_g, w_out, norm2_g, w_router,
        b_router, w_gate_up, b_gate_up, w_down, b_down,
    )
    return second_block(
        x, c_2, ctx_2, c_ctx_2, ada_w_2, ada_b_2, mix_pre_g_2, mix_post_g_2, w_in_2, q_norm_g_2,
        k_norm_g_2, w_attn_o_2, gmlp_norm_g_2, gmlp_ws_2, gmlp_bs_2, w_gmlp_o_2, conv_w_2,
        conv_b_2, conv_norm_g_2, conv_norm_b_2, w_conv_o_2, w_out_2, ffn_pre_g_2, ffn_post_g_2,
        w_ff1_2, w_ff2_2,
    )


_drawn_inputs = setup_inputs


def setup_inputs(seed=0):
    import zlib

    import numpy as np

    out = dict(_drawn_inputs(seed))
    spreads = {}
    factors = {'norm1_g': 2.817,
     'a_q_norm_g': 8.0,
     'a_k_norm_g': 8.0,
     'b_q_norm_g': 5.135,
     'b_k_norm_g': 4.755,
     'lambda_q1': 8.0,
     'lambda_q2': 2.914,
     'diff_norm_g': 4.555,
     'b_router': 4.59,
     'b_gate_up': 8.0,
     'b_down': 8.0,
     'ctx_2': 3.116,
     'q_norm_g_2': 8.0,
     'k_norm_g_2': 8.0,
     'conv_b_2': 7.909,
     'conv_norm_b_2': 8.0}
    for name, (base, spread) in spreads.items():
        noise = np.random.default_rng([zlib.crc32(name.encode()), seed]).standard_normal(out[name].shape)
        drawn = base * np.exp(spread * noise) if base else spread * noise
        out[name] = jnp.asarray(drawn.astype(out[name].dtype))
    for name, factor in factors.items():
        out[name] = (out[name] * factor).astype(out[name].dtype)
    return out
```

```python
from contextlib import ExitStack, contextmanager

import numpy as np

import concourse.bass as bass
from concourse import mybir

F32 = mybir.dt.float32
I32 = mybir.dt.int32
U32 = mybir.dt.uint32
ALU = mybir.AluOpType
ACT = mybir.ActivationFunctionType
AX = mybir.AxisListType.X

P = 128
D = 1024
KD = D // P
SEQ = 256
TT = SEQ // P
HD1 = 64
A_HEADS, B_HEADS = 8, 4
NE, TOPK = 32, 4
LIMIT, ALPHA = 7.0, 1.702
LAMBDA_INIT = 0.2
EPS = 1e-6
CAP = 96
NPASS = -(-SEQ // CAP)
RING = 6
CPE = 12
LAYERS = 2
H2, HD2, KV2 = 8, 128, 2
TAPS = 31
PADT = TAPS // 2
SEGW = SEQ + 2 * PADT
GELU_C = 2.0 * 0.7978845608028654

CH = {}


def _plan():
    c = 0

    def put(name, n):
        nonlocal c
        CH[name] = c
        c += n
    put("ada", 24)
    put("w_in", 12)
    put("w_out", 4)
    put("moe", NE * CPE)
    CH["after_moe"] = c
    for l in range(LAYERS):
        put(("ada", l), 24)
        put(("cg", l), 8)
        put(("gu", l), 4)
        put(("gv", l), 4)
        for br in ("gmlp", "attn", "conv"):
            if br == "attn":
                put(("qkv", l), 6)
            for n in range(2):
                put(("gate", br, l, n), 2)
                put(("out", br, l, n), 2)
        put(("w_out", l), 4)
        for h in range(2):
            put(("ff1", l, h), 8)
            put(("ff2", l, h), 8)
    CH["total"] = c


_plan()

COL = {}


def _cols():
    c = 0

    def put(name, n):
        nonlocal c
        COL[name] = c
        c += n
    put("cond", 24)
    put("b_ada", 48)
    put("norm1", 8)
    put("norm2", 8)
    put("qk_a", 2)
    put("qk_b", 2)
    put("diff", 1)
    for l in range(LAYERS):
        for n, w in (("ada_b", 48), ("mix_pre", 8), ("mix_post", 8), ("gmlp_norm", 8), ("conv_b", 8),
                     ("conv_g", 8), ("conv_nb", 8), ("ffn_pre", 8), ("ffn_post", 8), ("conv_w", TAPS * 8)):
            put((n, l), w)
    put("b_gu", NE * 16)
    COL["total"] = c


_cols()
ROW = {"lam": 0, "qk": 256, "bs": 256 + 512, "b_router": 256 + 512 + 1024, "total": 256 + 512 + 1024 + 32}
CST = {}


def _cst():
    c = 0
    for name, n in (("ident", 128), ("ones", 128), ("tri", 128), ("iota", CAP), ("iotae", NE), ("cos", 128),
                    ("sin", 256), ("distA", 384), ("distB", 384), ("cnt", 384)):
        CST[name] = c
        c += n
    CST["total"] = c


_cst()

AREA = 31456
NSTAT = 640


class Signals:

    def __init__(self, nc, ctx, known, per):
        self.nc, self.ctx, self.known, self.per = nc, ctx, known, per
        self.sems, self.count, self.marks, self.newper = {}, {}, {}, {}
        self.tag, self.i, self.prefix, self.asked = None, None, "", -1

    def sem(self, name):
        if name not in self.sems:
            self.sems[name] = self.ctx.enter_context(self.nc.semaphore(name))
        return self.sems[name]

    def mark(self, name, *keys, inc=1):
        name = self.prefix + name
        self.count[name] = self.count.get(name, 0) + inc
        for key in keys:
            assert (self.prefix, key) not in self.marks, key
            self.marks[self.prefix, key] = (name, self.count[name], self.tag)
        return self.sem(name), inc

    def at(self, key, lag=0):
        found = self.known.get((self.prefix, key)) or self.known.get(("", key))
        if found is None:
            assert not self.known, key
            return self.sem("unknown"), 1
        name, v, tag = found
        step, trips = self.per.get((tag, name), (0, 1))
        if tag is not None and tag == self.tag:
            v -= lag * step
            assert v >= 1, (key, v)
            return self.sem(name), self.i * step + v
        return self.sem(name), v + step * (trips - 1)

    def last(self, name):
        name = self.prefix + name
        if self.tag is None:
            return self.sem(name), self.count[name]
        return self.sem(name), self.i * self.per.get((self.tag, name), (1, 1))[0] + self.count[name]

    @contextmanager
    def loop(self, eng, tag, trips):
        start = dict(self.count)
        self.tag = self.prefix + tag
        with eng.Fori(0, trips) as i:
            self.i = i
            yield i
        for name, n in list(self.count.items()):
            d = n - start.get(name, 0)
            if d:
                self.newper[self.tag, name] = (d, trips)
                self.count[name] += d * (trips - 1)
        self.tag = None


def build(nc, args, known, per):
    stream, cols_d, rows_d, cst_d, x_d, ctx_d, ws_d, wr_d, bd_d, out_d = args
    with ExitStack() as ctx:
        def sb(name, shape, dt=F32):
            return ctx.enter_context(nc.sbuf_tensor(name, shape, dt))

        ring = sb("ring", [P, RING, 4, 512])
        cols = sb("cols", [P, COL["total"]])
        rows = sb("rows", [P, ROW["total"]])
        cst = sb("cst", [P, CST["total"]])
        ws = sb("ws", [P, LAYERS, 4, P])
        x = sb("x", [P, TT, D])
        mod = sb("mod", [P, 48])
        modb = sb("modb", [P, 2, 48])
        aff = sb("aff", [P, 8, KD])
        cond = sb("cond", [P, 24])
        stats = sb("stats", [P, NSTAT])
        area = sb("area", [P, AREA])
        flag = sb("flag", [P, 2], I32)
        idx = sb("idx", [P, TT, 8], U32)
        ps = ctx.enter_context(nc.psum_tensor("ps", [P, 8, 512], F32))
        K = Signals(nc, ctx, known, per)
        mark, at, last = K.mark, K.at, K.last
        landed = [K.sem(f"weights_landed{s}") for s in range(RING)]

        def v(off, *shape):
            n = int(np.prod(shape))
            assert off + n <= AREA, (off, n)
            ap = area[:, off:off + n]
            if len(shape) == 2:
                ap = ap.rearrange("p (a b) -> p a b", a=shape[0])
            if len(shape) == 3:
                ap = ap.rearrange("p (a b c) -> p a b c", a=shape[0], b=shape[1])
            return ap

        stat_at = {}
        stat_n = [0]

        def stat(key, n=1):
            if isinstance(key, tuple) and key[-1] in ("ms", "rt", "rstd"):
                key = key[:-1] + ("ssq",)
            if key not in stat_at:
                stat_at[key] = stat_n[0]
                stat_n[0] += n
                assert stat_n[0] <= NSTAT, stat_n
            return stats[:, stat_at[key]:stat_at[key] + n]

        def col(name, i=0, n=1):
            return cols[:, COL[name] + i:COL[name] + i + n]

        def con(name, n, off=0):
            return cst[:, CST[name] + off:CST[name] + off + n]

        ident, ones = con("ident", P), con("ones", P)

        B1 = 2048
        xn1 = v(B1, TT, D)
        hT1 = v(B1 + 2048, KD, SEQ)
        proj = v(B1 + 4096, TT, 3072)
        qkT = v(B1 + 10240, 4, 4, SEQ)
        o1 = v(B1 + 14336, TT, D)
        sbuf_s = v(B1 + 16384, 2, 384)
        sbuf_e = v(B1 + 17152, 4, 384)
        sbuf_p = v(B1 + 18688, 2, 384)
        sbuf_pt = v(B1 + 19456, 2, 384)
        junk1 = v(B1 + 20224, D)
        sq1 = v(B1 + 21248, 512)
        xT = v(B1 + 4096, KD, CAP)
        gbuf = v(B1 + 4864, 2, 4 * CAP)
        ubuf = v(B1 + 5632, 2, 4 * CAP)
        sbuf_g = v(B1 + 6400, 2, 4 * CAP)
        actb = v(B1 + 7168, KD, CAP)
        ysb = v(B1 + 7936, D)
        yacc = v(B1 + 8960, KD, SEQ)
        sel = v(B1 + 11008, TT, CAP)
        selg = v(B1 + 11200, TT, CAP)
        selgT = v(B1 + 11392, SEQ)
        slot = v(B1 + 11648, NE + 1, TT)
        gate = v(B1 + 11714, NE, TT)
        lgt = v(B1 + 11778, TT, NE)
        top8 = v(B1 + 11842, TT, 8)
        idxf = v(B1 + 11858, TT, 8)
        gex = v(B1 + 11874, TT, 8)
        pick = v(B1 + 11890, TT, NE)
        gpick = v(B1 + 11954, TT, NE)
        eqb = v(B1 + 12018, TT, NE)
        gateT = v(B1 + 12082, SEQ)
        wr = v(24000, KD, NE)
        bdn = v(24300, D)
        bgu = v(B1 + 13618, 16)
        ctxr = v(0, TT, D)
        hT = v(2048, KD, 512)
        merged = v(6144, KD, 512)
        glp = v(10240, KD, 2, SEGW)
        xnb = v(10240, 4, D)
        hid = v(10240, 16, 512)
        cv = v(14816, KD, 512)
        uT = v(18912, KD, 512)
        yb = v(18912, 4, D)
        gv = v(23008, 4, D)
        kT = v(23008, KV2, 512)
        vb = v(24032, 4, 256)
        bcv = v(25056, 2, D)
        tmp = v(27104, 8, 512)

        scr = v(25056, 4, 512)
        ptb = [v(25056, 4, SEQ), v(26080, 4, SEQ)]
        glsq = v(10240, KD, 512)
        dgb = v(31200, 2, P)
        condv = cond[:, 8:24].rearrange("p (s k) -> p k s", s=2)
        xn1v = v(B1, KD, SEQ)
        spill_landed = [K.sem(f"spill_weights_landed{s}") for s in range(RING)]
        units_of = {l: [(h, s) for h in range(H2) for s in range((4 - 2 * l) // 2)] for l in range(LAYERS)}

        junk1b = v(B1 + 20224, D)
        junkb = v(27104 + 2048, D)

        def gelu_items(l):
            nt = 4 if l == 0 else 2
            L = f"L{l}"
            return ([((( L, "gu"), f), uT[:, f, 0:nt * P], nt * P) for f in range(KD)]
                    + [(((L, "gv", g), t), gv[:, t, 512 * g:512 * g + 512], 512) for g in range(2) for t in range(nt)])

        bank_of, users = {}, {}
        block = ctx.enter_context(nc.Block())

        @block.tensor
        def _(pe):
            mm = nc.tensor.matmul
            nxt = {"acc": 0, "aux": 0}

            def claim(pool, key):
                b = (0 if pool == "acc" else 4) + nxt[pool] % 4
                nxt[pool] += 1
                if b in users:
                    pe.wait_ge(*at(("drained", users[b])))
                users[b] = key
                bank_of[key] = b
                return b

            def chunk(c):
                if c > K.asked:
                    pe.wait_ge(landed[c % RING], 16 * (c // RING + 1))
                    K.asked = c
                return ring[:, c % RING]

            def closed(ins, key, c, last_of_chunk, last_of_group):
                if last_of_chunk:
                    ins.then_inc(*mark("weights_used", ("chunk", c), *([("full", key)] if last_of_group else [])))
                elif last_of_group:
                    ins.then_inc(*mark("product_full", ("full", key)))

            def features(first, kgs, rhs, n, key, j0=0, nb=4):
                for j in range(nb):
                    b = claim("acc", (key, j0 + j))
                    for k in range(4 * kgs):
                        w = chunk(first + k // 4)
                        i = mm(ps[:, b, 0:n], w[:, k % 4, j * P:(j + 1) * P], rhs(k),
                               start=(k == 0), stop=(k == 4 * kgs - 1))
                        closed(i, (key, j0 + j), first + k // 4, j == nb - 1 and k % 4 == 3, k == 4 * kgs - 1)

            def tokens(first, kgs, lhs, tiles, key):
                for t in range(tiles):
                    b = claim("acc", (key, t))
                    for k in range(4 * kgs):
                        w = chunk(first + k // 4)
                        i = mm(ps[:, b, :], lhs(k, t), w[:, k % 4, :], start=(k == 0), stop=(k == 4 * kgs - 1))
                        closed(i, (key, t), first + k // 4, t == tiles - 1 and k % 4 == 3, k == 4 * kgs - 1)

            def ada(first, rhs, n, key):
                b = claim("aux", key)
                for g in range(12):
                    for j in range(4):
                        f = g * 4 + j
                        for k in range(KD):
                            c = first + 2 * g + k // 4
                            i = mm(ps[:, b, f * n:(f + 1) * n], chunk(c)[:, k % 4, j * P:(j + 1) * P], rhs(k),
                                   start=(k == 0), stop=(k == KD - 1))
                            closed(i, key, c, j == 3 and k % 4 == 3, g == 11 and j == 3 and k == KD - 1)

            def turn(src, key, n, ready):
                b = claim("aux", key)
                for r in ready:
                    pe.wait_ge(*at(r))
                for j in range(n):
                    i = nc.tensor.transpose(ps[:, b, j * P:(j + 1) * P], src(j), ident)
                i.then_inc(*mark("turned", ("full", key)))

            pe.wait_ge(*at("cst"))
            pe.wait_ge(*at("cond"))
            ada(CH["ada"], lambda k: cond[:, k:k + 1], 1, "ada")
            for k in range(KD):
                turn(lambda t: xn1[:, t, k * P:(k + 1) * P], ("h1", k), TT, ["xn1"])
            for k in range(KD):
                pe.wait_ge(*at(("drained", ("h1", k))))
            for g in range(6):
                tokens(CH["w_in"] + 2 * g, 2, lambda k, t: hT1[:, k, t * P:(t + 1) * P], TT, ("proj", g))
            for m in range(4):
                for t in range(TT):
                    c0 = (0, 512, 1536, 2048)[m] + 0
                    turn(lambda j: proj[:, t, c0 + j * P:c0 + (j + 1) * P], ("qk", m, t), 4, [("qkn", m)])

            def head(key, q, k, hp, lo):
                b = claim("acc", key)
                for m in (q, k):
                    for t in range(TT):
                        pe.wait_ge(*at(("drained", ("qk", m, t))))
                for t in range(TT):
                    n = P * (t + 1)
                    i = mm(ps[:, b, P * t:P * t + n], qkT[lo:lo + HD1, q, hp, t * P:(t + 1) * P],
                           qkT[lo:lo + HD1, k, hp, 0:n], start=True, stop=True)
                i.then_inc(*mark("scores_full", ("full", key)))

            def weigh(key, vcol, n):
                turn(lambda j: sbuf_p[:, key[1] % 2, j * P:(j + 1) * P], ("pt",) + key, 3, [("prob",) + key])
                b = claim("aux", ("o",) + key)
                pe.wait_ge(*at(("drained", ("pt",) + key)))
                pt = sbuf_pt[:, key[1] % 2]
                for t in range(TT):
                    for s in range(t + 1):
                        i = mm(ps[:, b, t * n:(t + 1) * n], pt[:, (t + s) * P:(t + s + 1) * P],
                               proj[:, s, vcol:vcol + n], start=(s == 0), stop=(s == t))
                i.then_inc(*mark("heads_full", ("full", ("o",) + key)))

            for h in range(A_HEADS + 1):
                if h < A_HEADS:
                    head(("A", h), 0, 1, h // 2, HD1 * (h % 2))
                if h:
                    weigh(("A", h - 1), 1024 + HD1 * (h - 1), HD1)
            for h in range(B_HEADS + 1):
                if h < B_HEADS:
                    for c in range(2):
                        head(("B", h, c), 2, 3, h, HD1 * c)
                if h:
                    weigh(("B", h - 1), 2560 + P * (h - 1), P)
            for k in range(KD):
                turn(lambda t: o1[:, t, k * P:(k + 1) * P], ("oT", k), TT, ["oA" if k < 4 else "oB"])
            for k in range(KD):
                pe.wait_ge(*at(("drained", ("oT", k))))
            for g in range(2):
                features(CH["w_out"] + 2 * g, 2, lambda k: hT1[:, k, :], SEQ, "mix", 4 * g)
            for t in range(TT):
                for g in range(2):
                    turn(lambda j: xn1v[:, 4 * g + j, t * P:(t + 1) * P], ("mixT", t, g), 4,
                         [("drained", ("mix", 4 * g + 3)), ("drained", ("mix", 4 * g + 2))])
            for k in range(KD):
                turn(lambda t: xn1[:, t, k * P:(k + 1) * P], ("h2", k), TT, ["xn2"])
            b = claim("aux", "logits")
            for k in range(KD):
                pe.wait_ge(*at(("drained", ("h2", k))))
            pe.wait_ge(*at("wr"))
            for t in range(TT):
                for k in range(KD):
                    i = mm(ps[:, b, t * NE:(t + 1) * NE], hT1[:, k, t * P:(t + 1) * P], wr[:, k, :],
                           start=(k == 0), stop=(k == KD - 1))
            i.then_inc(*mark("router_full", ("full", "logits")))
            b = claim("aux", "rank")
            pe.wait_ge(*at("pick"))
            for t in range(TT):
                if t:
                    mm(ps[:, b, t * NE:(t + 1) * NE], ones, pick[:, 0, :], start=True, stop=False)
                mm(ps[:, b, t * NE:(t + 1) * NE], con("tri", P), pick[:, t, :], start=(t == 0), stop=True)
            for t in range(TT):
                i = mm(ps[:, b, 2 * NE:3 * NE], ones, pick[:, t, :], start=(t == 0), stop=(t == TT - 1))
            i.then_inc(*mark("router_full", ("full", "rank")))
            b = claim("aux", "gateT")
            pe.wait_ge(*at("gpick"))
            for t in range(TT):
                i = nc.tensor.transpose(ps[0:NE, b, t * P:(t + 1) * P], gpick[:, t, :], ident)
            i.then_inc(*mark("router_full", ("full", "gateT")))
            pe.wait_ge(*at(("drained", "gateT")))
            pe.wait_ge(*at("bdn"))
            for g in range(4):
                b = claim("aux", ("bias", g))
                for j in range(2):
                    i = mm(ps[:, b, j * SEQ:(j + 1) * SEQ], bdn[0:NE, (2 * g + j) * P:(2 * g + j + 1) * P],
                           gateT[0:NE, :], start=True, stop=True)
                i.then_inc(*mark("router_full", ("full", ("bias", g))))

            for key in [k for k in users.values()]:
                pe.wait_ge(*at(("drained", key)))

            def expert_chunk(ci, wait_it):
                s = (CH["moe"] + ci) % RING
                if wait_it:
                    if K.prefix:
                        base = 16 * (2 * NE * (K.spill_pass) + ci // RING + 1)
                        pe.wait_ge(spill_landed[s], K.i * 32 + base)
                    else:
                        pe.wait_ge(landed[s], K.i * 32 + 16 * ((CH["moe"] + ci) // RING + 1))
                return ring[:, s]

            def gather(gk):
                for g in range(2):
                    for j in range(4):
                        k = 4 * g + j
                        for t in range(TT):
                            i = mm(ps[:, 4 + g, j * CAP:(j + 1) * CAP], xn1[:, t, k * P:(k + 1) * P],
                                   sel[:, t, :], start=(t == 0), stop=(t == TT - 1))
                    i.then_inc(*mark("gather_full", ("full", (gk, g))))

            def scatter(lag_tag, first_wait):
                for g in range(4):
                    b = (6, 7, 4, 5)[g]
                    first_wait(g)
                    for j in range(2):
                        k = 2 * g + j
                        i = mm(ps[:, b, j * SEQ:(j + 1) * SEQ], ysb[0:CAP, k * P:(k + 1) * P],
                               selgT[0:CAP, :], start=True, stop=True)
                    i.then_inc(*mark("scatter_full", ("full", (lag_tag, g))))

            def experts(tag):
                pe.wait_ge(*at(("sel0", tag)))
                gather(("g0", tag))
                with K.loop(pe, tag, NE):
                    for g in range(4):
                        if g < 2:
                            pe.wait_ge(*at((tag, "xT", g), lag=1))
                        if g == 0:
                            pe.wait_ge(*at((tag, "selgT"), lag=1))
                            pe.wait_ge(*at((tag, "xT", 1), lag=1))
                        pe.wait_ge(*at((tag, "h", g), lag=1))
                        for j in range(4):
                            for k in range(KD):
                                ci = 2 * g + k // 4
                                w = expert_chunk(ci, j == 0 and k % 4 == 0)
                                i = mm(ps[:, g, j * CAP:(j + 1) * CAP], w[:, k % 4, j * P:(j + 1) * P], xT[:, k, :],
                                       start=(k == 0), stop=(k == KD - 1))
                                if j == 3 and k % 4 == 3:
                                    i.then_inc(*mark("weights_used", (tag, "chunk", ci)))
                    pe.wait_ge(*at((tag, "sel")))
                    pe.wait_ge(*at((tag, "y+", 3), lag=1))
                    gather((tag, "g"))
                    def bank_read(g):
                        if g == 0:
                            pe.wait_ge(*at((tag, "y", 1), lag=1))
                        if g == 2:
                            pe.wait_ge(*at((tag, "xT", 1)))
                    scatter((tag, "s"), bank_read)
                    pe.wait_ge(*at((tag, "selg")))
                    pe.wait_ge(*at((tag, "h", 0)))
                    for t in range(TT):
                        i = nc.tensor.transpose(ps[0:CAP, 0, t * P:(t + 1) * P], selg[:, t, :], ident)
                    i.then_inc(*mark("gather_full", (tag, "selT")))
                    pe.wait_ge(*at((tag, "act", 1)))
                    for g in range(2):
                        pe.wait_ge(*at((tag, "y+", g)))
                        for k in range(KD):
                            ci = 8 + 2 * g + k // 4
                            w = expert_chunk(ci, k % 4 == 0)
                            i = mm(ps[0:CAP, 6 + g, :], actb[:, k, :], w[:, k % 4, :],
                                   start=(k == 0), stop=(k == KD - 1))
                            if k % 4 == 3:
                                i.then_inc(*mark("weights_used", (tag, "chunk", ci)))

                def last_read(g):
                    if g == 0:
                        pe.wait_ge(*at((tag, "y", 1)))
                        pe.wait_ge(*at((tag, "selgT")))
                    if g == 2:
                        pe.wait_ge(*at((tag, "y+", 3)))
                scatter(("s_end", tag), last_read)

            pe.wait_ge(*at(("zero", "moe")))
            experts("moe")
            pe.wait_ge(*at("flag"))
            over = nc.tensor.value_load(flag[0:1, 0:1], min_val=0, max_val=1)
            with nc.tensor.If(over > 0):
                K.prefix = "spill_"
                for p in range(1, NPASS):
                    K.spill_pass = p - 1
                    pe.wait_ge(*at(("y_end", f"moe{p - 1}" if p > 1 else "moe", 3)))
                    pe.wait_ge(*at(("zero", f"moe{p}")))
                    experts(f"moe{p}")
                pe.wait_ge(*at(("y_end", f"moe{NPASS - 1}", 3)))
                K.prefix = ""
            users.clear()
            for t in range(TT):
                for g in range(2):
                    turn(lambda j: yacc[:, 4 * g + j, t * P:(t + 1) * P], ("moeT", t, g), 4, ["yg"])

            for l in range(LAYERS):
                nt = 4 if l == 0 else 2
                N = nt * P
                L = f"L{l}"
                ada(CH["ada", l], lambda k: condv[:, k, :], 2, (L, "ada"))
                for k in range(KD):
                    turn(lambda t: xnb[:, t, k * P:(k + 1) * P], (L, "h", k), 4, [(L, "xn")])
                for k in range(KD):
                    pe.wait_ge(*at(("drained", (L, "h", k))))
                hx = lambda k: hT[:, k, 0:N]
                for g in range(4):
                    features(CH["cg", l] + 2 * g, 2, hx, N, (L, "cg"), 4 * g)
                for g in range(2):
                    features(CH["gu", l] + 2 * g, 2, hx, N, (L, "gu"), 4 * g)
                for g in range(2):
                    tokens(CH["gv", l] + 2 * g, 2, lambda k, t: hT[:, k, t * P:(t + 1) * P], nt, (L, "gv", g))
                pe.wait_ge(*at("ws"))
                for f in range(KD):
                    b = claim("aux", (L, "sv", f))
                    pe.wait_ge(*at((L, "gvn")))
                    for t in range(nt):
                        i = mm(ps[:, b, t * P:(t + 1) * P], gv[:, t, f * P:(f + 1) * P], ws[:, l, f // 2, :],
                               start=True, stop=True)
                    i.then_inc(*mark("mixed_full", ("full", (L, "sv", f))))

                def branch(br, src, ready, between=None):
                    for g in range(2):
                        if g and between:
                            between()
                        features(CH["gate", br, l, g], 2, hx, N, (L, "gate", br), 4 * g)
                        if g == 0:
                            for r in ready:
                                pe.wait_ge(*at(r))
                        features(CH["out", br, l, g], 2, lambda k: src[:, k, 0:N], N, (L, "out", br), 4 * g)
                branch("gmlp", uT, [(L, "usv", f) for f in range(KD)])
                for g in range(3):
                    tokens(CH["qkv", l] + 2 * g, 2, lambda k, t: hT[:, k, t * P:(t + 1) * P],
                           4 if g == 2 else nt, (L, "qkv", g))
                    for t in range(nt if g else 0):
                        turn(lambda j: tmp[:, t, j * P:(j + 1) * P], (L, "q", g - 1, t), 4, [(L, "qr", g - 1, t)])
                for t in range(4):
                    turn(lambda j: tmp[:, 4 + t % 4, j * P:(j + 1) * P], (L, "k", t), 2, [(L, "kr", t)])

                def attend(h, seg):
                    nk = 4 if seg == 0 else 2
                    k0 = 0 if seg == 0 else 2
                    key = (L, h, seg)
                    for t in range(TT):
                        b = claim("acc", (key, "s", t))
                        for tt in range(4):
                            pe.wait_ge(*at(("drained", (L, "k", tt))))
                        pe.wait_ge(*at(("drained", (L, "q", h // 4, 2 * seg + t))))
                        i = mm(ps[:, b, 0:nk * P], uT[:, h, (2 * seg + t) * P:(2 * seg + t + 1) * P],
                               kT[:, h // 4, k0 * P:(k0 + nk) * P], start=True, stop=True)
                        i.then_inc(*mark("scores_full", ("full", (key, "s", t))))

                def average(h, seg):
                    nk = 4 if seg == 0 else 2
                    k0 = 0 if seg == 0 else 2
                    key = (L, h, seg)
                    par = units_of[l].index((h, seg)) % 2
                    for t in range(TT):
                        turn(lambda j: tmp[:, 2 * par + t, j * P:(j + 1) * P], (key, "pt", t), nk, [(key, "p", t)])
                    b = claim("aux", (key, "o"))
                    for t in range(TT):
                        pe.wait_ge(*at(("drained", (key, "pt", t))))
                    for j in range(nk):
                        i = mm(ps[:, b, 0:SEQ], vb[:, k0 + j, (h // 4) * P:(h // 4 + 1) * P], ptb[par][:, j, :],
                               start=(j == 0), stop=(j == nk - 1))
                    i.then_inc(*mark("heads_full", ("full", (key, "o"))))
                units = [(h, s) for h in range(H2) for s in range(nt // 2)]
                for n in range(len(units) + 1):
                    if n < len(units):
                        attend(*units[n])
                    if n:
                        average(*units[n - 1])
                def feature_sum(which, src, ready):
                    b = claim("aux", (L, which))
                    for k in range(KD):
                        pe.wait_ge(*at((L, ready, k)))
                        i = mm(ps[:, b, 0:N], ones, src[:, k, 0:N], start=(k == 0), stop=(k == KD - 1))
                    i.then_inc(*mark("mixed_full", ("full", (L, which))))
                feature_sum("mu", cv, "cv")
                branch("attn", uT, [("drained", ((L, h, s), "o")) for h, s in units],
                       lambda: feature_sum("var", glsq, "cvsq"))
                branch("conv", cv, [(L, "cvn", k) for k in range(KD)])
                for k in range(KD):
                    pe.wait_ge(*at((L, "merged", k)))
                for g in range(2):
                    tokens(CH["w_out", l] + 2 * g, 2, lambda k, t: merged[:, k, t * P:(t + 1) * P], nt, (L, "wo", g))

                def spread(which):
                    for s in range(nt // 2):
                        for g in range(2):
                            b = claim("aux", (L, "bc", which, s, g))
                            for j in range(4):
                                k = 4 * g + j
                                pe.wait_ge(*at((L, "dg", which, s, k)))
                                i = mm(ps[:, b, j * P:(j + 1) * P], ones, dgb[:, k % 2], start=True, stop=True)
                                i.then_inc(*mark("spread_full", (L, "bcm", which, s, k), *([("full", (L, "bc", which, s, g))] if j == 3 else [])))
                spread(0)
                for k in range(KD):
                    turn(lambda t: xnb[:, t, k * P:(k + 1) * P], (L, "h2", k), nt, [(L, "xn2")])
                for k in range(KD):
                    pe.wait_ge(*at(("drained", (L, "h2", k))))
                for hf in range(2):
                    for g in range(4):
                        features(CH["ff1", l, hf] + 2 * g, 2, hx, N, (L, "ff1", hf), 4 * g)
                    for j in range(16):
                        pe.wait_ge(*at((L, "hid", hf, j)))
                    for g in range(2):
                        tokens(CH["ff2", l, hf] + 4 * g, 4, lambda k, t: hid[:, k, t * P:(t + 1) * P], nt, (L, "ff2", hf, g))
                spread(1)
            return


        @block.vector
        def _(dve):
            V = nc.vector
            TS, TT_, STT = V.tensor_scalar, V.tensor_tensor, V.scalar_tensor_tensor

            def B(key):
                return bank_of[key]

            def rstd_of(key, n, width):
                dve.wait_ge(*at(("ssq", key)))
                TS(stat((key, "ms"), n), stat((key, "ssq"), n), 1.0 / width, EPS, ALU.mult, ALU.add).then_inc(*mark("means_ready", ("ms", key)))
                dve.wait_ge(*at(("root", key)))
                V.reciprocal(stat((key, "rstd"), n), stat((key, "rt"), n)).then_inc(*mark("vector_steps"))
                dve.wait_ge(*last("vector_steps"))
                return stat((key, "rstd"), n)

            dve.wait_ge(*at("cols"))
            dve.wait_ge(*at("cond_sig"))
            TT_(cond[:, :], cond[:, :], col("cond", 0, 24), ALU.mult).then_inc(*mark("cond_ready", "cond"))
            r = rstd_of("x1", TT, D)
            for t in range(TT):
                i = TS(xn1[:, t, :], x[:, t, :], r[:, t:t + 1], None, ALU.mult)
            i.then_inc(*mark("normed", "xn1"))
            dve.wait_ge(*at("rows"))
            for l in range(LAYERS):
                q = rows[:, ROW["qk"] + 256 * l:ROW["qk"] + 256 * l + P]
                TS(q, q, HD2 ** -0.5, None, ALU.mult).then_inc(*mark("vector_steps"))
                dve.wait_ge(*last("vector_steps"))
            lam = rows[:, 0:256].rearrange("p (a d) -> p a d", a=4)
            for m in range(2):
                TT_(junk1[:, 64 * m:64 * m + 64], lam[:, 2 * m], lam[:, 2 * m + 1], ALU.mult).then_inc(*mark("vector_steps"))
                dve.wait_ge(*last("vector_steps"))
            V.tensor_reduce(stat("ldot", 2), junk1[:, 0:128].rearrange("p (a d) -> p a d", a=2), AX, ALU.add).then_inc(*mark("lambda_dots", "ldot"))
            dve.wait_ge(*at("lexp"))
            TT_(stat("lam"), stat("lexp", 2)[:, 0:1], stat("lexp", 2)[:, 1:2], ALU.subtract).then_inc(*mark("vector_steps"))
            dve.wait_ge(*last("vector_steps"))
            TS(stat("lam"), stat("lam"), LAMBDA_INIT, None, ALU.add).then_inc(*mark("vector_steps"))
            dve.wait_ge(*last("vector_steps"))

            dve.wait_ge(*at(("full", "ada")))
            TT_(mod[:, :], ps[:, B("ada"), 0:48], col("b_ada", 0, 48), ALU.add).then_inc(*mark("vector_steps", ("drained", "ada")))
            dve.wait_ge(*last("vector_steps"))
            STT(aff[:, 0], mod[:, 8:16], 1.0, col("norm1", 0, 8), ALU.add, ALU.mult).then_inc(*mark("vector_steps"))
            dve.wait_ge(*last("vector_steps"))
            STT(aff[:, 1], mod[:, 32:40], 1.0, col("norm2", 0, 8), ALU.add, ALU.mult).then_inc(*mark("vector_steps"))
            dve.wait_ge(*last("vector_steps"))

            def modulate(name, A, sh):
                for k in range(KD):
                    dve.wait_ge(*at(("full", (name, k))))
                    TS(hT1[:, k, :], ps[:, B((name, k)), 0:SEQ], aff[:, A, k:k + 1], mod[:, sh + k:sh + k + 1],
                            ALU.mult, ALU.add).then_inc(*mark("modulated", ("drained", (name, k))))
            modulate("h1", 0, 0)

            heads = lambda m, t: proj[:, t, (0, 512, 1536, 2048)[m]:(0, 512, 1536, 2048)[m] + 512].rearrange(
                "p (h d) -> p h d", d=HD1)
            for m in range(4):
                for t in range(TT):
                    dve.wait_ge(*at(("drained", (("proj", (0, 1, 3, 4)[m]), t))))
                    TT_(sq1.rearrange("p (h d) -> p h d", d=HD1), heads(m, t), heads(m, t), ALU.mult).then_inc(*mark("vector_steps"))
                    dve.wait_ge(*last("vector_steps"))
                    V.tensor_reduce(stat((("qk", m), "ssq"), 16)[:, 8 * t:8 * t + 8],
                                         sq1.rearrange("p (h d) -> p h d", d=HD1), AX, ALU.add).then_inc(*mark("vector_steps", *([("ssq", ("qk", m))] if t else [])))
                    dve.wait_ge(*last("vector_steps"))
                r = rstd_of(("qk", m), 16, HD1)
                for t in range(TT):
                    i = TT_(heads(m, t), heads(m, t), r[:, 8 * t:8 * t + 8].unsqueeze(2).to_broadcast([P, 8, HD1]), ALU.mult)
                i.then_inc(*mark("normed", ("qkn", m)))
            for m in range(4):
                for t in range(TT):
                    dve.wait_ge(*at(("full", ("qk", m, t))))
                    g = col("qk_a" if m < 2 else "qk_b", m % 2)
                    TS(qkT[:, m, :, t * P:(t + 1) * P],
                            ps[:, B(("qk", m, t)), :].rearrange("p (a q) -> p a q", a=4), g,
                            HD1 ** -0.5 if m % 2 == 0 else 1.0, ALU.mult, ALU.mult).then_inc(*mark("turned_read", ("drained", ("qk", m, t))))

            def masked(key, dist, slope, sb_):
                dve.wait_ge(*at(("full", key)))
                STT(sbuf_s[:, sb_], con(dist, 384), -slope, ps[:, B(key), 0:384], ALU.mult, ALU.add).then_inc(*mark("vector_steps", ("drained", key)))
                dve.wait_ge(*last("vector_steps"))
                for t in range(TT):
                    i = V.tensor_reduce(stat((key, "nm"), 2)[:, t:t + 1], sbuf_s[:, sb_, P * t:P * t + P * (t + 1)],
                                        AX, ALU.max, negate=True)
                i.then_inc(*mark("maxima_ready", ("nm", key)))

            def outA(h):
                key = ("o", "A", h)
                dve.wait_ge(*at(("full", key)))
                i = TT_(o1[:, :, HD1 * h:HD1 * h + HD1], ps[:, B(key), 0:128].rearrange("p (t d) -> p t d", t=TT),
                        stat((("A", h), "rden"), 2).unsqueeze(2).to_broadcast([P, TT, HD1]), ALU.mult)
                i.then_inc(*mark("heads_read", ("drained", key), *(["oA"] if h == A_HEADS - 1 else [])))

            def turned_prob(key):
                dve.wait_ge(*at(("full", ("pt",) + key)))
                V.tensor_copy(sbuf_pt[:, key[1] % 2], ps[:, B(("pt",) + key), 0:384]).then_inc(*mark("turned_read", ("drained", ("pt",) + key)))

            for h in range(A_HEADS + 1):
                if h < A_HEADS:
                    masked(("A", h), "distA", 2.0 ** -(h + 1), h % 2)
                if h:
                    turned_prob(("A", h - 1))
                if h < A_HEADS:
                    dve.wait_ge(*at(("exp", ("A", h))))
                    for t in range(TT):
                        sl = slice(P * t, P * t + P * (t + 1))
                        i = V.tensor_tensor_reduce(sbuf_p[:, h % 2, sl], sbuf_e[:, h % 4, sl], con("cnt", 384)[:, sl], 1.0, 0.0,
                                                   ALU.mult, ALU.add, stat((("A", h), "den"), 2)[:, t:t + 1])
                    i.then_inc(*mark("vector_steps", ("prob", "A", h)))
                    dve.wait_ge(*last("vector_steps"))
                    V.reciprocal(stat((("A", h), "rden"), 2), stat((("A", h), "den"), 2)).then_inc(*mark("vector_steps"))
                    dve.wait_ge(*last("vector_steps"))
                if h:
                    outA(h - 1)

            def outB(h):
                key = ("o", "B", h)
                dve.wait_ge(*at(("full", key)))
                ov = o1[:, :, 512 + P * h:512 + P * h + P]
                V.tensor_copy(ov, ps[:, B(key), 0:256].rearrange("p (t d) -> p t d", t=TT)).then_inc(*mark("vector_steps", ("drained", key)))
                dve.wait_ge(*last("vector_steps"))
                sv_ = sq1[:, 0:256].rearrange("p (t d) -> p t d", t=TT)
                TT_(sv_, ov, ov, ALU.mult).then_inc(*mark("vector_steps"))
                dve.wait_ge(*last("vector_steps"))
                V.tensor_reduce(stat(("oB", "ssq"), 8).rearrange("p (t h) -> p h t", h=4)[:, h], sv_, AX, ALU.add).then_inc(*mark("vector_steps", *([("ssq", "oB")] if h == B_HEADS - 1 else [])))
                dve.wait_ge(*last("vector_steps"))

            for h in range(B_HEADS + 1):
                if h < B_HEADS:
                    for c in range(2):
                        masked(("B", h, c), "distB", 2.0 ** (-2 * (h + 1)), c)
                if h:
                    turned_prob(("B", h - 1))
                if h < B_HEADS:
                    for c in range(2):
                        dve.wait_ge(*at(("exp", ("B", h, c))))
                        V.reciprocal(stat(("B", h, c, "rd"), 2), stat((("B", h, c), "den"), 2)).then_inc(*mark("vector_steps"))
                        dve.wait_ge(*last("vector_steps"))
                    rd0, rd1 = stat(("B", h, 0, "rd"), 2), stat(("B", h, 1, "rd"), 2)
                    TS(rd1, rd1, stat("lam"), None, ALU.mult).then_inc(*mark("vector_steps"))
                    dve.wait_ge(*last("vector_steps"))
                    e0, e1 = 2 * (h % 2), 2 * (h % 2) + 1
                    for t in range(TT):
                        sl = slice(P * t, P * t + P * (t + 1))
                        TS(sbuf_e[:, e1, sl], sbuf_e[:, e1, sl], rd1[:, t:t + 1], None, ALU.mult).then_inc(*mark("vector_steps"))
                        dve.wait_ge(*last("vector_steps"))
                        STT(sbuf_p[:, h % 2, sl], sbuf_e[:, e0, sl], rd0[:, t:t + 1], sbuf_e[:, e1, sl],
                                 ALU.mult, ALU.subtract).then_inc(*mark("vector_steps", *([("prob", "B", h)] if t else [])))
                        dve.wait_ge(*last("vector_steps"))
                if h:
                    outB(h - 1)
            r = rstd_of("oB", 8, 2 * HD1)
            TS(r, r, 1.0 - LAMBDA_INIT, None, ALU.mult).then_inc(*mark("vector_steps"))
            dve.wait_ge(*last("vector_steps"))
            for t in range(TT):
                ov = o1[:, t, 512:1024].rearrange("p (h d) -> p h d", h=4)
                i = TT_(ov, ov, r[:, 4 * t:4 * t + 4].unsqueeze(2).to_broadcast([P, 4, P]), ALU.mult)
            i.then_inc(*mark("normed", "oB"))
            for k in range(KD):
                dve.wait_ge(*at(("full", ("oT", k))))
                g = col("diff") if k >= 4 else 1.0
                TS(hT1[:, k, :], ps[:, B(("oT", k)), 0:SEQ], g, None, ALU.mult).then_inc(*mark("turned_read", ("drained", ("oT", k))))
            for k in range(KD):
                dve.wait_ge(*at(("full", ("mix", k))))
                TS(xn1v[:, k, :], ps[:, B(("mix", k)), 0:SEQ], mod[:, 16 + k:17 + k], None, ALU.mult).then_inc(*mark("gated", ("drained", ("mix", k))))
            for t in range(TT):
                for g in range(2):
                    dve.wait_ge(*at(("full", ("mixT", t, g))))
                    xs = x[:, t, 512 * g:512 * g + 512]
                    TT_(xs, xs, ps[:, B(("mixT", t, g)), :], ALU.add).then_inc(*mark("x_updated", ("drained", ("mixT", t, g)), *(["x1"] if t == 1 and g == 1 else [])))
            r = rstd_of("x2", TT, D)
            for t in range(TT):
                i = TS(xn1[:, t, :], x[:, t, :], r[:, t:t + 1], None, ALU.mult)
            i.then_inc(*mark("normed", "xn2"))
            modulate("h2", 1, 24)
            dve.wait_ge(*at(("full", "logits")))
            TT_(lgt, ps[:, B("logits"), 0:2 * NE].rearrange("p (t e) -> p t e", t=TT),
                     rows[:, ROW["b_router"]:ROW["b_router"] + NE].unsqueeze(1).to_broadcast([P, TT, NE]), ALU.add).then_inc(*mark("vector_steps", ("drained", "logits")))
            dve.wait_ge(*last("vector_steps"))
            for t in range(TT):
                V.max(top8[:, t, :], lgt[:, t, :]).then_inc(*mark("vector_steps"))
                dve.wait_ge(*last("vector_steps"))
                V.max_index(idx[:, t, :], top8[:, t, :], lgt[:, t, :]).then_inc(*mark("vector_steps"))
                dve.wait_ge(*last("vector_steps"))
                V.tensor_copy(idxf[:, t, :], idx[:, t, :]).then_inc(*mark("vector_steps"))
                dve.wait_ge(*last("vector_steps"))
                TS(gex[:, t, 0:TOPK], top8[:, t, 0:TOPK], top8[:, t, 0:1], None, ALU.subtract).then_inc(*mark("vector_steps", ("gdiff", t)))
                dve.wait_ge(*last("vector_steps"))
            for t in range(TT):
                dve.wait_ge(*at(("gexp", t)))
                V.reciprocal(stat(("gr", t)), stat(("gsum", t))).then_inc(*mark("vector_steps"))
                dve.wait_ge(*last("vector_steps"))
                TS(gex[:, t, 0:TOPK], gex[:, t, 0:TOPK], stat(("gr", t)), None, ALU.mult).then_inc(*mark("vector_steps"))
                dve.wait_ge(*last("vector_steps"))
            iotae = con("iotae", NE)
            for t in range(TT):
                for j in range(TOPK):
                    ix, gj = idxf[:, t, j:j + 1], gex[:, t, j:j + 1]
                    if j == 0:
                        TS(pick[:, t, :], iotae, ix, None, ALU.is_equal).then_inc(*mark("vector_steps"))
                        dve.wait_ge(*last("vector_steps"))
                        TS(gpick[:, t, :], iotae, ix, gj, ALU.is_equal, ALU.mult).then_inc(*mark("vector_steps"))
                        dve.wait_ge(*last("vector_steps"))
                    else:
                        STT(pick[:, t, :], iotae, ix, pick[:, t, :], ALU.is_equal, ALU.add).then_inc(*mark("vector_steps", *(["pick"] if t and j == TOPK - 1 else [])))
                        dve.wait_ge(*last("vector_steps"))
                        TS(eqb[:, t, :], iotae, ix, gj, ALU.is_equal, ALU.mult).then_inc(*mark("vector_steps"))
                        dve.wait_ge(*last("vector_steps"))
                        TT_(gpick[:, t, :], gpick[:, t, :], eqb[:, t, :], ALU.add).then_inc(*mark("vector_steps", *(["gpick"] if t and j == TOPK - 1 else [])))
                        dve.wait_ge(*last("vector_steps"))
            V.memset(slot[:, NE, :], 4000.0).then_inc(*mark("vector_steps"))
            dve.wait_ge(*last("vector_steps"))
            dve.wait_ge(*at(("full", "rank")))
            for t in range(TT):
                STT(slot[:, 0:NE, t], pick[:, t, :], -1000.0, ps[:, B("rank"), t * NE:(t + 1) * NE], ALU.mult, ALU.add).then_inc(*mark("vector_steps"))
                dve.wait_ge(*last("vector_steps"))
                V.tensor_copy(gate[:, :, t], gpick[:, t, :]).then_inc(*mark("vector_steps"))
                dve.wait_ge(*last("vector_steps"))
            TS(slot[:, 0:NE, :], slot[:, 0:NE, :], 1000.0, None, ALU.add).then_inc(*mark("vector_steps"))
            dve.wait_ge(*last("vector_steps"))
            V.tensor_reduce(stat("most"), ps[:, B("rank"), 2 * NE:3 * NE], AX, ALU.max).then_inc(*mark("vector_steps", ("drained", "rank")))
            dve.wait_ge(*last("vector_steps"))
            TS(flag[:, 0:1], stat("most"), float(CAP), None, ALU.is_gt).then_inc(*mark("vector_steps", "flag"))
            dve.wait_ge(*last("vector_steps"))
            dve.wait_ge(*at(("full", "gateT")))
            V.tensor_copy(gateT[0:NE, :], ps[0:NE, B("gateT"), 0:SEQ]).then_inc(*mark("vector_steps", ("drained", "gateT")))
            dve.wait_ge(*last("vector_steps"))
            for g in range(4):
                dve.wait_ge(*at(("full", ("bias", g))))
                V.tensor_copy(yacc[:, 2 * g:2 * g + 2, :], ps[:, B(("bias", g)), :].rearrange("p (j q) -> p j q", j=2)).then_inc(*mark("vector_steps", ("drained", ("bias", g))))
                dve.wait_ge(*last("vector_steps"))
            V.memset(ysb, 0.0).then_inc(*mark("vector_steps"))
            dve.wait_ge(*last("vector_steps"))

            iot = con("iota", CAP).unsqueeze(1).to_broadcast([P, TT, CAP])

            def gathered(gk, names):
                for g in range(2):
                    dve.wait_ge(*at(("full", (gk, g))))
                    for j in range(4):
                        k = 4 * g + j
                        i = TS(xT[:, k, :], ps[:, 4 + g, j * CAP:(j + 1) * CAP], aff[:, 1, k:k + 1],
                               mod[:, 24 + k:25 + k], ALU.mult, ALU.add)
                        if j < 2 and names == "first":
                            i.then_inc(*mark("products_read"))
                        if j == 3:
                            i.then_inc(*mark("inputs_ready", *([] if names == "first" else [names + (g,)])))

            def summed(sk, names):
                for g in range(4):
                    dve.wait_ge(*at(("full", (sk, g))))
                    ya = yacc[:, 2 * g:2 * g + 2, :]
                    TT_(ya, ya, ps[:, (6, 7, 4, 5)[g], :].rearrange("p (j q) -> p j q", j=2), ALU.add).then_inc(*mark("sums_updated", names + (g,)))

            def experts(tag):
                V.memset(selgT, 0.0).then_inc(*mark("vector_steps", ("zero", tag)))
                dve.wait_ge(*last("vector_steps"))
                V.memset(stat(("primer", tag)), 0.0).then_inc(*mark("sums_updated"))
                TT_(sel, iot, slot[:, 0:1, :].rearrange("p e t -> p t e").to_broadcast([P, TT, CAP]), ALU.is_equal).then_inc(*mark("vector_steps", ("sel0", tag)))
                dve.wait_ge(*last("vector_steps"))
                gathered(("g0", tag), "first")
                with K.loop(dve, tag, NE) as e:
                    V.tensor_copy(bgu, cols[:, bass.ds(e * 16 + COL["b_gu"], 16)]).then_inc(*mark("vector_steps"))
                    dve.wait_ge(*last("vector_steps"))
                    row = lambda a, n: a[:, bass.ds(e + n, 1), :].rearrange("p e t -> p t e").to_broadcast([P, TT, CAP])
                    dve.wait_ge(*at((tag, "selT"), lag=1))
                    TT_(selg, iot, row(slot, 0), ALU.is_equal).then_inc(*mark("vector_steps"))
                    dve.wait_ge(*last("vector_steps"))
                    TT_(selg, selg, row(gate, 0), ALU.mult).then_inc(*mark("vector_steps", (tag, "selg")))
                    dve.wait_ge(*last("vector_steps"))
                    dve.wait_ge(*at(("full", ((tag, "g"), 1)), lag=1))
                    TT_(sel, iot, row(slot, 1), ALU.is_equal).then_inc(*mark("vector_steps", (tag, "sel")))
                    dve.wait_ge(*last("vector_steps"))
                    for h in range(2):
                        for which, dst, ci in (("g", gbuf, 4 * h + 1), ("u", ubuf, 4 * h + 3)):
                            dve.wait_ge(*at((tag, "chunk", ci)))
                            g = 2 * h + (which == "u")
                            for j in range(4):
                                f = (4 * h + j) + (8 if which == "u" else 0)
                                i = TS(dst[:, h, j * CAP:(j + 1) * CAP], ps[:, g, j * CAP:(j + 1) * CAP],
                                       bgu[:, f:f + 1], LIMIT, ALU.add, ALU.min)
                            i.then_inc(*mark("products_read", (tag, "h", g)))
                        dve.wait_ge(*last("products_read"))
                        TS(ubuf[:, h], ubuf[:, h], -LIMIT, 1.0, ALU.max, ALU.add).then_inc(*mark("vector_steps"))
                        dve.wait_ge(*last("vector_steps"))
                        dve.wait_ge(*at((tag, "sig", h)))
                        TT_(gbuf[:, h], gbuf[:, h], sbuf_g[:, h], ALU.mult).then_inc(*mark("vector_steps"))
                        dve.wait_ge(*last("vector_steps"))
                        TT_(actb[:, 4 * h:4 * h + 4, :].rearrange("p j c -> p (j c)"), gbuf[:, h], ubuf[:, h], ALU.mult).then_inc(*mark("hidden_ready", (tag, "act", h)))
                    gathered((tag, "g"), (tag, "xT"))
                    summed((tag, "s"), (tag, "y+"))
                summed(("s_end", tag), ("y_end", tag))

            experts("moe")
            dve.wait_ge(*at("flag"))
            over = nc.vector.value_load(flag[0:1, 0:1], min_val=0, max_val=1)
            with nc.vector.If(over > 0):
                K.prefix = "spill_"
                for p in range(1, NPASS):
                    TS(slot[:, :, :], slot[:, :, :], -float(CAP), None, ALU.add).then_inc(*mark("vector_steps"))
                    dve.wait_ge(*last("vector_steps"))
                    experts(f"moe{p}")
                dve.wait_ge(*last("sums_updated"))
                K.prefix = ""
            dve.wait_ge(*last("sums_updated"))
            for k in range(KD):
                i = TS(yacc[:, k, :], yacc[:, k, :], mod[:, 40 + k:41 + k], None, ALU.mult)
            i.then_inc(*mark("gated", "yg"))
            for t in range(TT):
                for g in range(2):
                    dve.wait_ge(*at(("full", ("moeT", t, g))))
                    xs = x[:, t, 512 * g:512 * g + 512]
                    TT_(xs, xs, ps[:, B(("moeT", t, g)), :], ALU.add).then_inc(*mark("x_updated", ("drained", ("moeT", t, g)), *(["x2"] if t == 1 and g == 1 else [])))

            dve.wait_ge(*last("x_updated"))
            for l in range(LAYERS):
                nt = 4 if l == 0 else 2
                ns = nt // 2
                N = nt * P
                L = f"L{l}"
                dve.wait_ge(*at(("full", (L, "ada"))))
                av = ps[:, B((L, "ada")), 0:96].rearrange("p (f s) -> p s f", s=2)
                for s in range(2):
                    TT_(modb[:, s, :], av[:, s, :], col(("ada_b", l), 0, 48), ALU.add).then_inc(*mark("vector_steps", *([("drained", (L, "ada"))] if s else [])))
                    dve.wait_ge(*last("vector_steps"))
                for s in range(2):
                    STT(aff[:, 0 + s], modb[:, s, 8:16], 1.0, col(("mix_pre", l), 0, 8), ALU.add, ALU.mult).then_inc(*mark("vector_steps"))
                    dve.wait_ge(*last("vector_steps"))
                    STT(aff[:, 2 + s], modb[:, s, 32:40], 1.0, col(("ffn_pre", l), 0, 8), ALU.add, ALU.mult).then_inc(*mark("vector_steps"))
                    dve.wait_ge(*last("vector_steps"))
                    TT_(aff[:, 4 + s], modb[:, s, 16:24], col(("mix_post", l), 0, 8), ALU.mult).then_inc(*mark("vector_steps"))
                    dve.wait_ge(*last("vector_steps"))
                    TT_(aff[:, 6 + s], modb[:, s, 40:48], col(("ffn_post", l), 0, 8), ALU.mult).then_inc(*mark("vector_steps"))
                    dve.wait_ge(*last("vector_steps"))

                def normalise(key, n, ready):
                    r = rstd_of(key, n, D)
                    for t in range(n):
                        src = x[:, t, :] if t < TT else ctxr[:, t - TT, :]
                        i = TS(xnb[:, t, :], src, r[:, t:t + 1], None, ALU.mult)
                    i.then_inc(*mark("normed", ready))

                def modulate2(name, n, A, sh):
                    for k in range(KD):
                        dve.wait_ge(*at(("full", (L, name, k))))
                        for s in range(n // 2):
                            i = TS(hT[:, k, s * SEQ:(s + 1) * SEQ], ps[:, B((L, name, k)), s * SEQ:(s + 1) * SEQ],
                                   aff[:, A + s, k:k + 1], modb[:, s, sh + k:sh + k + 1], ALU.mult, ALU.add)
                        i.then_inc(*mark("modulated", ("drained", (L, name, k))))
                normalise((L, "n1"), 4, (L, "xn"))
                modulate2("h", 4, 0, 0)
                V.memset(glp[:, :, :, 0:PADT], 0.0).then_inc(*mark("vector_steps"))
                dve.wait_ge(*last("vector_steps"))
                V.memset(glp[:, :, :, SEQ + PADT:SEGW], 0.0).then_inc(*mark("vector_steps"))
                dve.wait_ge(*last("vector_steps"))
                segs = lambda a: a.rearrange("p (s q) -> p s q", s=ns)
                for k in range(KD):
                    ka, kb = ((L, "cg"), 2 * k), ((L, "cg"), 2 * k + 1)
                    dve.wait_ge(*at(("full", ka)))
                    dve.wait_ge(*at(("drained", kb)))
                    TT_(glp[:, k, 0:ns, PADT:PADT + SEQ], segs(ps[:, B(ka), 0:N]), segs(tmp[:, k % 4, 0:N]), ALU.mult).then_inc(*mark("products_taken", ("drained", ka)))
                dve.wait_ge(*last("products_taken"))

                def conv():
                    w = lambda k, tap: col(("conv_w", l), tap * 8 + k)
                    for k0 in range(0, KD, 2):
                        for tap in range(TAPS):
                            for k in (k0, k0 + 1):
                                src = glp[:, k, 0:ns, tap:tap + SEQ]
                                dst = segs(cv[:, k, 0:N])
                                if tap == 0:
                                    i = TS(dst, src, w(k, 0), col(("conv_b", l), k), ALU.mult, ALU.add)
                                else:
                                    dve.wait_ge(*at((L, "tap", k, tap - 1)))
                                    i = STT(dst, src, w(k, tap), dst, ALU.mult, ALU.add)
                                i.then_inc(*mark("conv_taps", (L, "tap", k, tap), *([(L, "cv", k)] if tap == TAPS - 1 else [])))
                                yield
                taps = conv()

                def fill(n):
                    for _ in range(n):
                        if next(taps, 0) == 0:
                            return

                def gelu(items):
                    for n in range(len(items) + 1):
                        if n < len(items):
                            key, dst, w_ = items[n]
                            tb = tmp[:, n % 4, 0:w_]
                            dve.wait_ge(*at(("sq", key)))
                            TS(tb, tb, 0.044715, 1.0, ALU.mult, ALU.add).then_inc(*mark("vector_steps"))
                            dve.wait_ge(*last("vector_steps"))
                            TT_(tb, tb, ps[:, B(key), 0:w_], ALU.mult).then_inc(*mark("cubics_ready", ("cub", key)))
                            fill(3)
                        if n:
                            key, dst, w_ = items[n - 1]
                            dve.wait_ge(*at(("gs", key)))
                            TT_(dst, tmp[:, (n - 1) % 4, 0:w_], ps[:, B(key), 0:w_], ALU.mult).then_inc(*mark("products_taken", ("drained", key)))
                            fill(3)
                gelu(gelu_items(l))
                dve.wait_ge(*last("products_taken"))
                r = rstd_of((L, "gv"), nt, D)
                for t in range(nt):
                    i = TS(gv[:, t, :], gv[:, t, :], r[:, t:t + 1], None, ALU.mult)
                i.then_inc(*mark("normed", (L, "gvn")))
                for f in range(KD):
                    dve.wait_ge(*at(("full", (L, "sv", f))))
                    b = B((L, "sv", f))
                    bs = rows[:, ROW["bs"] + 512 * l + 128 * (f // 2):ROW["bs"] + 512 * l + 128 * (f // 2) + 128]
                    tl = lambda a: a.rearrange("p (t q) -> p t q", q=P)
                    STT(tl(tmp[:, 4 + f % 2, 0:N]), tl(ps[:, b, 0:N]), col(("gmlp_norm", l), f),
                             bs.unsqueeze(1).to_broadcast([P, nt, P]), ALU.mult, ALU.add).then_inc(*mark("vector_steps", ("drained", (L, "sv", f))))
                    dve.wait_ge(*last("vector_steps"))
                    TT_(uT[:, f, 0:N], tmp[:, 4 + f % 2, 0:N], uT[:, f, 0:N], ALU.mult).then_inc(*mark("gated", (L, "usv", f)))

                def take(br, first, nfill):
                    for f in range(KD):
                        key = ((L, "out", br), f)
                        dve.wait_ge(*at(("full", key)))
                        dve.wait_ge(*at(("drained", ((L, "gate", br), f))))
                        if first:
                            TT_(merged[:, f, 0:N], ps[:, B(key), 0:N], tmp[:, f % 4, 0:N], ALU.mult).then_inc(*mark("products_taken", ("drained", key)))
                        else:
                            if f >= 4:
                                dve.wait_ge(*at((L, "added", br, f - 4)))
                            TT_(tmp[:, 4 + f % 4, 0:N], ps[:, B(key), 0:N], tmp[:, f % 4, 0:N], ALU.mult).then_inc(*mark("products_taken", ("drained", key)))
                        fill(nfill)
                take("gmlp", True, 8)

                def head_norm(g, t):
                    key = ((L, "qkv", g), t)
                    nh = 4 if g < 2 else 2
                    w_ = nh * P
                    gains = rows[:, ROW["qk"] + 256 * l + 128 * (g == 2):ROW["qk"] + 256 * l + 128 * (g == 2) + 128]
                    hv = lambda a: a.rearrange("p (h d) -> p h d", d=P)
                    dve.wait_ge(*at(("sq", key)))
                    V.tensor_reduce(stat((key, "ssq"), 4)[:, 0:nh], hv(scr[:, t % 2, 0:w_]), AX, ALU.add).then_inc(*mark("vector_steps", ("ssq", key)))
                    dve.wait_ge(*last("vector_steps"))
                    fill(2)
                    r = rstd_of(key, nh, HD2)
                    if g == 2:
                        dve.wait_ge(*at(("vcopied", key)))
                    qn = scr[:, 2, 0:w_]
                    TT_(hv(qn), hv(ps[:, B(key), 0:w_]), r.unsqueeze(2).to_broadcast([P, nh, P]), ALU.mult).then_inc(*mark("vector_steps", ("drained", key)))
                    dve.wait_ge(*last("vector_steps"))
                    if g == 2:
                        dst = tmp[:, 4 + t, 0:w_]
                    else:
                        dst = tmp[:, t, 0:w_]
                        if g:
                            dve.wait_ge(*at(("full", (L, "q", g - 1, t))))
                    ready = (L, "kr", t) if g == 2 else (L, "qr", g, t)
                    gb = gains.unsqueeze(1).to_broadcast([P, nh, P])
                    if t >= TT:
                        TT_(hv(dst), hv(qn), gb, ALU.mult).then_inc(*mark("normed", ready))
                    else:
                        TT_(hv(qn), hv(qn), gb, ALU.mult).then_inc(*mark("vector_steps"))
                        dve.wait_ge(*last("vector_steps"))
                        c_ = con("cos", 64, 64 * t).unsqueeze(1).to_broadcast([P, 2 * nh, 64])
                        halves = lambda a: a.rearrange("p (h d) -> p h d", d=64)
                        two = lambda a: a.rearrange("p (h b d) -> p b h d", b=2, d=64)
                        TT_(halves(dst), halves(qn), c_, ALU.mult).then_inc(*mark("vector_steps"))
                        dve.wait_ge(*last("vector_steps"))
                        for b2 in range(2):
                            s_ = con("sin", 64, 128 * t + 64 * b2).unsqueeze(1).to_broadcast([P, nh, 64])
                            TT_(two(scr[:, 3, 0:w_])[:, b2], two(qn)[:, 1 - b2], s_, ALU.mult).then_inc(*mark("vector_steps"))
                            dve.wait_ge(*last("vector_steps"))
                        TT_(dst, dst, scr[:, 3, 0:w_], ALU.add).then_inc(*mark("normed", ready))
                    dve.wait_ge(*last("normed"))
                    fill(5)
                for g in range(3):
                    for t in range(4 if g == 2 else nt):
                        head_norm(g, t)
                for t in range(4):
                    dve.wait_ge(*at(("full", (L, "k", t))))
                    V.tensor_copy(kT[:, :, t * P:(t + 1) * P],
                                       ps[:, B((L, "k", t)), 0:256].rearrange("p (h q) -> p h q", h=2)).then_inc(*mark("turned_read", ("drained", (L, "k", t))))

                units = units_of[l]
                for n in range(len(units) + 1):
                    if n < len(units):
                        h, seg = units[n]
                        key = (L, h, seg)
                        nk = 4 if seg == 0 else 2
                        for t in range(TT):
                            dve.wait_ge(*at(("full", (key, "s", t))))
                            V.tensor_reduce(stat(("nm", n % 2, t)), ps[:, B((key, "s", t)), 0:nk * P], AX, ALU.max, negate=True).then_inc(*mark("maxima_ready", (key, "nm", t)))
                        for t in range(TT):
                            dve.wait_ge(*at(("drained", (key, "s", t))))
                            V.reciprocal(stat(("rden", t)), stat(("den", n % 2, t))).then_inc(*mark("vector_steps"))
                            dve.wait_ge(*last("vector_steps"))
                            if n >= 2:
                                dve.wait_ge(*at(("full", ((L,) + units[n - 2], "pt", t))))
                            TS(tmp[:, 2 * (n % 2) + t, 0:nk * P], tmp[:, 4 + 2 * (n % 2) + t, 0:nk * P], stat(("rden", t)), None,
                                    ALU.mult).then_inc(*mark("vector_steps", (key, "p", t)))
                            dve.wait_ge(*last("vector_steps"))
                    if n:
                        h, seg = units[n - 1]
                        key = (L, h, seg)
                        dve.wait_ge(*at(("full", (key, "o"))))
                        V.tensor_copy(uT[:, h, seg * SEQ:(seg + 1) * SEQ], ps[:, B((key, "o")), 0:SEQ]).then_inc(*mark("heads_read", ("drained", (key, "o"))))
                    fill(2)
                fill(1000)
                dve.wait_ge(*at(("full", (L, "mu"))))
                TS(scr[:, 0, 0:N], ps[:, B((L, "mu")), 0:N], 1.0 / D, None, ALU.mult).then_inc(*mark("vector_steps", ("drained", (L, "mu"))))
                dve.wait_ge(*last("vector_steps"))
                for k in range(KD):
                    TT_(cv[:, k, 0:N], cv[:, k, 0:N], scr[:, 0, 0:N], ALU.subtract).then_inc(*mark("centred", (L, "cvc", k)))

                def take_one(br, f):
                    key = ((L, "out", br), f)
                    dve.wait_ge(*at(("full", key)))
                    dve.wait_ge(*at(("drained", ((L, "gate", br), f))))
                    if f >= 4:
                        dve.wait_ge(*at((L, "added", br, f - 4)))
                    TT_(tmp[:, 4 + f % 4, 0:N], ps[:, B(key), 0:N], tmp[:, f % 4, 0:N], ALU.mult).then_inc(*mark("products_taken", ("drained", key)))
                for f in range(4):
                    take_one("attn", f)
                dve.wait_ge(*at(("full", (L, "var"))))
                TS(scr[:, 1, 0:N], ps[:, B((L, "var")), 0:N], 1.0 / D, EPS, ALU.mult, ALU.add).then_inc(*mark("vector_steps", ("drained", (L, "var")), ("ms", (L, "cvn"))))
                dve.wait_ge(*last("vector_steps"))
                dve.wait_ge(*at(("root", (L, "cvn"))))
                V.reciprocal(scr[:, 1, 0:N], scr[:, 1, 0:N]).then_inc(*mark("vector_steps"))
                dve.wait_ge(*last("vector_steps"))
                for k in range(KD):
                    TT_(cv[:, k, 0:N], cv[:, k, 0:N], scr[:, 1, 0:N], ALU.mult).then_inc(*mark("vector_steps"))
                    dve.wait_ge(*last("vector_steps"))
                    TS(cv[:, k, 0:N], cv[:, k, 0:N], col(("conv_g", l), k), col(("conv_nb", l), k), ALU.mult, ALU.add).then_inc(*mark("normed", (L, "cvz", k)))
                    if k:
                        dve.wait_ge(*at((L, "cvs", k - 1)))
                        TT_(cv[:, k - 1, 0:N], cv[:, k - 1, 0:N], scr[:, 2 + (k - 1) % 2, 0:N], ALU.mult).then_inc(*mark("silu_ready", (L, "cvn", k - 1)))
                dve.wait_ge(*at((L, "cvs", KD - 1)))
                TT_(cv[:, KD - 1, 0:N], cv[:, KD - 1, 0:N], scr[:, 2 + (KD - 1) % 2, 0:N], ALU.mult).then_inc(*mark("silu_ready", (L, "cvn", KD - 1)))
                for f in range(4, KD):
                    take_one("attn", f)
                for f in range(KD):
                    if f < 4:
                        dve.wait_ge(*at((L, "added", "attn", f + 4)))
                    take_one("conv", f)

                def diagonals(which):
                    for s in range(ns):
                        for k in range(KD):
                            n = s * KD + k
                            if n >= 2:
                                dve.wait_ge(*at((L, "bcm", which, (n - 2) // KD, (n - 2) % KD)))
                            TS(dgb[:, k % 2], ident, aff[:, 4 + 2 * which + s, k:k + 1], None, ALU.mult).then_inc(*mark("diagonals", (L, "dg", which, s, k)))

                def residual(which, ready):
                    r = rstd_of((L, "y", which), nt, D)
                    for s in range(ns):
                        for g in range(2):
                            dve.wait_ge(*at(("drained", (L, "bc", which, s, g))))
                    for t in range(nt):
                        STT(yb[:, t, :], yb[:, t, :], r[:, t:t + 1], bcv[:, t // 2, :], ALU.mult, ALU.mult).then_inc(*mark("vector_steps"))
                        dve.wait_ge(*last("vector_steps"))
                        dst = x[:, t, :] if t < TT else ctxr[:, t - TT, :]
                        TT_(dst, dst, yb[:, t, :], ALU.add).then_inc(*mark("vector_steps", *([(L, ready)] if t == nt - 1 else []), *([(L, ready, "x")] if t == TT - 1 else [])))
                        dve.wait_ge(*last("vector_steps"))
                diagonals(0)
                residual(0, "x1")
                normalise((L, "n2"), nt, (L, "xn2"))
                modulate2("h2", nt, 2, 24)
                for hf in range(2):
                    if hf:
                        dve.wait_ge(*at(("full", ((L, "ff2", 0, 1), nt - 1))))
                    for j in range(16):
                        key = ((L, "ff1", hf), j)
                        dve.wait_ge(*at(("drained", key)))
                        TT_(hid[:, j, 0:N], tmp[:, j % 8, 0:N], tmp[:, j % 8, 0:N], ALU.mult).then_inc(*mark("hidden_ready", (L, "hid", hf, j)))
                for g in range(2):
                    for t in range(nt):
                        key = ((L, "ff2", 1, g), t)
                        dve.wait_ge(*at(("full", key)))
                        dve.wait_ge(*at(("drained", ((L, "ff2", 0, g), t))))
                        ys = yb[:, t, 512 * g:512 * g + 512]
                        TT_(ys, ys, ps[:, B(key), :], ALU.add).then_inc(*mark("products_taken", ("drained", key)))
                diagonals(1)
                residual(1, "x2")

        @block.scalar
        def _(act):
            A = nc.scalar.activation

            def B(key):
                return bank_of[key]
            for dst, src, name in ((cols[:, :], cols_d, "cols"), (x[:, :, :], x_d, "x"), (cst[:, :], cst_d, "cst"),
                                   (rows[:, :], rows_d.partition_broadcast(P), "rows"), (ws[:, :, :, :], ws_d, "ws"),
                                   (wr[:, :, :], wr_d, "wr"), (bdn[0:NE, :], bd_d, "bdn"), (ctxr[:, :, :], ctx_d, "ctx")):
                act.dma_start(dst, src).then_inc(*mark("load_" + name, name, inc=16))

            def sumsq(key, tiles, junk, ready=()):
                for r in ready:
                    act.wait_ge(*at(r))
                for t, src in enumerate(tiles):
                    i = A(junk, src, ACT.Square, accum_out=stat((key, "ssq"), len(tiles))[:, t:t + 1])
                    i.then_inc(*mark("squares_summed", *([("ssq", key)] if t == len(tiles) - 1 else [])))
                    act.wait_ge(*last("squares_summed"))
                root(key, len(tiles))

            def root(key, n):
                act.wait_ge(*at(("ms", key)))
                A(stat((key, "rt"), n), stat((key, "ms"), n), ACT.Sqrt).then_inc(*mark("roots_ready", ("root", key)))

            act.wait_ge(*at("cols"))
            A(cond[:, :], col("cond", 0, 24), ACT.Sigmoid).then_inc(*mark("sigmoids", "cond_sig"))
            act.wait_ge(*at("x"))
            sumsq("x1", [x[:, t, :] for t in range(TT)], junk1b)
            act.wait_ge(*at("ldot"))
            A(stat("lexp", 2), stat("ldot", 2), ACT.Exp).then_inc(*mark("exps_ready", "lexp"))
            for g in range(6):
                for t in range(TT):
                    act.wait_ge(*at(("full", (("proj", g), t))))
                    A(proj[:, t, 512 * g:512 * g + 512], ps[:, B((("proj", g), t)), :], ACT.Identity).then_inc(*mark("products_copied", ("drained", (("proj", g), t))))
                if g in (0, 1, 3, 4):
                    pass
            for m in range(4):
                root(("qk", m), 16)
            for h in range(A_HEADS):
                act.wait_ge(*at(("nm", ("A", h))))
                for t in range(TT):
                    sl = slice(P * t, P * t + P * (t + 1))
                    i = A(sbuf_e[:, h % 4, sl], sbuf_s[:, h % 2, sl], ACT.Exp, bias=stat((("A", h), "nm"), 2)[:, t:t + 1])
                i.then_inc(*mark("exps_ready", ("exp", ("A", h))))
            for h in range(B_HEADS):
                for c in range(2):
                    key = ("B", h, c)
                    act.wait_ge(*at(("nm", key)))
                    for t in range(TT):
                        sl = slice(P * t, P * t + P * (t + 1))
                        i = A(sbuf_e[:, 2 * (h % 2) + c, sl], sbuf_s[:, c, sl], ACT.Exp, bias=stat((key, "nm"), 2)[:, t:t + 1],
                              accum_out=stat((key, "den"), 2)[:, t:t + 1])
                    i.then_inc(*mark("exps_ready", ("exp", key)))
            root("oB", 8)
            sumsq("x2", [x[:, t, :] for t in range(TT)], junk1b, ["x1"])
            for t in range(TT):
                act.wait_ge(*at(("gdiff", t)))
                A(gex[:, t, 0:TOPK], gex[:, t, 0:TOPK], ACT.Exp, accum_out=stat(("gsum", t))).then_inc(*mark("exps_ready", ("gexp", t)))

            def experts(tag):
                for name in ("selection_ready", "outputs_ready"):
                    A(stat(("primer", tag, name)), stat(("x1", "rt"), TT)[:, 0:1], ACT.Identity).then_inc(*mark(name))
                with K.loop(act, tag, NE):
                    for h in range(2):
                        act.wait_ge(*at((tag, "h", 2 * h)))
                        A(sbuf_g[:, h], gbuf[:, h], ACT.Sigmoid, scale=ALPHA).then_inc(*mark("sigmoids", (tag, "sig", h)))
                    act.wait_ge(*at((tag, "selT")))
                    A(selgT[0:CAP, :], ps[0:CAP, 0, 0:SEQ], ACT.Identity).then_inc(*mark("selection_ready", (tag, "selgT")))
                    for g in range(2):
                        act.wait_ge(*at((tag, "chunk", 9 + 2 * g)))
                        A(ysb[0:CAP, 512 * g:512 * g + 512], ps[0:CAP, 6 + g, :], ACT.Identity).then_inc(*mark("outputs_ready", (tag, "y", g)))
            experts("moe")
            act.wait_ge(*at("flag"))
            over = nc.scalar.value_load(flag[0:1, 0:1], min_val=0, max_val=1)
            with nc.scalar.If(over > 0):
                K.prefix = "spill_"
                for p in range(1, NPASS):
                    experts(f"moe{p}")
                K.prefix = ""

            for l in range(LAYERS):
                nt = 4 if l == 0 else 2
                ns = nt // 2
                N = nt * P
                L = f"L{l}"
                rowsx = [x[:, t, :] for t in range(TT)] + [ctxr[:, t, :] for t in range(TT)]
                act.wait_ge(*at("ctx"))
                sumsq((L, "n1"), rowsx, junkb, ["x2"] if l == 0 else [("L0", "x2")])
                for k in range(KD):
                    kb = ((L, "cg"), 2 * k + 1)
                    act.wait_ge(*at(("full", kb)))
                    if k >= 4:
                        act.wait_ge(*at(("drained", ((L, "cg"), 2 * k - 8))))
                    A(tmp[:, k % 4, 0:N], ps[:, B(kb), 0:N], ACT.Sigmoid).then_inc(*mark("gates_ready", ("drained", kb)))
                items = gelu_items(l)
                for n in range(len(items) + 1):
                    if n < len(items):
                        key, dst, w_ = items[n]
                        act.wait_ge(*at(("full", key)))
                        act.wait_ge(*at(("drained", items[n - 4][0]) if n >= 4 else ("drained", ((L, "cg"), 8 + 2 * n))))
                        A(tmp[:, n % 4, 0:w_], ps[:, B(key), 0:w_], ACT.Square).then_inc(*mark("squares_ready", ("sq", key)))
                    if n:
                        key, dst, w_ = items[n - 1]
                        act.wait_ge(*at(("cub", key)))
                        A(tmp[:, (n - 1) % 4, 0:w_], tmp[:, (n - 1) % 4, 0:w_], ACT.Sigmoid, scale=GELU_C).then_inc(*mark("sigmoids", ("gs", key)))
                sumsq((L, "gv"), [gv[:, t, :] for t in range(nt)], junkb, [("drained", items[-1][0])])

                def gates(br, fs, prev):
                    for f in fs:
                        key = ((L, "gate", br), f)
                        act.wait_ge(*at(("full", key)))
                        act.wait_ge(*at(("drained", ((L, "out", br), f - 4)) if f >= 4 else prev(f)))
                        A(tmp[:, f % 4, 0:N], ps[:, B(key), 0:N], ACT.Sigmoid).then_inc(*mark("gates_ready", ("drained", key)))
                gates("gmlp", range(KD), lambda f: ("drained", items[len(items) - 4 + f][0]))
                for g in range(3):
                    for t in range(4 if g == 2 else nt):
                        key = ((L, "qkv", g), t)
                        w_ = 512 if g < 2 else 256
                        act.wait_ge(*at(("full", key)))
                        A(scr[:, t % 2, 0:w_], ps[:, B(key), 0:w_], ACT.Square).then_inc(*mark("squares_ready", ("sq", key)))
                        if g == 2:
                            A(vb[:, t, :], ps[:, B(key), 256:512], ACT.Identity).then_inc(*mark("values_ready", ("vcopied", key)))
                        root(key, 4 if g < 2 else 2)
                    for t in range(nt if g else 0):
                        act.wait_ge(*at(("full", (L, "q", g - 1, t))))
                        A(uT[:, 4 * g - 4:4 * g, t * P:(t + 1) * P],
                               ps[:, B((L, "q", g - 1, t)), :].rearrange("p (h q) -> p h q", h=4), ACT.Identity).then_inc(*mark("turned_copied", ("drained", (L, "q", g - 1, t))))
                units = units_of[l]
                for n in range(len(units) + 1):
                    if n < len(units):
                        h, seg = units[n]
                        key = (L, h, seg)
                        nk = 4 if seg == 0 else 2
                        for t in range(TT):
                            act.wait_ge(*at((key, "nm", t)))
                            if n >= 2:
                                act.wait_ge(*at(((L,) + units[n - 2], "p", t)))
                            A(tmp[:, 4 + 2 * (n % 2) + t, 0:nk * P], ps[:, B((key, "s", t)), 0:nk * P], ACT.Exp,
                                   bias=stat(("nm", n % 2, t)), accum_out=stat(("den", n % 2, t))).then_inc(*mark("exps_ready", ("drained", (key, "s", t))))
                    if n:
                        h, seg = units[n - 1]
                        key = (L, h, seg)
                        nk = 4 if seg == 0 else 2
                        for t in range(TT):
                            act.wait_ge(*at(("full", (key, "pt", t))))
                            if n >= 3:
                                act.wait_ge(*at(("full", ((L,) + units[n - 3], "o"))))
                            A(ptb[(n - 1) % 2][:, 0:nk, t * P:(t + 1) * P],
                                   ps[:, B((key, "pt", t)), 0:nk * P].rearrange("p (j q) -> p j q", j=nk), ACT.Identity).then_inc(*mark("turned_copied", ("drained", (key, "pt", t))))
                for k in range(KD):
                    act.wait_ge(*at((L, "cvc", k)))
                    A(glsq[:, k, 0:N], cv[:, k, 0:N], ACT.Square).then_inc(*mark("squares_ready", (L, "cvsq", k)))
                gates("attn", range(4), lambda f: ("full", ((L,) + units[len(units) - 2 + f // 2], "pt", f % 2)))
                act.wait_ge(*at(("ms", (L, "cvn"))))
                A(scr[:, 1, 0:N], scr[:, 1, 0:N], ACT.Sqrt).then_inc(*mark("roots_ready", ("root", (L, "cvn"))))
                for k in range(KD):
                    act.wait_ge(*at((L, "cvz", k)))
                    if k >= 2:
                        act.wait_ge(*at((L, "cvn", k - 2)))
                    A(scr[:, 2 + k % 2, 0:N], cv[:, k, 0:N], ACT.Sigmoid).then_inc(*mark("sigmoids", (L, "cvs", k)))
                gates("attn", range(4, KD), None)
                gates("conv", range(KD), lambda f: ("drained", ((L, "out", "attn"), f + 4)))

                def spread(which):
                    for s in range(ns):
                        for g in range(2):
                            act.wait_ge(*at(("full", (L, "bc", which, s, g))))
                            A(bcv[:, s, 512 * g:512 * g + 512], ps[:, B((L, "bc", which, s, g)), :], ACT.Identity).then_inc(*mark("spread_copied", ("drained", (L, "bc", which, s, g))))
                for g in range(2):
                    for t in range(nt):
                        key = ((L, "wo", g), t)
                        act.wait_ge(*at(("full", key)))
                        A(yb[:, t, 512 * g:512 * g + 512], ps[:, B(key), :], ACT.Identity).then_inc(*mark("products_copied", ("drained", key)))
                act.wait_ge(*last("products_copied"))
                sumsq((L, "y", 0), [yb[:, t, :] for t in range(nt)], junkb)
                spread(0)
                sumsq((L, "n2"), rowsx[0:nt], junkb, [(L, "x1")])
                for hf in range(2):
                    for j in range(16):
                        key = ((L, "ff1", hf), j)
                        act.wait_ge(*at(("full", key)))
                        if j >= 8:
                            act.wait_ge(*at((L, "hid", hf, j - 8)))
                        elif hf:
                            act.wait_ge(*at((L, "hid", 0, j + 8)))
                        A(tmp[:, j % 8, 0:N], ps[:, B(key), 0:N], ACT.Relu).then_inc(*mark("relus_ready", ("drained", key)))
                    if hf == 0:
                        for g in range(2):
                            for t in range(nt):
                                key = ((L, "ff2", 0, g), t)
                                act.wait_ge(*at(("full", key)))
                                A(yb[:, t, 512 * g:512 * g + 512], ps[:, B(key), :], ACT.Identity).then_inc(*mark("products_copied", ("drained", key)))
                sumsq((L, "y", 1), [yb[:, t, :] for t in range(nt)], junkb, [("drained", ((L, "ff2", 1, 1), nt - 1))])
                spread(1)

        @block.gpsimd
        def _(pool):
            for l in range(LAYERS):
                nt = 4 if l == 0 else 2
                N = nt * P
                L = f"L{l}"
                for br in ("attn", "conv"):
                    for f in range(KD):
                        pool.wait_ge(*at(("drained", ((L, "out", br), f))))
                        if br == "conv":
                            pool.wait_ge(*at((L, "added", "attn", f)))
                        nc.gpsimd.tensor_tensor(merged[:, f, 0:N], merged[:, f, 0:N], tmp[:, 4 + f % 4, 0:N], ALU.add).then_inc(*mark("branches_added", (L, "added", br, f), *([(L, "merged", f)] if br == "conv" else [])))

        @block.sync
        def _(sp):
            used = K.sem("weights_used")

            def load(c, slot_, sem):
                sp.dma_start(ring[:, slot_], stream[c].rearrange("p (k n) -> p k n", k=4)).then_inc(sem, 16)

            def one(c):
                if c >= RING:
                    sp.wait_ge(used, c - RING + 1)
                load(c, c % RING, landed[c % RING])

            end, cut = CH["total"], CH["after_moe"]
            for c in range(RING):
                one(c)
            rounds = cut // RING
            with sp.Fori(1, rounds) as r:
                for s in range(RING):
                    sp.wait_ge(used, r * RING + (s - RING + 1))
                    load(r * RING + s, s, landed[s])
            for c in range(rounds * RING, cut):
                one(c)
            if end > cut:
                sp.wait_ge(*at("flag"))
                over = nc.sync.value_load(flag[0:1, 0:1], min_val=0, max_val=1)
                with nc.sync.If(over > 0):
                    sp.wait_ge(used, CH["after_moe"])
                    again = K.sem("spill_weights_used")
                    for ci in range(CPE):
                        if ci >= RING:
                            sp.wait_ge(again, ci - RING + 1)
                        s = (CH["moe"] + ci) % RING
                        load(CH["moe"] + ci, s, spill_landed[s])
                    for p in range(NPASS - 1):
                        with sp.Fori(0 if p else 1, NE) as e:
                            for ci in range(CPE):
                                sp.wait_ge(again, e * CPE + (CPE * NE * p + ci - RING + 1))
                                s = (CH["moe"] + ci) % RING
                                load(e * CPE + (CH["moe"] + ci), s, spill_landed[s])
                    sp.wait_ge(again, CPE * NE * (NPASS - 1))
            nxt_c = cut
            while nxt_c < end and nxt_c % RING:
                one(nxt_c)
                nxt_c += 1
            if nxt_c < end:
                full_ = end // RING
                with sp.Fori(nxt_c // RING, full_) as r:
                    for s in range(RING):
                        sp.wait_ge(used, r * RING + (s - RING + 1))
                        load(r * RING + s, s, landed[s])
                for c in range(full_ * RING, end):
                    one(c)
            for name in ("ws", "wr", "bdn", "ctx"):
                sp.wait_ge(*at(name))
            sp.wait_ge(*at(("L1", "x2")))
            sp.dma_start(out_d, x[:, :, :]).then_inc(*mark("stored", "out", inc=16))
            sp.wait_ge(K.sem("stored"), 16)
    return K


def _constants():
    c = np.zeros((P, CST["total"]), np.float32)
    p = np.arange(P)
    c[:, CST["ident"]:CST["ident"] + P] = np.eye(P)
    c[:, CST["ones"]:CST["ones"] + P] = 1
    c[:, CST["tri"]:CST["tri"] + P] = p[:, None] < p[None, :]
    c[:, CST["iota"]:CST["iota"] + CAP] = np.arange(CAP)
    c[:, CST["iotae"]:CST["iotae"] + NE] = np.arange(NE)
    freqs = HD2 // 4
    inv = np.float32(10000.0) ** (-np.arange(freqs, dtype=np.float32) / np.float32(freqs))
    tok = np.arange(SEQ)
    ang = np.concatenate([(tok // 64).astype(np.float32)[:, None] * inv, (tok % 64).astype(np.float32)[:, None] * inv], -1)
    cos, sin = np.cos(ang).astype(np.float32), np.sin(ang).astype(np.float32)
    for t in range(TT):
        c[:, CST["cos"] + 64 * t:CST["cos"] + 64 * t + 64] = cos[t * P:(t + 1) * P]
        c[:, CST["sin"] + 128 * t:CST["sin"] + 128 * t + 64] = -sin[t * P:(t + 1) * P]
        c[:, CST["sin"] + 128 * t + 64:CST["sin"] + 128 * t + 128] = sin[t * P:(t + 1) * P]
        d = (t * P + p)[:, None] - np.arange(P * (t + 1))[None, :]
        cnt = (((d >= 0) & (d <= 128)).astype(int) + ((d >= 0) & (d % 4 == 0)) + ((d >= 0) & (d % 16 == 0)))
        at = P * t
        c[:, CST["cnt"] + at:CST["cnt"] + at + d.shape[1]] = cnt
        c[:, CST["distA"] + at:CST["distA"] + at + d.shape[1]] = np.where(cnt > 0, d, 1e30)
        c[:, CST["distB"] + at:CST["distB"] + at + d.shape[1]] = np.where(d >= 0, d, 1e30)
    return c


def _chunks(w):
    k, n = w.shape
    return w.reshape(k // 512, 4, P, n // 512, 512).transpose(3, 0, 2, 1, 4).reshape(-1, P, 2048)


def kernel(**inputs):
    import concourse.bacc as bacc
    from concourse.bass_utils import run_bass_kernel_spmd as run

    a = {n: np.asarray(w) for n, w in inputs.items()}
    stream = np.empty((CH["total"], P, 2048), np.float32)

    def put(name, w):
        c = _chunks(w)
        at = name if isinstance(name, int) else CH[name]
        stream[at:at + len(c)] = c

    put("ada", a["w_ada"][0])
    put("w_in", a["w_in"][0])
    put("w_out", a["w_out"][0])
    for e in range(NE):
        gu = a["w_gate_up"][0, e].reshape(D, 2, 2, 512).transpose(0, 2, 1, 3).reshape(D, 2 * D)
        put(CH["moe"] + CPE * e, gu)
        put(CH["moe"] + CPE * e + 8, a["w_down"][0, e])
    for l in range(LAYERS):
        w = a["w_in_2"][l]
        put(("ada", l), a["ada_w_2"][l])
        cg = w[:, 3584:5632].reshape(D, 2, KD, P).transpose(0, 2, 1, 3).reshape(D, 2 * D)
        put(("cg", l), cg)
        put(("gu", l), w[:, 1536:2560])
        put(("gv", l), w[:, 2560:3584])
        put(("qkv", l), w[:, 0:1536])
        for br, off, out in (("attn", 0, "w_attn_o_2"), ("gmlp", 1024, "w_gmlp_o_2"), ("conv", 2048, "w_conv_o_2")):
            for n in range(2):
                put(("gate", br, l, n), w[:, 5632 + off + 512 * n:5632 + off + 512 * n + 512])
                put(("out", br, l, n), a[out][l][:, 512 * n:512 * n + 512])
        put(("w_out", l), a["w_out_2"][l])
        for h in range(2):
            put(("ff1", l, h), a["w_ff1_2"][l][:, 2048 * h:2048 * h + 2048])
            put(("ff2", l, h), a["w_ff2_2"][l][2048 * h:2048 * h + 2048])

    column = {}

    def features(name, w):
        w = np.ascontiguousarray(w).reshape(-1, P).T
        columns[:, COL[name]:COL[name] + w.shape[1]] = w

    columns = np.zeros((P, COL["total"]), np.float32)
    features("cond", np.concatenate([a["c"].ravel(), a["c_2"].ravel(), a["c_ctx_2"].ravel()]))
    features("b_ada", a["b_ada"])
    features("norm1", a["norm1_g"])
    features("norm2", a["norm2_g"])
    features("qk_a", np.concatenate([a["a_q_norm_g"], a["a_q_norm_g"], a["a_k_norm_g"], a["a_k_norm_g"]], 0))
    features("qk_b", np.concatenate([a["b_q_norm_g"], a["b_q_norm_g"], a["b_k_norm_g"], a["b_k_norm_g"]], 0))
    features("diff", a["diff_norm_g"])
    features("b_gu", a["b_gate_up"][0])
    for l in range(LAYERS):
        for n, w in (("ada_b", "ada_b_2"), ("mix_pre", "mix_pre_g_2"), ("mix_post", "mix_post_g_2"),
                     ("gmlp_norm", "gmlp_norm_g_2"), ("conv_b", "conv_b_2"), ("conv_g", "conv_norm_g_2"),
                     ("conv_nb", "conv_norm_b_2"), ("ffn_pre", "ffn_pre_g_2"), ("ffn_post", "ffn_post_g_2"),
                     ("conv_w", "conv_w_2")):
            features((n, l), a[w][l])
    row = np.concatenate([a["lambda_q1"].ravel(), a["lambda_k1"].ravel(), a["lambda_q2"].ravel(), a["lambda_k2"].ravel()]
                         + [a[n][l].ravel() for l in range(LAYERS) for n in ("q_norm_g_2", "k_norm_g_2")]
                         + [a["gmlp_bs_2"].ravel(), a["b_router"].ravel()])
    arrays = {
        "stream": stream,
        "columns": columns,
        "row_vectors": row,
        "constants": _constants(),
        "x_tiles": np.ascontiguousarray(a["x"][0].reshape(TT, P, D).transpose(1, 0, 2)),
        "ctx_tiles": np.ascontiguousarray(a["ctx_2"][0].reshape(TT, P, D).transpose(1, 0, 2)),
        "spatial": np.ascontiguousarray(a["gmlp_ws_2"].transpose(3, 0, 1, 2)),
        "router": np.ascontiguousarray(a["w_router"][0].reshape(KD, P, NE).transpose(1, 0, 2)),
        "down_bias": np.ascontiguousarray(a["b_down"][0]),
    }

    def program(known, per):
        nc = bacc.Bacc("TRN2", target_bir_lowering=False, num_devices=1)
        args = [nc.dram_tensor(n, w.shape, F32, kind="ExternalInput").ap() for n, w in arrays.items()]
        args.append(nc.dram_tensor("out", (P, TT, D), F32, kind="ExternalOutput").ap())
        return nc, build(nc, args, known, per)

    _, first = program({}, {})
    nc, _ = program(first.marks, first.newper)
    got = run(nc, [arrays], core_ids=[0]).results[0]["out"]
    return got.transpose(1, 0, 2).reshape(1, SEQ, D)
```

```python
from contextlib import ExitStack, contextmanager

import numpy as np

import concourse.bass as bass
from concourse import mybir

F32 = mybir.dt.float32
I32 = mybir.dt.int32
U32 = mybir.dt.uint32
ALU = mybir.AluOpType
ACT = mybir.ActivationFunctionType
AX = mybir.AxisListType.X

P = 128
D = 1024
KD = D // P
SEQ = 256
TT = SEQ // P
HD1 = 64
A_HEADS, B_HEADS = 8, 4
NE, TOPK = 32, 4
LIMIT, ALPHA = 7.0, 1.702
LAMBDA_INIT = 0.2
EPS = 1e-6
CAP = 96
NPASS = -(-SEQ // CAP)
RING = 6
CPE = 12
MODW = 384
MOD1 = 6 * D // MODW
MODF = MODW // P
EARLY = 6
LAYERS = 2
H2, HD2, KV2 = 8, 128, 2
TAPS = 31
PADT = TAPS // 2
SEGW = SEQ + 2 * PADT
GELU_C = 2.0 * 0.7978845608028654

CH = {}


def _plan():
    c = 0

    def put(name, n):
        nonlocal c
        CH[name] = c
        c += n
    put("w_in", 12)
    put("w_out", 4)
    put("moe", NE * CPE)
    CH["after_moe"] = c
    for l in range(LAYERS):
        put(("cg", l), 8)
        put(("gu", l), 4)
        put(("gv", l), 4)
        for br in ("gmlp", "attn", "conv"):
            if br == "attn":
                put(("qkv", l), 6)
            for n in range(2):
                put(("gate", br, l, n), 2)
                put(("out", br, l, n), 2)
        put(("w_out", l), 4)
        for h in range(2):
            put(("ff1", l, h), 8)
            put(("ff2", l, h), 8)
    CH["total"] = c


_plan()

COL = {}


def _cols():
    c = 0

    def put(name, n):
        nonlocal c
        COL[name] = c
        c += n
    put("cond", 24)
    put("b_ada", 48)
    put("norm1", 8)
    put("norm2", 8)
    put("qk_a", 2)
    put("qk_b", 2)
    put("diff", 1)
    for l in range(LAYERS):
        for n, w in (("ada_b", 48), ("mix_pre", 8), ("mix_post", 8), ("gmlp_norm", 8), ("conv_b", 8),
                     ("conv_g", 8), ("conv_nb", 8), ("ffn_pre", 8), ("ffn_post", 8), ("conv_w", TAPS * 8)):
            put((n, l), w)
    put("b_gu", NE * 16)
    COL["total"] = c


_cols()
ROW = {"lam": 0, "qk": 256, "bs": 256 + 512, "b_router": 256 + 512 + 1024, "total": 256 + 512 + 1024 + 32}
CST = {}


def _cst():
    c = 0
    for name, n in (("ident", 128), ("ones", 128), ("tri", 128), ("iota", CAP), ("iotae", NE), ("cos", 128),
                    ("sin", 256), ("distA", 384), ("distB", 384), ("cnt", 384)):
        CST[name] = c
        c += n
    CST["total"] = c


_cst()

AREA = 31456
NSTAT = 640


class Signals:

    def __init__(self, nc, ctx, known, per):
        self.nc, self.ctx, self.known, self.per = nc, ctx, known, per
        self.sems, self.count, self.marks, self.newper = {}, {}, {}, {}
        self.tag, self.i, self.prefix, self.asked = None, None, "", -1

    def sem(self, name):
        if name not in self.sems:
            self.sems[name] = self.ctx.enter_context(self.nc.semaphore(name))
        return self.sems[name]

    def mark(self, name, *keys, inc=1):
        name = self.prefix + name
        self.count[name] = self.count.get(name, 0) + inc
        for key in keys:
            assert (self.prefix, key) not in self.marks, key
            self.marks[self.prefix, key] = (name, self.count[name], self.tag)
        return self.sem(name), inc

    def at(self, key, lag=0):
        found = self.known.get((self.prefix, key)) or self.known.get(("", key))
        if found is None:
            assert not self.known, key
            return self.sem("unknown"), 1
        name, v, tag = found
        step, trips = self.per.get((tag, name), (0, 1))
        if tag is not None and tag == self.tag:
            v -= lag * step
            assert v >= 1, (key, v)
            return self.sem(name), self.i * step + v
        return self.sem(name), v + step * (trips - 1)

    def last(self, name):
        name = self.prefix + name
        if self.tag is None:
            return self.sem(name), self.count[name]
        return self.sem(name), self.i * self.per.get((self.tag, name), (1, 1))[0] + self.count[name]

    @contextmanager
    def loop(self, eng, tag, trips):
        start = dict(self.count)
        self.tag = self.prefix + tag
        with eng.Fori(0, trips) as i:
            self.i = i
            yield i
        for name, n in list(self.count.items()):
            d = n - start.get(name, 0)
            if d:
                self.newper[self.tag, name] = (d, trips)
                self.count[name] += d * (trips - 1)
        self.tag = None


def build(nc, args, known, per):
    stream, mods_d, cols_d, rows_d, cst_d, x_d, ctx_d, ws_d, wr_d, bd_d, out_d = args
    with ExitStack() as ctx:
        def sb(name, shape, dt=F32):
            return ctx.enter_context(nc.sbuf_tensor(name, shape, dt))

        ring = sb("ring", [P, RING, 4, 512])
        cols = sb("cols", [P, COL["total"]])
        rows = sb("rows", [P, ROW["total"]])
        cst = sb("cst", [P, CST["total"]])
        ws = sb("ws", [P, LAYERS, 4, P])
        x = sb("x", [P, TT, D])
        mod = sb("mod", [P, 48])
        modb = sb("modb", [P, 2, 48])
        aff = sb("aff", [P, 8, KD])
        cond = sb("cond", [P, 24])
        stats = sb("stats", [P, NSTAT])
        area = sb("area", [P, AREA])
        flag = sb("flag", [P, 2], I32)
        idx = sb("idx", [P, TT, 8], U32)
        ps = ctx.enter_context(nc.psum_tensor("ps", [P, 8, 512], F32))
        K = Signals(nc, ctx, known, per)
        mark, at, last = K.mark, K.at, K.last
        landed = [K.sem(f"weights_landed{s}") for s in range(RING)]
        mods_landed = [K.sem(f"modulation_weights_landed{s}") for s in range(2)]

        def v(off, *shape):
            n = int(np.prod(shape))
            assert off + n <= AREA, (off, n)
            ap = area[:, off:off + n]
            if len(shape) == 2:
                ap = ap.rearrange("p (a b) -> p a b", a=shape[0])
            if len(shape) == 3:
                ap = ap.rearrange("p (a b c) -> p a b c", a=shape[0], b=shape[1])
            return ap

        stat_at = {}
        stat_n = [0]

        def stat(key, n=1):
            if isinstance(key, tuple) and key[-1] in ("ms", "rt", "rstd"):
                key = key[:-1] + ("ssq",)
            if key not in stat_at:
                stat_at[key] = stat_n[0]
                stat_n[0] += n
                assert stat_n[0] <= NSTAT, stat_n
            return stats[:, stat_at[key]:stat_at[key] + n]

        def col(name, i=0, n=1):
            return cols[:, COL[name] + i:COL[name] + i + n]

        def con(name, n, off=0):
            return cst[:, CST[name] + off:CST[name] + off + n]

        ident, ones = con("ident", P), con("ones", P)

        B1 = 2048
        xn1 = v(B1, TT, D)
        hT1 = v(B1 + 2048, KD, SEQ)
        proj = v(B1 + 4096, TT, 3072)
        qkT = v(B1 + 10240, 4, 4, SEQ)
        o1 = v(B1 + 14336, TT, D)
        sbuf_s = v(B1 + 16384, 2, 384)
        sbuf_e = v(B1 + 17152, 4, 384)
        sbuf_p = v(B1 + 18688, 2, 384)
        sbuf_pt = v(B1 + 19456, 2, 384)
        junk1 = v(B1 + 20224, D)
        sq1 = v(B1 + 21248, 512)
        xT = v(B1 + 4096, KD, CAP)
        gbuf = v(B1 + 4864, 2, 4 * CAP)
        ubuf = v(B1 + 5632, 2, 4 * CAP)
        sbuf_g = v(B1 + 6400, 2, 4 * CAP)
        actb = v(B1 + 7168, KD, CAP)
        ysb = v(B1 + 7936, D)
        yacc = v(B1 + 8960, KD, SEQ)
        sel = v(B1 + 11008, TT, CAP)
        selg = v(B1 + 11200, TT, CAP)
        selgT = v(B1 + 11392, SEQ)
        slot = v(B1 + 11648, NE + 1, TT)
        gate = v(B1 + 11714, NE, TT)
        lgt = v(B1 + 11778, TT, NE)
        top8 = v(B1 + 11842, TT, 8)
        idxf = v(B1 + 11858, TT, 8)
        gex = v(B1 + 11874, TT, 8)
        pick = v(B1 + 11890, TT, NE)
        gpick = v(B1 + 11954, TT, NE)
        eqb = v(B1 + 12018, TT, NE)
        gateT = v(B1 + 12082, SEQ)
        wr = v(23808, KD, NE)
        bdn = v(24064, D)
        mods = v(25088, 2, KD * MODW)

        def part1(g):
            return v(B1 + 14336 if g == EARLY - 1 else MODW * (g % EARLY if g < EARLY else g - EARLY), MODW)
        part2 = v(B1 + 13640, 2, MODW)
        mod2 = con("distA", 2 * 48 * LAYERS).rearrange("p (l f s) -> p l s f", l=LAYERS, s=2)
        mod2w = con("distA", 2 * 48 * LAYERS)
        bgu = v(B1 + 13618, 16)
        ctxr = v(0, TT, D)
        hT = v(2048, KD, 512)
        merged = v(6144, KD, 512)
        glp = v(10240, KD, 2, SEGW)
        xnb = v(18912, 4, D)
        hid = v(10240, 16, 512)
        cv = v(14816, KD, 512)
        uT = v(18912, KD, 512)
        yb = v(18912, 4, D)
        gv = v(23008, 4, D)
        kT = v(23008, KV2, 512)
        vb = v(24032, 4, 256)
        bcv = v(25056, 2, D)
        tmp = v(27104, 8, 512)

        scr = v(25056, 4, 512)
        ptb = [v(25056, 4, SEQ), v(26080, 4, SEQ)]
        glsq = v(10240, KD, 512)
        dgb = [v(10240, 16, P), v(6144, 16, P)]
        condv = cond[:, 8:24].rearrange("p (s k) -> p k s", s=2)
        xn1v = v(B1, KD, SEQ)
        spill_landed = [K.sem(f"spill_weights_landed{s}") for s in range(RING)]
        units_of = {l: [(h, s) for h in range(H2) for s in range((4 - 2 * l) // 2)] for l in range(LAYERS)}

        junk1b = v(B1 + 20224, D)
        junkb = v(27104 + 2048, D)

        def gelu_items(l):
            nt = 4 if l == 0 else 2
            L = f"L{l}"
            return ([((( L, "gu"), f), uT[:, f, 0:nt * P], nt * P) for f in range(KD)]
                    + [(((L, "gv", g), t), gv[:, t, 512 * g:512 * g + 512], 512) for g in range(2) for t in range(nt)])

        bank_of, users = {}, {}
        block = ctx.enter_context(nc.Block())

        @block.tensor
        def _(pe):
            mm = nc.tensor.matmul
            nxt = {"acc": 0, "aux": 0}

            def claim(pool, key):
                b = (0 if pool == "acc" else 4) + nxt[pool] % 4
                nxt[pool] += 1
                if b in users:
                    pe.wait_ge(*at(("drained", users[b])))
                users[b] = key
                bank_of[key] = b
                return b

            def chunk(c):
                if c > K.asked:
                    pe.wait_ge(landed[c % RING], 16 * (c // RING + 1))
                    K.asked = c
                return ring[:, c % RING]

            def closed(ins, key, c, last_of_chunk, last_of_group):
                if last_of_chunk:
                    ins.then_inc(*mark("weights_used", ("chunk", c), *([("full", key)] if last_of_group else [])))
                elif last_of_group:
                    ins.then_inc(*mark("product_full", ("full", key)))

            def features(first, kgs, rhs, n, key, j0=0, nb=4, ready=None):
                for j in range(nb):
                    b = claim("acc", (key, j0 + j))
                    for k in range(4 * kgs):
                        if ready and j == 0:
                            pe.wait_ge(*at(ready[k]))
                        w = chunk(first + k // 4)
                        i = mm(ps[:, b, 0:n], w[:, k % 4, j * P:(j + 1) * P], rhs(k),
                               start=(k == 0), stop=(k == 4 * kgs - 1))
                        closed(i, (key, j0 + j), first + k // 4, j == nb - 1 and k % 4 == 3, k == 4 * kgs - 1)

            def tokens(first, kgs, lhs, tiles, key, ready=None):
                for t in range(tiles):
                    b = claim("acc", (key, t))
                    for k in range(4 * kgs):
                        if ready and t == 0:
                            pe.wait_ge(*at(ready[k]))
                        w = chunk(first + k // 4)
                        i = mm(ps[:, b, :], lhs(k, t), w[:, k % 4, :], start=(k == 0), stop=(k == 4 * kgs - 1))
                        closed(i, (key, t), first + k // 4, t == tiles - 1 and k % 4 == 3, k == 4 * kgs - 1)

            def close_sums(key, chunks, b):
                for m, g in enumerate(chunks):
                    pe.wait_ge(*at(("part", g)))
                    for j in range(MODF):
                        f = MODF * m + j
                        i = mm(ps[:, b, f:f + 1], part1(g)[:, j * P:(j + 1) * P], ones[:, 0:1], start=True, stop=True)
                i.then_inc(*mark("modulation_full", ("full", key)))

            def turn(src, key, n, ready):
                b = claim("aux", key)
                for r in ready:
                    pe.wait_ge(*at(r))
                for j in range(n):
                    i = nc.tensor.transpose(ps[:, b, j * P:(j + 1) * P], src(j), ident)
                i.then_inc(*mark("turned", ("full", key)))

            pe.wait_ge(*at("cst"))
            close_sums("ada", range(EARLY), claim("aux", "ada"))
            for k in range(KD):
                turn(lambda t: xn1[:, t, k * P:(k + 1) * P], ("h1", k), TT, ["xn1"])
            for g in range(6):
                tokens(CH["w_in"] + 2 * g, 2, lambda k, t: hT1[:, k, t * P:(t + 1) * P], TT, ("proj", g),
                       None if g else [("drained", ("h1", k)) for k in range(KD)])
            for m in range(4):
                for t in range(TT):
                    c0 = (0, 512, 1536, 2048)[m] + 0
                    turn(lambda j: proj[:, t, c0 + j * P:c0 + (j + 1) * P], ("qk", m, t), 4, [("qkn", m)])

            def head(key, q, k, hp, lo):
                b = claim("acc", key)
                for m in (q, k):
                    for t in range(TT):
                        pe.wait_ge(*at(("drained", ("qk", m, t))))
                for t in range(TT):
                    n = P * (t + 1)
                    i = mm(ps[:, b, P * t:P * t + n], qkT[lo:lo + HD1, q, hp, t * P:(t + 1) * P],
                           qkT[lo:lo + HD1, k, hp, 0:n], start=True, stop=True)
                i.then_inc(*mark("scores_full", ("full", key)))

            def weigh(key, vcol, n):
                turn(lambda j: sbuf_p[:, key[1] % 2, j * P:(j + 1) * P], ("pt",) + key, 3, [("prob",) + key])
                b = claim("aux", ("o",) + key)
                pe.wait_ge(*at(("drained", ("pt",) + key)))
                pt = sbuf_pt[:, key[1] % 2]
                for t in range(TT):
                    for s in range(t + 1):
                        i = mm(ps[:, b, t * n:(t + 1) * n], pt[:, (t + s) * P:(t + s + 1) * P],
                               proj[:, s, vcol:vcol + n], start=(s == 0), stop=(s == t))
                i.then_inc(*mark("heads_full", ("full", ("o",) + key)))

            for h in range(A_HEADS + 1):
                if h < A_HEADS:
                    head(("A", h), 0, 1, h // 2, HD1 * (h % 2))
                if h:
                    weigh(("A", h - 1), 1024 + HD1 * (h - 1), HD1)
                    close_sums(("ada", h), [EARLY + h - 1], claim("aux", ("ada", h)))
            for h in range(B_HEADS + 1):
                if h < B_HEADS:
                    for c in range(2):
                        head(("B", h, c), 2, 3, h, HD1 * c)
                if h:
                    weigh(("B", h - 1), 2560 + P * (h - 1), P)
                if h in (1, 2):
                    g = EARLY + A_HEADS + h - 1
                    close_sums(("ada", g), [g], claim("aux", ("ada", g)))
            for k in range(KD):
                turn(lambda t: o1[:, t, k * P:(k + 1) * P], ("oT", k), TT, ["oA" if k < 4 else "oB"])
            for g in range(2):
                features(CH["w_out"] + 2 * g, 2, lambda k: hT1[:, k, :], SEQ, "mix", 4 * g,
                         ready=None if g else [("drained", ("oT", k)) for k in range(KD)])
            for t in range(TT):
                for g in range(2):
                    turn(lambda j: xn1v[:, 4 * g + j, t * P:(t + 1) * P], ("mixT", t, g), 4,
                         [("drained", ("mix", 4 * g + 3)), ("drained", ("mix", 4 * g + 2))])
            for k in range(KD):
                turn(lambda t: xn1[:, t, k * P:(k + 1) * P], ("h2", k), TT, ["xn2"])
            b = claim("aux", "logits")
            pe.wait_ge(*at("wr"))
            for t in range(TT):
                for k in range(KD):
                    if t == 0:
                        pe.wait_ge(*at(("drained", ("h2", k))))
                    i = mm(ps[:, b, t * NE:(t + 1) * NE], hT1[:, k, t * P:(t + 1) * P], wr[:, k, :],
                           start=(k == 0), stop=(k == KD - 1))
            i.then_inc(*mark("router_full", ("full", "logits")))
            b = claim("aux", "rank")
            pe.wait_ge(*at("pick"))
            pe.wait_ge(*at("tables"))
            for t in range(TT):
                if t:
                    mm(ps[:, b, t * NE:(t + 1) * NE], ones, pick[:, 0, :], start=True, stop=False)
                mm(ps[:, b, t * NE:(t + 1) * NE], con("tri", P), pick[:, t, :], start=(t == 0), stop=True)
            for t in range(TT):
                i = mm(ps[:, b, 2 * NE:3 * NE], ones, pick[:, t, :], start=(t == 0), stop=(t == TT - 1))
            i.then_inc(*mark("router_full", ("full", "rank")))
            b = claim("aux", "gateT")
            pe.wait_ge(*at("gpick"))
            for t in range(TT):
                i = nc.tensor.transpose(ps[0:NE, b, t * P:(t + 1) * P], gpick[:, t, :], ident)
            i.then_inc(*mark("router_full", ("full", "gateT")))
            pe.wait_ge(*at(("drained", "gateT")))
            pe.wait_ge(*at("bdn"))
            for g in range(4):
                b = claim("aux", ("bias", g))
                for j in range(2):
                    i = mm(ps[:, b, j * SEQ:(j + 1) * SEQ], bdn[0:NE, (2 * g + j) * P:(2 * g + j + 1) * P],
                           gateT[0:NE, :], start=True, stop=True)
                i.then_inc(*mark("router_full", ("full", ("bias", g))))

            for key in [k for k in users.values()]:
                pe.wait_ge(*at(("drained", key)))

            def expert_chunk(ci, wait_it):
                s = (CH["moe"] + ci) % RING
                if wait_it:
                    if K.prefix:
                        base = 16 * (2 * NE * (K.spill_pass) + ci // RING + 1)
                        pe.wait_ge(spill_landed[s], K.i * 32 + base)
                    else:
                        pe.wait_ge(landed[s], K.i * 32 + 16 * ((CH["moe"] + ci) // RING + 1))
                return ring[:, s]

            def gather(gk):
                for g in range(2):
                    for j in range(4):
                        k = 4 * g + j
                        for t in range(TT):
                            i = mm(ps[:, 4 + g, j * CAP:(j + 1) * CAP], xn1[:, t, k * P:(k + 1) * P],
                                   sel[:, t, :], start=(t == 0), stop=(t == TT - 1))
                    i.then_inc(*mark("gather_full", ("full", (gk, g))))

            def scatter(lag_tag, first_wait):
                for g in range(4):
                    b = (6, 7, 4, 5)[g]
                    first_wait(g)
                    for j in range(2):
                        k = 2 * g + j
                        i = mm(ps[:, b, j * SEQ:(j + 1) * SEQ], ysb[0:CAP, k * P:(k + 1) * P],
                               selgT[0:CAP, :], start=True, stop=True)
                    i.then_inc(*mark("scatter_full", ("full", (lag_tag, g))))

            def experts(tag):
                pe.wait_ge(*at(("sel0", tag)))
                gather(("g0", tag))
                with K.loop(pe, tag, NE):
                    for g in range(4):
                        if g < 2:
                            pe.wait_ge(*at((tag, "xT", g), lag=1))
                        if g == 0:
                            pe.wait_ge(*at((tag, "selgT"), lag=1))
                            pe.wait_ge(*at((tag, "xT", 1), lag=1))
                        pe.wait_ge(*at((tag, "h", g), lag=1))
                        if tag == "moe" and g == 3:
                            pe.wait_ge(*at((tag, "part")))
                            for j in range(MODF):
                                for s in range(2):
                                    i = mm(ps[:, 3, 4 * CAP + 2 * j + s:4 * CAP + 2 * j + s + 1], part2[:, s, j * P:(j + 1) * P], ones[:, 0:1],
                                           start=True, stop=True)
                            i.then_inc(*mark("modulation_full", (tag, "mod2")))
                        for j in range(4):
                            for k in range(KD):
                                ci = 2 * g + k // 4
                                w = expert_chunk(ci, j == 0 and k % 4 == 0)
                                i = mm(ps[:, g, j * CAP:(j + 1) * CAP], w[:, k % 4, j * P:(j + 1) * P], xT[:, k, :],
                                       start=(k == 0), stop=(k == KD - 1))
                                if j == 3 and k % 4 == 3:
                                    i.then_inc(*mark("weights_used", (tag, "chunk", ci)))
                    pe.wait_ge(*at((tag, "sel")))
                    pe.wait_ge(*at((tag, "y+", 3), lag=1))
                    gather((tag, "g"))
                    def bank_read(g):
                        if g == 0:
                            pe.wait_ge(*at((tag, "y", 1), lag=1))
                        if g == 2:
                            pe.wait_ge(*at((tag, "xT", 1)))
                    scatter((tag, "s"), bank_read)
                    pe.wait_ge(*at((tag, "selg")))
                    pe.wait_ge(*at((tag, "h", 0)))
                    for t in range(TT):
                        i = nc.tensor.transpose(ps[0:CAP, 0, t * P:(t + 1) * P], selg[:, t, :], ident)
                    i.then_inc(*mark("gather_full", (tag, "selT")))
                    pe.wait_ge(*at((tag, "act", 1)))
                    for g in range(2):
                        pe.wait_ge(*at((tag, "y+", g)))
                        for k in range(KD):
                            ci = 8 + 2 * g + k // 4
                            w = expert_chunk(ci, k % 4 == 0)
                            i = mm(ps[0:CAP, 6 + g, :], actb[:, k, :], w[:, k % 4, :],
                                   start=(k == 0), stop=(k == KD - 1))
                            if k % 4 == 3:
                                i.then_inc(*mark("weights_used", (tag, "chunk", ci)))

                def last_read(g):
                    if g == 0:
                        pe.wait_ge(*at((tag, "y", 1)))
                        pe.wait_ge(*at((tag, "selgT")))
                    if g == 2:
                        pe.wait_ge(*at((tag, "y+", 3)))
                scatter(("s_end", tag), last_read)

            pe.wait_ge(*at(("zero", "moe")))
            experts("moe")
            pe.wait_ge(*at("flag"))
            over = nc.tensor.value_load(flag[0:1, 0:1], min_val=0, max_val=1)
            with nc.tensor.If(over > 0):
                K.prefix = "spill_"
                for p in range(1, NPASS):
                    K.spill_pass = p - 1
                    pe.wait_ge(*at(("y_end", f"moe{p - 1}" if p > 1 else "moe", 3)))
                    pe.wait_ge(*at(("zero", f"moe{p}")))
                    experts(f"moe{p}")
                pe.wait_ge(*at(("y_end", f"moe{NPASS - 1}", 3)))
                K.prefix = ""
            users.clear()
            for t in range(TT):
                for g in range(2):
                    turn(lambda j: yacc[:, 4 * g + j, t * P:(t + 1) * P], ("moeT", t, g), 4, ["yg"])

            for l in range(LAYERS):
                nt = 4 if l == 0 else 2
                N = nt * P
                L = f"L{l}"
                for k in range(KD):
                    turn(lambda t: xnb[:, t, k * P:(k + 1) * P], (L, "h", k), 4, [(L, "xn", t) for t in range(4)])
                hx = lambda k: hT[:, k, 0:N]
                for g in range(4):
                    features(CH["cg", l] + 2 * g, 2, hx, N, (L, "cg"), 4 * g,
                             ready=None if g else [("drained", (L, "h", k)) for k in range(KD)])
                for g in range(2):
                    features(CH["gu", l] + 2 * g, 2, hx, N, (L, "gu"), 4 * g)
                for g in range(2):
                    tokens(CH["gv", l] + 2 * g, 2, lambda k, t: hT[:, k, t * P:(t + 1) * P], nt, (L, "gv", g))
                def spatial():
                    pe.wait_ge(*at("ws"))
                    for f in range(KD):
                        b = claim("aux", (L, "sv", f))
                        pe.wait_ge(*at((L, "gvn")))
                        for t in range(nt):
                            i = mm(ps[:, b, t * P:(t + 1) * P], gv[:, t, f * P:(f + 1) * P], ws[:, l, f // 2, :],
                                   start=True, stop=True)
                        i.then_inc(*mark("mixed_full", ("full", (L, "sv", f))))

                def branch(br, src, ready, between=None, after_gate=None):
                    for g in range(2):
                        if g and between:
                            between()
                        features(CH["gate", br, l, g], 2, hx, N, (L, "gate", br), 4 * g)
                        if g == 0 and after_gate:
                            after_gate()
                        features(CH["out", br, l, g], 2, lambda k: src[:, k, 0:N], N, (L, "out", br), 4 * g,
                                 ready=None if g else ready)
                branch("gmlp", uT, [(L, "usv", f) for f in range(KD)], after_gate=spatial)
                for g in range(3):
                    tokens(CH["qkv", l] + 2 * g, 2, lambda k, t: hT[:, k, t * P:(t + 1) * P],
                           4 if g == 2 else nt, (L, "qkv", g))
                    for t in range(nt if g else 0):
                        turn(lambda j: tmp[:, t, j * P:(j + 1) * P], (L, "q", g - 1, t), 4, [(L, "qr", g - 1, t)])
                for t in range(4):
                    turn(lambda j: tmp[:, 4 + t % 4, j * P:(j + 1) * P], (L, "k", t), 2, [(L, "kr", t)])

                def attend(h, seg):
                    nk = 4 if seg == 0 else 2
                    k0 = 0 if seg == 0 else 2
                    key = (L, h, seg)
                    for t in range(TT):
                        b = claim("acc", (key, "s", t))
                        for tt in range(4):
                            pe.wait_ge(*at(("drained", (L, "k", tt))))
                        pe.wait_ge(*at(("drained", (L, "q", h // 4, 2 * seg + t))))
                        i = mm(ps[:, b, 0:nk * P], uT[:, h, (2 * seg + t) * P:(2 * seg + t + 1) * P],
                               kT[:, h // 4, k0 * P:(k0 + nk) * P], start=True, stop=True)
                        i.then_inc(*mark("scores_full", ("full", (key, "s", t))))

                def turn_probs(h, seg):
                    nk = 4 if seg == 0 else 2
                    key = (L, h, seg)
                    par = units.index((h, seg)) % 2
                    for t in range(TT):
                        turn(lambda j: tmp[:, 2 * par + t, j * P:(j + 1) * P], (key, "pt", t), nk, [(key, "p", t)])

                def average(h, seg):
                    nk = 4 if seg == 0 else 2
                    k0 = 0 if seg == 0 else 2
                    key = (L, h, seg)
                    par = units.index((h, seg)) % 2
                    b = claim("aux", (key, "o"))
                    for t in range(TT):
                        pe.wait_ge(*at(("drained", (key, "pt", t))))
                    for j in range(nk):
                        i = mm(ps[:, b, 0:SEQ], vb[:, k0 + j, (h // 4) * P:(h // 4 + 1) * P], ptb[par][:, j, :],
                               start=(j == 0), stop=(j == nk - 1))
                    i.then_inc(*mark("heads_full", ("full", (key, "o"))))
                units = units_of[l]
                for n in range(len(units) + 2):
                    if n < len(units):
                        attend(*units[n])
                    if 1 <= n <= len(units):
                        turn_probs(*units[n - 1])
                    if n >= 2:
                        average(*units[n - 2])

                def feature_sum(which, src, ready):
                    b = claim("aux", (L, which))
                    for k in range(KD):
                        pe.wait_ge(*at((L, ready, k)))
                        i = mm(ps[:, b, 0:N], ones, src[:, k, 0:N], start=(k == 0), stop=(k == KD - 1))
                    i.then_inc(*mark("mixed_full", ("full", (L, which))))
                def spread(which):
                    for s in range(nt // 2):
                        for g in range(2):
                            b = claim("aux", (L, "bc", which, s, g))
                            for j in range(4):
                                k = 4 * g + j
                                pe.wait_ge(*at((L, "dg", which, s, k)))
                                i = mm(ps[:, b, j * P:(j + 1) * P], ones, dgb[which][:, KD * s + k], start=True, stop=True)
                            i.then_inc(*mark("spread_full", ("full", (L, "bc", which, s, g))))

                branch("attn", uT, [("drained", ((L, h, nt // 2 - 1), "o")) for h in range(H2)],
                       lambda: feature_sum("mu", cv, "cv"))
                feature_sum("var", glsq, "cvsq")
                branch("conv", cv, [(L, "cvn", k) for k in range(KD)], lambda: spread(0))
                for g in range(2):
                    tokens(CH["w_out", l] + 2 * g, 2, lambda k, t: merged[:, k, t * P:(t + 1) * P], nt, (L, "wo", g),
                           None if g else [(L, "merged", k) for k in range(KD)])

                for k in range(KD):
                    turn(lambda t: xnb[:, t, k * P:(k + 1) * P], (L, "h2", k), nt, [(L, "xn2", t) for t in range(nt)])
                for hf in range(2):
                    for g in range(4):
                        features(CH["ff1", l, hf] + 2 * g, 2, hx, N, (L, "ff1", hf), 4 * g,
                                 ready=None if g or hf else [("drained", (L, "h2", k)) for k in range(KD)])
                    if hf == 0:
                        spread(1)
                    for g in range(2):
                        tokens(CH["ff2", l, hf] + 4 * g, 4, lambda k, t: hid[:, k, t * P:(t + 1) * P], nt, (L, "ff2", hf, g),
                               None if g else [(L, "hid", hf, j) for j in range(16)])
            return


        @block.vector
        def _(dve):
            V = nc.vector
            TS, TT_, STT = V.tensor_scalar, V.tensor_tensor, V.scalar_tensor_tensor

            def B(key):
                return bank_of[key]

            def rstd_of(key, n, width):
                dve.wait_ge(*at(("ssq", key)))
                TS(stat((key, "ms"), n), stat((key, "ssq"), n), 1.0 / width, EPS, ALU.mult, ALU.add).then_inc(*mark("means_ready", ("ms", key)))
                dve.wait_ge(*at(("root", key)))
                V.reciprocal(stat((key, "rstd"), n), stat((key, "rt"), n)).then_inc(*mark("vector_steps"))
                dve.wait_ge(*last("vector_steps"))
                return stat((key, "rstd"), n)

            dve.wait_ge(*at("cols"))
            dve.wait_ge(*at("cond_sig"))
            TT_(cond[:, :], cond[:, :], col("cond", 0, 24), ALU.mult).then_inc(*mark("cond_ready", "cond"))
            def partial_sums(g):
                dve.wait_ge(mods_landed[g % 2], 16 * (g // 2 + 1))
                w = mods[:, g % 2].rearrange("p (k n) -> p k n", k=KD)
                acc = part1(g)
                TS(acc, w[:, 0], cond[:, 0:1], None, ALU.mult).then_inc(*mark("partial_steps"))
                for k in range(1, KD):
                    dve.wait_ge(*last("partial_steps"))
                    STT(acc, w[:, k], cond[:, k:k + 1], acc, ALU.mult, ALU.add).then_inc(*mark("partial_steps", *([("part", g)] if k == KD - 1 else [])))

            def take_mod(key, f0, n):
                dve.wait_ge(*at(("full", key)))
                TT_(mod[:, f0:f0 + n], ps[:, B(key), 0:n], col("b_ada", f0, n), ALU.add).then_inc(*mark("vector_steps", ("drained", key)))
                dve.wait_ge(*last("vector_steps"))

            dve.wait_ge(*last("cond_ready"))
            for g in range(EARLY):
                if g == 2:
                    r = rstd_of("x1", TT, D)
                    for t in range(TT):
                        i = TS(xn1[:, t, :], x[:, t, :], r[:, t:t + 1], None, ALU.mult)
                    i.then_inc(*mark("normed", "xn1"))
                partial_sums(g)
            take_mod("ada", 0, EARLY * MODF)
            STT(aff[:, 0], mod[:, 8:16], 1.0, col("norm1", 0, 8), ALU.add, ALU.mult).then_inc(*mark("vector_steps"))
            dve.wait_ge(*last("vector_steps"))

            def modulate(name, A, sh):
                for k in range(KD):
                    dve.wait_ge(*at(("full", (name, k))))
                    TS(hT1[:, k, :], ps[:, B((name, k)), 0:SEQ], aff[:, A, k:k + 1], mod[:, sh + k:sh + k + 1],
                            ALU.mult, ALU.add).then_inc(*mark("modulated", ("drained", (name, k))))
            modulate("h1", 0, 0)
            dve.wait_ge(*at("rows"))
            for l in range(LAYERS):
                q = rows[:, ROW["qk"] + 256 * l:ROW["qk"] + 256 * l + P]
                TS(q, q, HD2 ** -0.5, None, ALU.mult).then_inc(*mark("vector_steps"))
                dve.wait_ge(*last("vector_steps"))
            lam = rows[:, 0:256].rearrange("p (a d) -> p a d", a=4)
            for m in range(2):
                TT_(junk1[:, 64 * m:64 * m + 64], lam[:, 2 * m], lam[:, 2 * m + 1], ALU.mult).then_inc(*mark("vector_steps"))
                dve.wait_ge(*last("vector_steps"))
            V.tensor_reduce(stat("ldot", 2), junk1[:, 0:128].rearrange("p (a d) -> p a d", a=2), AX, ALU.add).then_inc(*mark("lambda_dots", "ldot"))
            dve.wait_ge(*at("lexp"))
            TT_(stat("lam"), stat("lexp", 2)[:, 0:1], stat("lexp", 2)[:, 1:2], ALU.subtract).then_inc(*mark("vector_steps"))
            dve.wait_ge(*last("vector_steps"))
            TS(stat("lam"), stat("lam"), LAMBDA_INIT, None, ALU.add).then_inc(*mark("vector_steps"))
            dve.wait_ge(*last("vector_steps"))

            heads = lambda m, t: proj[:, t, (0, 512, 1536, 2048)[m]:(0, 512, 1536, 2048)[m] + 512].rearrange(
                "p (h d) -> p h d", d=HD1)
            for m in range(4):
                for g in ((6, 7), (8, 9), (10, 11, 12, 13), ())[m]:
                    partial_sums(g)
                for t in range(TT):
                    dve.wait_ge(*at(("drained", (("proj", (0, 1, 3, 4)[m]), t))))
                    TT_(sq1.rearrange("p (h d) -> p h d", d=HD1), heads(m, t), heads(m, t), ALU.mult).then_inc(*mark("vector_steps"))
                    dve.wait_ge(*last("vector_steps"))
                    V.tensor_reduce(stat((("qk", m), "ssq"), 16)[:, 8 * t:8 * t + 8],
                                         sq1.rearrange("p (h d) -> p h d", d=HD1), AX, ALU.add).then_inc(*mark("vector_steps", *([("ssq", ("qk", m))] if t else [])))
                    dve.wait_ge(*last("vector_steps"))
                r = rstd_of(("qk", m), 16, HD1)
                for t in range(TT):
                    i = TT_(heads(m, t), heads(m, t), r[:, 8 * t:8 * t + 8].unsqueeze(2).to_broadcast([P, 8, HD1]), ALU.mult)
                i.then_inc(*mark("normed", ("qkn", m)))
            for m in range(4):
                for t in range(TT):
                    dve.wait_ge(*at(("full", ("qk", m, t))))
                    g = col("qk_a" if m < 2 else "qk_b", m % 2)
                    TS(qkT[:, m, :, t * P:(t + 1) * P],
                            ps[:, B(("qk", m, t)), :].rearrange("p (a q) -> p a q", a=4), g,
                            HD1 ** -0.5 if m % 2 == 0 else 1.0, ALU.mult, ALU.mult).then_inc(*mark("turned_read", ("drained", ("qk", m, t))))

            dve.wait_ge(*at("tables"))

            def masked(key, dist, slope, sb_):
                dve.wait_ge(*at(("full", key)))
                STT(sbuf_s[:, sb_], con(dist, 384), -slope, ps[:, B(key), 0:384], ALU.mult, ALU.add).then_inc(*mark("vector_steps", ("drained", key)))
                dve.wait_ge(*last("vector_steps"))
                for t in range(TT):
                    i = V.tensor_reduce(stat((key, "nm"), 2)[:, t:t + 1], sbuf_s[:, sb_, P * t:P * t + P * (t + 1)],
                                        AX, ALU.max, negate=True)
                i.then_inc(*mark("maxima_ready", ("nm", key)))

            def outA(h):
                key = ("o", "A", h)
                dve.wait_ge(*at(("full", key)))
                i = TT_(o1[:, :, HD1 * h:HD1 * h + HD1], ps[:, B(key), 0:128].rearrange("p (t d) -> p t d", t=TT),
                        stat((("A", h), "rden"), 2).unsqueeze(2).to_broadcast([P, TT, HD1]), ALU.mult)
                i.then_inc(*mark("heads_read", ("drained", key), *(["oA"] if h == A_HEADS - 1 else [])))

            for h in range(A_HEADS + 1):
                if h < A_HEADS:
                    masked(("A", h), "distA", 2.0 ** -(h + 1), h % 2)
                if h in (1, 4):
                    partial_sums({1: 14, 4: 15}[h])
                if h < A_HEADS:
                    dve.wait_ge(*at(("exp", ("A", h))))
                    for t in range(TT):
                        sl = slice(P * t, P * t + P * (t + 1))
                        i = V.tensor_tensor_reduce(sbuf_p[:, h % 2, sl], sbuf_e[:, h % 4, sl], con("cnt", 384)[:, sl], 1.0, 0.0,
                                                   ALU.mult, ALU.add, stat((("A", h), "den"), 2)[:, t:t + 1])
                    i.then_inc(*mark("vector_steps", ("prob", "A", h)))
                    dve.wait_ge(*last("vector_steps"))
                    V.reciprocal(stat((("A", h), "rden"), 2), stat((("A", h), "den"), 2)).then_inc(*mark("vector_steps"))
                    dve.wait_ge(*last("vector_steps"))
                if h:
                    outA(h - 1)
                    take_mod(("ada", h), MODF * (EARLY + h - 1), MODF)

            def outB(h):
                key = ("o", "B", h)
                dve.wait_ge(*at(("full", key)))
                ov = o1[:, :, 512 + P * h:512 + P * h + P]
                V.tensor_copy(ov, ps[:, B(key), 0:256].rearrange("p (t d) -> p t d", t=TT)).then_inc(*mark("vector_steps", ("drained", key)))
                dve.wait_ge(*last("vector_steps"))
                sv_ = sq1[:, 0:256].rearrange("p (t d) -> p t d", t=TT)
                TT_(sv_, ov, ov, ALU.mult).then_inc(*mark("vector_steps"))
                dve.wait_ge(*last("vector_steps"))
                V.tensor_reduce(stat(("oB", "ssq"), 8).rearrange("p (t h) -> p h t", h=4)[:, h], sv_, AX, ALU.add).then_inc(*mark("vector_steps", *([("ssq", "oB")] if h == B_HEADS - 1 else [])))
                dve.wait_ge(*last("vector_steps"))

            for h in range(B_HEADS + 1):
                if h < B_HEADS:
                    for c in range(2):
                        masked(("B", h, c), "distB", 2.0 ** (-2 * (h + 1)), c)
                if h < B_HEADS:
                    for c in range(2):
                        dve.wait_ge(*at(("exp", ("B", h, c))))
                        V.reciprocal(stat(("B", h, c, "rd"), 2), stat((("B", h, c), "den"), 2)).then_inc(*mark("vector_steps"))
                        dve.wait_ge(*last("vector_steps"))
                    rd0, rd1 = stat(("B", h, 0, "rd"), 2), stat(("B", h, 1, "rd"), 2)
                    TS(rd1, rd1, stat("lam"), None, ALU.mult).then_inc(*mark("vector_steps"))
                    dve.wait_ge(*last("vector_steps"))
                    e0, e1 = 2 * (h % 2), 2 * (h % 2) + 1
                    for t in range(TT):
                        sl = slice(P * t, P * t + P * (t + 1))
                        TS(sbuf_e[:, e1, sl], sbuf_e[:, e1, sl], rd1[:, t:t + 1], None, ALU.mult).then_inc(*mark("vector_steps"))
                        dve.wait_ge(*last("vector_steps"))
                        STT(sbuf_p[:, h % 2, sl], sbuf_e[:, e0, sl], rd0[:, t:t + 1], sbuf_e[:, e1, sl],
                                 ALU.mult, ALU.subtract).then_inc(*mark("vector_steps", *([("prob", "B", h)] if t else [])))
                        dve.wait_ge(*last("vector_steps"))
                if h:
                    outB(h - 1)
                if h in (1, 2):
                    g = EARLY + A_HEADS + h - 1
                    take_mod(("ada", g), MODF * g, MODF)
            STT(aff[:, 1], mod[:, 32:40], 1.0, col("norm2", 0, 8), ALU.add, ALU.mult).then_inc(*mark("vector_steps"))
            dve.wait_ge(*last("vector_steps"))
            r = rstd_of("oB", 8, 2 * HD1)
            TS(r, r, 1.0 - LAMBDA_INIT, None, ALU.mult).then_inc(*mark("vector_steps"))
            dve.wait_ge(*last("vector_steps"))
            for t in range(TT):
                ov = o1[:, t, 512:1024].rearrange("p (h d) -> p h d", h=4)
                i = TT_(ov, ov, r[:, 4 * t:4 * t + 4].unsqueeze(2).to_broadcast([P, 4, P]), ALU.mult)
            i.then_inc(*mark("normed", "oB"))
            for k in range(KD):
                dve.wait_ge(*at(("full", ("oT", k))))
                g = col("diff") if k >= 4 else 1.0
                TS(hT1[:, k, :], ps[:, B(("oT", k)), 0:SEQ], g, None, ALU.mult).then_inc(*mark("turned_read", ("drained", ("oT", k))))
            for k in range(KD):
                dve.wait_ge(*at(("full", ("mix", k))))
                TS(xn1v[:, k, :], ps[:, B(("mix", k)), 0:SEQ], mod[:, 16 + k:17 + k], None, ALU.mult).then_inc(*mark("gated", ("drained", ("mix", k))))
            for t in range(TT):
                for g in range(2):
                    dve.wait_ge(*at(("full", ("mixT", t, g))))
                    xs = x[:, t, 512 * g:512 * g + 512]
                    TT_(xs, xs, ps[:, B(("mixT", t, g)), :], ALU.add).then_inc(*mark("x_updated", ("drained", ("mixT", t, g)), *(["x1"] if t == 1 and g == 1 else [])))
            V.memset(ysb, 0.0).then_inc(*mark("vector_steps"))
            r = rstd_of("x2", TT, D)
            for t in range(TT):
                i = TS(xn1[:, t, :], x[:, t, :], r[:, t:t + 1], None, ALU.mult)
            i.then_inc(*mark("normed", "xn2"))
            modulate("h2", 1, 24)
            dve.wait_ge(*at(("full", "logits")))
            TT_(lgt, ps[:, B("logits"), 0:2 * NE].rearrange("p (t e) -> p t e", t=TT),
                     rows[:, ROW["b_router"]:ROW["b_router"] + NE].unsqueeze(1).to_broadcast([P, TT, NE]), ALU.add).then_inc(*mark("vector_steps", ("drained", "logits")))
            dve.wait_ge(*last("vector_steps"))
            for t in range(TT):
                V.max(top8[:, t, :], lgt[:, t, :]).then_inc(*mark("vector_steps"))
                dve.wait_ge(*last("vector_steps"))
                V.max_index(idx[:, t, :], top8[:, t, :], lgt[:, t, :]).then_inc(*mark("vector_steps"))
                dve.wait_ge(*last("vector_steps"))
                V.tensor_copy(idxf[:, t, :], idx[:, t, :]).then_inc(*mark("vector_steps"))
                dve.wait_ge(*last("vector_steps"))
                TS(gex[:, t, 0:TOPK], top8[:, t, 0:TOPK], top8[:, t, 0:1], None, ALU.subtract).then_inc(*mark("vector_steps", ("gdiff", t)))
                dve.wait_ge(*last("vector_steps"))
            for t in range(TT):
                dve.wait_ge(*at(("gexp", t)))
                V.reciprocal(stat(("gr", t)), stat(("gsum", t))).then_inc(*mark("vector_steps"))
                dve.wait_ge(*last("vector_steps"))
                TS(gex[:, t, 0:TOPK], gex[:, t, 0:TOPK], stat(("gr", t)), None, ALU.mult).then_inc(*mark("vector_steps"))
                dve.wait_ge(*last("vector_steps"))
            iotae = con("iotae", NE)
            for t in range(TT):
                for j in range(TOPK):
                    ix, gj = idxf[:, t, j:j + 1], gex[:, t, j:j + 1]
                    if j == 0:
                        TS(pick[:, t, :], iotae, ix, None, ALU.is_equal).then_inc(*mark("vector_steps"))
                        dve.wait_ge(*last("vector_steps"))
                        TS(gpick[:, t, :], iotae, ix, gj, ALU.is_equal, ALU.mult).then_inc(*mark("vector_steps"))
                        dve.wait_ge(*last("vector_steps"))
                    else:
                        STT(pick[:, t, :], iotae, ix, pick[:, t, :], ALU.is_equal, ALU.add).then_inc(*mark("vector_steps", *(["pick"] if t and j == TOPK - 1 else [])))
                        dve.wait_ge(*last("vector_steps"))
                        TS(eqb[:, t, :], iotae, ix, gj, ALU.is_equal, ALU.mult).then_inc(*mark("vector_steps"))
                        dve.wait_ge(*last("vector_steps"))
                        TT_(gpick[:, t, :], gpick[:, t, :], eqb[:, t, :], ALU.add).then_inc(*mark("vector_steps", *(["gpick"] if t and j == TOPK - 1 else [])))
                        dve.wait_ge(*last("vector_steps"))
            V.memset(slot[:, NE, :], 4000.0).then_inc(*mark("vector_steps"))
            dve.wait_ge(*last("vector_steps"))
            dve.wait_ge(*at(("full", "rank")))
            for t in range(TT):
                STT(slot[:, 0:NE, t], pick[:, t, :], -1000.0, ps[:, B("rank"), t * NE:(t + 1) * NE], ALU.mult, ALU.add).then_inc(*mark("vector_steps"))
                dve.wait_ge(*last("vector_steps"))
                V.tensor_copy(gate[:, :, t], gpick[:, t, :]).then_inc(*mark("vector_steps"))
                dve.wait_ge(*last("vector_steps"))
            TS(slot[:, 0:NE, :], slot[:, 0:NE, :], 1000.0, None, ALU.add).then_inc(*mark("vector_steps"))
            dve.wait_ge(*last("vector_steps"))
            V.tensor_reduce(stat("most"), ps[:, B("rank"), 2 * NE:3 * NE], AX, ALU.max).then_inc(*mark("vector_steps", ("drained", "rank")))
            dve.wait_ge(*last("vector_steps"))
            TS(flag[:, 0:1], stat("most"), float(CAP), None, ALU.is_gt).then_inc(*mark("vector_steps", "flag"))
            dve.wait_ge(*last("vector_steps"))
            dve.wait_ge(*at(("full", "gateT")))
            V.tensor_copy(gateT[0:NE, :], ps[0:NE, B("gateT"), 0:SEQ]).then_inc(*mark("vector_steps", ("drained", "gateT")))
            dve.wait_ge(*last("vector_steps"))
            for g in range(4):
                dve.wait_ge(*at(("full", ("bias", g))))
                V.tensor_copy(yacc[:, 2 * g:2 * g + 2, :], ps[:, B(("bias", g)), :].rearrange("p (j q) -> p j q", j=2)).then_inc(*mark("vector_steps", ("drained", ("bias", g))))
                dve.wait_ge(*last("vector_steps"))

            dve.wait_ge(*at("more_cols"))

            def normalise(L, norm, t, ready):
                r = rstd_of(((L, norm), t), 1, D)
                src = x[:, t, :] if t < TT else ctxr[:, t - TT, :]
                TS(xnb[:, t, :], src, r, None, ALU.mult).then_inc(*mark("normed", (L, ready, t)))
            for t in range(TT, 2 * TT):
                normalise("L0", "n1", t, "xn")

            iot = con("iota", CAP).unsqueeze(1).to_broadcast([P, TT, CAP])

            def gathered(gk, names):
                for g in range(2):
                    dve.wait_ge(*at(("full", (gk, g))))
                    for j in range(4):
                        k = 4 * g + j
                        i = TS(xT[:, k, :], ps[:, 4 + g, j * CAP:(j + 1) * CAP], aff[:, 1, k:k + 1],
                               mod[:, 24 + k:25 + k], ALU.mult, ALU.add)
                        if j < 2 and names == "first":
                            i.then_inc(*mark("products_read"))
                        if j == 3:
                            i.then_inc(*mark("inputs_ready", *([] if names == "first" else [names + (g,)])))

            def summed(sk, names):
                for g in range(4):
                    dve.wait_ge(*at(("full", (sk, g))))
                    ya = yacc[:, 2 * g:2 * g + 2, :]
                    TT_(ya, ya, ps[:, (6, 7, 4, 5)[g], :].rearrange("p (j q) -> p j q", j=2), ALU.add).then_inc(*mark("sums_updated", names + (g,)))

            def experts(tag):
                V.memset(selgT, 0.0).then_inc(*mark("vector_steps", ("zero", tag)))
                dve.wait_ge(*last("vector_steps"))
                V.memset(stat(("primer", tag)), 0.0).then_inc(*mark("sums_updated"))
                TT_(sel, iot, slot[:, 0:1, :].rearrange("p e t -> p t e").to_broadcast([P, TT, CAP]), ALU.is_equal).then_inc(*mark("vector_steps", ("sel0", tag)))
                dve.wait_ge(*last("vector_steps"))
                gathered(("g0", tag), "first")
                with K.loop(dve, tag, NE) as e:
                    V.tensor_copy(bgu, cols[:, bass.ds(e * 16 + COL["b_gu"], 16)]).then_inc(*mark("vector_steps"))
                    dve.wait_ge(*last("vector_steps"))
                    row = lambda a, n: a[:, bass.ds(e + n, 1), :].rearrange("p e t -> p t e").to_broadcast([P, TT, CAP])
                    dve.wait_ge(*at((tag, "selT"), lag=1))
                    TT_(selg, iot, row(slot, 0), ALU.is_equal).then_inc(*mark("vector_steps"))
                    dve.wait_ge(*last("vector_steps"))
                    TT_(selg, selg, row(gate, 0), ALU.mult).then_inc(*mark("vector_steps", (tag, "selg")))
                    dve.wait_ge(*last("vector_steps"))
                    dve.wait_ge(*at(("full", ((tag, "g"), 1)), lag=1))
                    TT_(sel, iot, row(slot, 1), ALU.is_equal).then_inc(*mark("vector_steps", (tag, "sel")))
                    dve.wait_ge(*last("vector_steps"))
                    if tag == "moe":
                        dve.wait_ge(mods_landed[0], e * 16 + 16 * (MOD1 // 2 + 1))
                        w = mods[:, 0].rearrange("p (k n) -> p k n", k=KD)
                        for k in range(KD):
                            for s in range(2):
                                c = cond[:, 8 + 8 * s + k:9 + 8 * s + k]
                                if k == 0:
                                    i = TS(part2[:, s], w[:, k], c, None, ALU.mult)
                                else:
                                    dve.wait_ge(*at(("moe", "pstep", k - 1, s)))
                                    i = STT(part2[:, s], w[:, k], c, part2[:, s], ALU.mult, ALU.add)
                                i.then_inc(*mark("shared_parts", ("moe", "pstep", k, s), *([("moe", "part")] if k == KD - 1 and s else [])))
                    for h in range(2):
                        for which, dst, ci in (("g", gbuf, 4 * h + 1), ("u", ubuf, 4 * h + 3)):
                            dve.wait_ge(*at((tag, "chunk", ci)))
                            g = 2 * h + (which == "u")
                            if tag == "moe" and g == 3:
                                dve.wait_ge(*at((tag, "mod2")))
                                V.tensor_copy(mod2w[:, bass.ds(e * (2 * MODF), 2 * MODF)], ps[:, 3, 4 * CAP:4 * CAP + 2 * MODF]).then_inc(*mark("modulation_read"))
                            for j in range(4):
                                f = (4 * h + j) + (8 if which == "u" else 0)
                                i = TS(dst[:, h, j * CAP:(j + 1) * CAP], ps[:, g, j * CAP:(j + 1) * CAP],
                                       bgu[:, f:f + 1], LIMIT, ALU.add, ALU.min)
                            i.then_inc(*mark("products_read", (tag, "h", g)))
                        dve.wait_ge(*last("products_read"))
                        TS(ubuf[:, h], ubuf[:, h], -LIMIT, 1.0, ALU.max, ALU.add).then_inc(*mark("vector_steps"))
                        dve.wait_ge(*last("vector_steps"))
                        dve.wait_ge(*at((tag, "sig", h)))
                        TT_(gbuf[:, h], gbuf[:, h], sbuf_g[:, h], ALU.mult).then_inc(*mark("vector_steps"))
                        dve.wait_ge(*last("vector_steps"))
                        TT_(actb[:, 4 * h:4 * h + 4, :].rearrange("p j c -> p (j c)"), gbuf[:, h], ubuf[:, h], ALU.mult).then_inc(*mark("hidden_ready", (tag, "act", h)))
                    gathered((tag, "g"), (tag, "xT"))
                    summed((tag, "s"), (tag, "y+"))
                summed(("s_end", tag), ("y_end", tag))

            experts("moe")
            dve.wait_ge(*at("flag"))
            over = nc.vector.value_load(flag[0:1, 0:1], min_val=0, max_val=1)
            with nc.vector.If(over > 0):
                K.prefix = "spill_"
                for p in range(1, NPASS):
                    TS(slot[:, :, :], slot[:, :, :], -float(CAP), None, ALU.add).then_inc(*mark("vector_steps"))
                    dve.wait_ge(*last("vector_steps"))
                    experts(f"moe{p}")
                dve.wait_ge(*last("sums_updated"))
                K.prefix = ""
            dve.wait_ge(*last("sums_updated"))
            for k in range(KD):
                i = TS(yacc[:, k, :], yacc[:, k, :], mod[:, 40 + k:41 + k], None, ALU.mult)
            i.then_inc(*mark("gated", "yg"))
            for t in range(TT):
                for g in range(2):
                    dve.wait_ge(*at(("full", ("moeT", t, g))))
                    xs = x[:, t, 512 * g:512 * g + 512]
                    TT_(xs, xs, ps[:, B(("moeT", t, g)), :], ALU.add).then_inc(*mark("x_updated", ("drained", ("moeT", t, g)), *([("x2", t)] if g == 1 else [])))

            for t in range(TT):
                normalise("L0", "n1", t, "xn")
            for l in range(LAYERS):
                nt = 4 if l == 0 else 2
                ns = nt // 2
                N = nt * P
                L = f"L{l}"
                dve.wait_ge(*last("modulation_read"))
                for s in range(2):
                    TT_(modb[:, s, :], mod2[:, l, s, :], col(("ada_b", l), 0, 48), ALU.add).then_inc(*mark("vector_steps"))
                    dve.wait_ge(*last("vector_steps"))
                for s in range(2):
                    STT(aff[:, 0 + s], modb[:, s, 8:16], 1.0, col(("mix_pre", l), 0, 8), ALU.add, ALU.mult).then_inc(*mark("vector_steps"))
                    dve.wait_ge(*last("vector_steps"))
                    STT(aff[:, 2 + s], modb[:, s, 32:40], 1.0, col(("ffn_pre", l), 0, 8), ALU.add, ALU.mult).then_inc(*mark("vector_steps"))
                    dve.wait_ge(*last("vector_steps"))
                    TT_(aff[:, 4 + s], modb[:, s, 16:24], col(("mix_post", l), 0, 8), ALU.mult).then_inc(*mark("vector_steps"))
                    dve.wait_ge(*last("vector_steps"))
                    TT_(aff[:, 6 + s], modb[:, s, 40:48], col(("ffn_post", l), 0, 8), ALU.mult).then_inc(*mark("vector_steps"))
                    dve.wait_ge(*last("vector_steps"))

                def modulate2(name, n, A, sh):
                    for k in range(KD):
                        dve.wait_ge(*at(("full", (L, name, k))))
                        for s in range(n // 2):
                            i = TS(hT[:, k, s * SEQ:(s + 1) * SEQ], ps[:, B((L, name, k)), s * SEQ:(s + 1) * SEQ],
                                   aff[:, A + s, k:k + 1], modb[:, s, sh + k:sh + k + 1], ALU.mult, ALU.add)
                        i.then_inc(*mark("modulated", ("drained", (L, name, k))))
                modulate2("h", 4, 0, 0)
                V.memset(glp[:, :, :, 0:PADT], 0.0).then_inc(*mark("vector_steps"))
                dve.wait_ge(*last("vector_steps"))
                V.memset(glp[:, :, :, SEQ + PADT:SEGW], 0.0).then_inc(*mark("vector_steps"))
                dve.wait_ge(*last("vector_steps"))
                segs = lambda a: a.rearrange("p (s q) -> p s q", s=ns)
                for k in range(KD):
                    ka, kb = ((L, "cg"), 2 * k), ((L, "cg"), 2 * k + 1)
                    dve.wait_ge(*at(("full", ka)))
                    dve.wait_ge(*at(("drained", kb)))
                    TT_(glp[:, k, 0:ns, PADT:PADT + SEQ], segs(ps[:, B(ka), 0:N]), segs(tmp[:, k % 4, 0:N]), ALU.mult).then_inc(*mark("products_taken", ("drained", ka)))
                dve.wait_ge(*last("products_taken"))

                def conv():
                    w = lambda k, tap: col(("conv_w", l), tap * 8 + k)
                    for k0 in range(0, KD, 2):
                        for tap in range(TAPS):
                            for k in (k0, k0 + 1):
                                src = glp[:, k, 0:ns, tap:tap + SEQ]
                                dst = segs(cv[:, k, 0:N])
                                if tap == 0:
                                    i = TS(dst, src, w(k, 0), col(("conv_b", l), k), ALU.mult, ALU.add)
                                else:
                                    dve.wait_ge(*at((L, "tap", k, tap - 1)))
                                    i = STT(dst, src, w(k, tap), dst, ALU.mult, ALU.add)
                                i.then_inc(*mark("conv_taps", (L, "tap", k, tap), *([(L, "cv", k)] if tap == TAPS - 1 else [])))
                                yield
                taps = conv()

                def fill(n):
                    for _ in range(n):
                        if next(taps, 0) == 0:
                            return

                def gelu(items):
                    for n in range(len(items) + 1):
                        if n < len(items):
                            key, dst, w_ = items[n]
                            tb = tmp[:, n % 4, 0:w_]
                            dve.wait_ge(*at(("sq", key)))
                            TS(tb, tb, 0.044715, 1.0, ALU.mult, ALU.add).then_inc(*mark("vector_steps"))
                            dve.wait_ge(*last("vector_steps"))
                            TT_(tb, tb, ps[:, B(key), 0:w_], ALU.mult).then_inc(*mark("cubics_ready", ("cub", key)))
                            fill(4)
                        if n:
                            key, dst, w_ = items[n - 1]
                            dve.wait_ge(*at(("gs", key)))
                            TT_(dst, tmp[:, (n - 1) % 4, 0:w_], ps[:, B(key), 0:w_], ALU.mult).then_inc(*mark("products_taken", ("drained", key)))
                            if n < len(items):
                                fill(3)
                gelu(gelu_items(l))
                dve.wait_ge(*last("products_taken"))
                r = rstd_of((L, "gv"), nt, D)
                for t in range(nt):
                    i = TS(gv[:, t, :], gv[:, t, :], r[:, t:t + 1], None, ALU.mult)
                i.then_inc(*mark("normed", (L, "gvn")))
                for f in range(KD):
                    dve.wait_ge(*at(("full", (L, "sv", f))))
                    b = B((L, "sv", f))
                    bs = rows[:, ROW["bs"] + 512 * l + 128 * (f // 2):ROW["bs"] + 512 * l + 128 * (f // 2) + 128]
                    tl = lambda a: a.rearrange("p (t q) -> p t q", q=P)
                    STT(tl(tmp[:, 4 + f % 2, 0:N]), tl(ps[:, b, 0:N]), col(("gmlp_norm", l), f),
                             bs.unsqueeze(1).to_broadcast([P, nt, P]), ALU.mult, ALU.add).then_inc(*mark("vector_steps", ("drained", (L, "sv", f))))
                    dve.wait_ge(*last("vector_steps"))
                    TT_(uT[:, f, 0:N], tmp[:, 4 + f % 2, 0:N], uT[:, f, 0:N], ALU.mult).then_inc(*mark("gated", (L, "usv", f)))

                def take(br, first, nfill):
                    for f in range(KD):
                        key = ((L, "out", br), f)
                        dve.wait_ge(*at(("full", key)))
                        dve.wait_ge(*at(("drained", ((L, "gate", br), f))))
                        if first:
                            TT_(merged[:, f, 0:N], ps[:, B(key), 0:N], tmp[:, f % 4, 0:N], ALU.mult).then_inc(*mark("products_taken", ("drained", key)))
                        else:
                            if f >= 4:
                                dve.wait_ge(*at((L, "added", br, f - 4)))
                            TT_(tmp[:, 4 + f % 4, 0:N], ps[:, B(key), 0:N], tmp[:, f % 4, 0:N], ALU.mult).then_inc(*mark("products_taken", ("drained", key)))
                        fill(nfill)
                take("gmlp", True, 14)

                def head_norm(g, t):
                    key = ((L, "qkv", g), t)
                    nh = 4 if g < 2 else 2
                    w_ = nh * P
                    gains = rows[:, ROW["qk"] + 256 * l + 128 * (g == 2):ROW["qk"] + 256 * l + 128 * (g == 2) + 128]
                    hv = lambda a: a.rearrange("p (h d) -> p h d", d=P)
                    dve.wait_ge(*at(("sq", key)))
                    V.tensor_reduce(stat((key, "ssq"), 4)[:, 0:nh], hv(scr[:, t % 2, 0:w_]), AX, ALU.add).then_inc(*mark("vector_steps", ("ssq", key)))
                    dve.wait_ge(*last("vector_steps"))
                    if g < 2:
                        fill(1)
                    r = rstd_of(key, nh, HD2)
                    if g == 2:
                        dve.wait_ge(*at(("vcopied", key)))
                    qn = scr[:, 2, 0:w_]
                    TT_(hv(qn), hv(ps[:, B(key), 0:w_]), r.unsqueeze(2).to_broadcast([P, nh, P]), ALU.mult).then_inc(*mark("vector_steps", ("drained", key)))
                    dve.wait_ge(*last("vector_steps"))
                    if g == 2:
                        dst = tmp[:, 4 + t, 0:w_]
                    else:
                        dst = tmp[:, t, 0:w_]
                        if g:
                            dve.wait_ge(*at(("full", (L, "q", g - 1, t))))
                    ready = (L, "kr", t) if g == 2 else (L, "qr", g, t)
                    gb = gains.unsqueeze(1).to_broadcast([P, nh, P])
                    if t >= TT:
                        TT_(hv(dst), hv(qn), gb, ALU.mult).then_inc(*mark("normed", ready))
                    else:
                        TT_(hv(qn), hv(qn), gb, ALU.mult).then_inc(*mark("vector_steps"))
                        dve.wait_ge(*last("vector_steps"))
                        c_ = con("cos", 64, 64 * t).unsqueeze(1).to_broadcast([P, 2 * nh, 64])
                        halves = lambda a: a.rearrange("p (h d) -> p h d", d=64)
                        two = lambda a: a.rearrange("p (h b d) -> p b h d", b=2, d=64)
                        TT_(halves(dst), halves(qn), c_, ALU.mult).then_inc(*mark("vector_steps"))
                        dve.wait_ge(*last("vector_steps"))
                        for b2 in range(2):
                            s_ = con("sin", 64, 128 * t + 64 * b2).unsqueeze(1).to_broadcast([P, nh, 64])
                            TT_(two(scr[:, 3, 0:w_])[:, b2], two(qn)[:, 1 - b2], s_, ALU.mult).then_inc(*mark("vector_steps"))
                            dve.wait_ge(*last("vector_steps"))
                        TT_(dst, dst, scr[:, 3, 0:w_], ALU.add).then_inc(*mark("normed", ready))
                    dve.wait_ge(*last("normed"))
                    if g < 2:
                        fill(2)
                for g in range(3):
                    for t in range(4 if g == 2 else nt):
                        head_norm(g, t)
                for t in range(4):
                    dve.wait_ge(*at(("full", (L, "k", t))))
                    V.tensor_copy(kT[:, :, t * P:(t + 1) * P],
                                       ps[:, B((L, "k", t)), 0:256].rearrange("p (h q) -> p h q", h=2)).then_inc(*mark("turned_read", ("drained", (L, "k", t))))

                units = units_of[l]
                for n in range(len(units)):
                    if n < len(units):
                        h, seg = units[n]
                        key = (L, h, seg)
                        nk = 4 if seg == 0 else 2
                        for t in range(TT):
                            dve.wait_ge(*at(("full", (key, "s", t))))
                            V.tensor_reduce(stat(("nm", n % 2, t)), ps[:, B((key, "s", t)), 0:nk * P], AX, ALU.max, negate=True).then_inc(*mark("maxima_ready", (key, "nm", t)))
                        for t in range(TT):
                            dve.wait_ge(*at(("drained", (key, "s", t))))
                            V.reciprocal(stat(("rden", t)), stat(("den", n % 2, t))).then_inc(*mark("vector_steps"))
                            dve.wait_ge(*last("vector_steps"))
                            if n >= 2:
                                dve.wait_ge(*at(("full", ((L,) + units[n - 2], "pt", t))))
                            TS(tmp[:, 2 * (n % 2) + t, 0:nk * P], tmp[:, 4 + 2 * (n % 2) + t, 0:nk * P], stat(("rden", t)), None,
                                    ALU.mult).then_inc(*mark("vector_steps", (key, "p", t)))
                            dve.wait_ge(*last("vector_steps"))
                    fill(1)
                def take_one(br, f):
                    key = ((L, "out", br), f)
                    dve.wait_ge(*at(("full", key)))
                    dve.wait_ge(*at(("drained", ((L, "gate", br), f))))
                    if f >= 4:
                        dve.wait_ge(*at((L, "added", br, f - 4)))
                    TT_(tmp[:, 4 + f % 4, 0:N], ps[:, B(key), 0:N], tmp[:, f % 4, 0:N], ALU.mult).then_inc(*mark("products_taken", ("drained", key)))
                for f in range(4):
                    take_one("attn", f)
                    fill(6)
                fill(1000)
                dve.wait_ge(*at(("full", (L, "mu"))))
                TS(scr[:, 0, 0:N], ps[:, B((L, "mu")), 0:N], 1.0 / D, None, ALU.mult).then_inc(*mark("vector_steps", ("drained", (L, "mu"))))
                dve.wait_ge(*last("vector_steps"))
                for k in range(KD):
                    TT_(cv[:, k, 0:N], cv[:, k, 0:N], scr[:, 0, 0:N], ALU.subtract).then_inc(*mark("centred", (L, "cvc", k)))

                for f in range(4, KD):
                    take_one("attn", f)
                dve.wait_ge(*at(("full", (L, "var"))))
                TS(scr[:, 1, 0:N], ps[:, B((L, "var")), 0:N], 1.0 / D, EPS, ALU.mult, ALU.add).then_inc(*mark("vector_steps", ("drained", (L, "var")), ("ms", (L, "cvn"))))
                dve.wait_ge(*last("vector_steps"))
                dve.wait_ge(*at(("root", (L, "cvn"))))
                V.reciprocal(scr[:, 1, 0:N], scr[:, 1, 0:N]).then_inc(*mark("vector_steps"))
                dve.wait_ge(*last("vector_steps"))
                for k in range(KD):
                    TT_(cv[:, k, 0:N], cv[:, k, 0:N], scr[:, 1, 0:N], ALU.mult).then_inc(*mark("vector_steps"))
                    dve.wait_ge(*last("vector_steps"))
                    TS(cv[:, k, 0:N], cv[:, k, 0:N], col(("conv_g", l), k), col(("conv_nb", l), k), ALU.mult, ALU.add).then_inc(*mark("normed", (L, "cvz", k)))
                    if k:
                        dve.wait_ge(*at((L, "cvs", k - 1)))
                        TT_(cv[:, k - 1, 0:N], cv[:, k - 1, 0:N], scr[:, 2 + (k - 1) % 2, 0:N], ALU.mult).then_inc(*mark("silu_ready", (L, "cvn", k - 1)))
                dve.wait_ge(*at((L, "cvs", KD - 1)))
                TT_(cv[:, KD - 1, 0:N], cv[:, KD - 1, 0:N], scr[:, 2 + (KD - 1) % 2, 0:N], ALU.mult).then_inc(*mark("silu_ready", (L, "cvn", KD - 1)))
                def diagonals(which):
                    for s in range(ns):
                        for k in range(KD):
                            TS(dgb[which][:, KD * s + k], ident, aff[:, 4 + 2 * which + s, k:k + 1], None, ALU.mult).then_inc(*mark("diagonals", (L, "dg", which, s, k)))
                diagonals(0)
                for f in range(KD):
                    if f < 4:
                        dve.wait_ge(*at((L, "added", "attn", f + 4)))
                    take_one("conv", f)

                def residual(which, t, ready):
                    r = rstd_of(((L, "y", which), t), 1, D)
                    for g in range(2):
                        dve.wait_ge(*at(("drained", (L, "bc", which, t // 2, g))))
                    STT(yb[:, t, :], yb[:, t, :], r, bcv[:, t // 2, :], ALU.mult, ALU.mult).then_inc(*mark("vector_steps"))
                    dve.wait_ge(*last("vector_steps"))
                    dst = x[:, t, :] if t < TT else ctxr[:, t - TT, :]
                    TT_(dst, dst, yb[:, t, :], ALU.add).then_inc(*mark("x_updated", (L, ready, t)))
                    dve.wait_ge(*last("x_updated"))
                for t in range(nt):
                    residual(0, t, "x1")
                    normalise(L, "n2", t, "xn2")
                modulate2("h2", nt, 2, 24)
                diagonals(1)
                for hf in range(2):
                    if hf:
                        dve.wait_ge(*at(("full", ((L, "ff2", 0, 1), nt - 1))))
                    for j in range(16):
                        key = ((L, "ff1", hf), j)
                        dve.wait_ge(*at(("drained", key)))
                        TT_(hid[:, j, 0:N], tmp[:, j % 8, 0:N], tmp[:, j % 8, 0:N], ALU.mult).then_inc(*mark("hidden_ready", (L, "hid", hf, j)))
                for g in range(2):
                    for t in range(nt):
                        key = ((L, "ff2", 1, g), t)
                        dve.wait_ge(*at(("full", key)))
                        dve.wait_ge(*at(("drained", ((L, "ff2", 0, g), t))))
                        ys = yb[:, t, 512 * g:512 * g + 512]
                        TT_(ys, ys, ps[:, B(key), :], ALU.add).then_inc(*mark("products_taken", ("drained", key)))
                        if g == 1:
                            residual(1, t, "x2")
                            if l + 1 < LAYERS:
                                normalise(f"L{l + 1}", "n1", t, "xn")

        @block.scalar
        def _(act):
            A = nc.scalar.activation

            def B(key):
                return bank_of[key]
            head, tri = COL["mix_pre", 0], CST["tri"]
            for dst, src, name in ((cols[:, 0:head], cols_d[:, 0:head], "cols"), (x[:, :, :], x_d, "x"),
                                   (cst[:, 0:tri], cst_d[:, 0:tri], "cst")):
                act.dma_start(dst, src).then_inc(*mark("load_" + name, name, inc=16))

            def sumsq(key, tiles, junk, ready=()):
                for r in ready:
                    act.wait_ge(*at(r))
                for t, src in enumerate(tiles):
                    i = A(junk, src, ACT.Square, accum_out=stat((key, "ssq"), len(tiles))[:, t:t + 1])
                    i.then_inc(*mark("squares_summed", *([("ssq", key)] if t == len(tiles) - 1 else [])))
                    act.wait_ge(*last("squares_summed"))
                root(key, len(tiles))

            def root(key, n):
                act.wait_ge(*at(("ms", key)))
                A(stat((key, "rt"), n), stat((key, "ms"), n), ACT.Sqrt).then_inc(*mark("roots_ready", ("root", key)))

            act.wait_ge(*at("cols"))
            A(cond[:, :], col("cond", 0, 24), ACT.Sigmoid).then_inc(*mark("sigmoids", "cond_sig"))
            act.wait_ge(*at("x"))
            sumsq("x1", [x[:, t, :] for t in range(TT)], junk1b)
            act.wait_ge(*at(("part", EARLY - 1)))
            for dst, src, name in ((rows[:, :], rows_d.partition_broadcast(P), "rows"),
                                   (cst[:, tri:], cst_d[:, tri:], "tables"), (cols[:, head:], cols_d[:, head:], "more_cols"),
                                   (wr[:, :, :], wr_d, "wr"), (bdn[0:NE, :], bd_d, "bdn"), (ws[:, :, :, :], ws_d, "ws")):
                act.dma_start(dst, src).then_inc(*mark("load_" + name, name, inc=16))
            act.wait_ge(*at("ldot"))
            A(stat("lexp", 2), stat("ldot", 2), ACT.Exp).then_inc(*mark("exps_ready", "lexp"))
            for g in range(6):
                for t in range(TT):
                    act.wait_ge(*at(("full", (("proj", g), t))))
                    A(proj[:, t, 512 * g:512 * g + 512], ps[:, B((("proj", g), t)), :], ACT.Identity).then_inc(*mark("products_copied", ("drained", (("proj", g), t))))
                if g in (2, 3, 4, 5):
                    root(("qk", g - 2), 16)
            heads1 = [("A", h) for h in range(A_HEADS)] + [("B", h) for h in range(B_HEADS)]

            def turned_prob(n):
                key = heads1[n]
                act.wait_ge(*at(("full", ("pt",) + key)))
                if n >= 2:
                    act.wait_ge(*at(("full", ("o",) + heads1[n - 2])))
                A(sbuf_pt[:, key[1] % 2], ps[:, B(("pt",) + key), 0:384], ACT.Identity).then_inc(*mark("turned_copied", ("drained", ("pt",) + key)))

            for h in range(A_HEADS):
                if h:
                    turned_prob(h - 1)
                act.wait_ge(*at(("nm", ("A", h))))
                for t in range(TT):
                    sl = slice(P * t, P * t + P * (t + 1))
                    i = A(sbuf_e[:, h % 4, sl], sbuf_s[:, h % 2, sl], ACT.Exp, bias=stat((("A", h), "nm"), 2)[:, t:t + 1])
                i.then_inc(*mark("exps_ready", ("exp", ("A", h))))
            turned_prob(A_HEADS - 1)
            for h in range(B_HEADS):
                if h:
                    turned_prob(A_HEADS + h - 1)
                for c in range(2):
                    key = ("B", h, c)
                    act.wait_ge(*at(("nm", key)))
                    for t in range(TT):
                        sl = slice(P * t, P * t + P * (t + 1))
                        i = A(sbuf_e[:, 2 * (h % 2) + c, sl], sbuf_s[:, c, sl], ACT.Exp, bias=stat((key, "nm"), 2)[:, t:t + 1],
                              accum_out=stat((key, "den"), 2)[:, t:t + 1])
                    i.then_inc(*mark("exps_ready", ("exp", key)))
            turned_prob(A_HEADS + B_HEADS - 1)
            root("oB", 8)
            act.wait_ge(*at(("full", ("ada", EARLY + A_HEADS + 1))))
            act.dma_start(ctxr[:, :, :], ctx_d).then_inc(*mark("load_ctx", "ctx", inc=16))
            sumsq("x2", [x[:, t, :] for t in range(TT)], junk1b, ["x1"])
            for t in range(TT):
                act.wait_ge(*at(("gdiff", t)))
                A(gex[:, t, 0:TOPK], gex[:, t, 0:TOPK], ACT.Exp, accum_out=stat(("gsum", t))).then_inc(*mark("exps_ready", ("gexp", t)))

            act.wait_ge(*at("ctx"))
            for t in range(TT):
                sumsq((("L0", "n1"), TT + t), [ctxr[:, t, :]], junk1b)

            def experts(tag):
                for name in ("selection_ready", "outputs_ready"):
                    A(stat(("primer", tag, name)), stat(("x1", "rt"), TT)[:, 0:1], ACT.Identity).then_inc(*mark(name))
                with K.loop(act, tag, NE):
                    for h in range(2):
                        act.wait_ge(*at((tag, "h", 2 * h)))
                        A(sbuf_g[:, h], gbuf[:, h], ACT.Sigmoid, scale=ALPHA).then_inc(*mark("sigmoids", (tag, "sig", h)))
                    act.wait_ge(*at((tag, "selT")))
                    A(selgT[0:CAP, :], ps[0:CAP, 0, 0:SEQ], ACT.Identity).then_inc(*mark("selection_ready", (tag, "selgT")))
                    for g in range(2):
                        act.wait_ge(*at((tag, "chunk", 9 + 2 * g)))
                        A(ysb[0:CAP, 512 * g:512 * g + 512], ps[0:CAP, 6 + g, :], ACT.Identity).then_inc(*mark("outputs_ready", (tag, "y", g)))
            experts("moe")
            act.wait_ge(*at("flag"))
            over = nc.scalar.value_load(flag[0:1, 0:1], min_val=0, max_val=1)
            with nc.scalar.If(over > 0):
                K.prefix = "spill_"
                for p in range(1, NPASS):
                    experts(f"moe{p}")
                K.prefix = ""

            for l in range(LAYERS):
                nt = 4 if l == 0 else 2
                ns = nt // 2
                N = nt * P
                L = f"L{l}"
                rowsx = [x[:, t, :] for t in range(TT)] + [ctxr[:, t, :] for t in range(TT)]
                if l == 0:
                    for t in range(TT):
                        sumsq((("L0", "n1"), t), rowsx[t:t + 1], junkb, [("x2", t)])
                for k in range(KD):
                    kb = ((L, "cg"), 2 * k + 1)
                    act.wait_ge(*at(("full", kb)))
                    if k >= 4:
                        act.wait_ge(*at(("drained", ((L, "cg"), 2 * k - 8))))
                    A(tmp[:, k % 4, 0:N], ps[:, B(kb), 0:N], ACT.Sigmoid).then_inc(*mark("gates_ready", ("drained", kb)))
                items = gelu_items(l)

                def gv_squares(n):
                    t = n - (len(items) - nt)
                    if t >= 0:
                        act.wait_ge(*at(("drained", items[n][0])))
                        A(junkb, gv[:, t, :], ACT.Square, accum_out=stat(((L, "gv"), "ssq"), nt)[:, t:t + 1]).then_inc(*mark("squares_summed", *([("ssq", (L, "gv"))] if t == nt - 1 else [])))
                        act.wait_ge(*last("squares_summed"))

                for n in range(len(items) + 1):
                    if n < len(items):
                        key, dst, w_ = items[n]
                        act.wait_ge(*at(("full", key)))
                        act.wait_ge(*at(("drained", items[n - 4][0]) if n >= 4 else ("drained", ((L, "cg"), 8 + 2 * n))))
                        A(tmp[:, n % 4, 0:w_], ps[:, B(key), 0:w_], ACT.Square).then_inc(*mark("squares_ready", ("sq", key)))
                    if n:
                        key, dst, w_ = items[n - 1]
                        act.wait_ge(*at(("cub", key)))
                        A(tmp[:, (n - 1) % 4, 0:w_], tmp[:, (n - 1) % 4, 0:w_], ACT.Sigmoid, scale=GELU_C).then_inc(*mark("sigmoids", ("gs", key)))
                    if n >= 2:
                        gv_squares(n - 2)
                gv_squares(len(items) - 1)
                root((L, "gv"), nt)

                def gates(br, fs, prev):
                    for f in fs:
                        key = ((L, "gate", br), f)
                        act.wait_ge(*at(("full", key)))
                        act.wait_ge(*at(("drained", ((L, "out", br), f - 4)) if f >= 4 else prev(f)))
                        A(tmp[:, f % 4, 0:N], ps[:, B(key), 0:N], ACT.Sigmoid).then_inc(*mark("gates_ready", ("drained", key)))
                gates("gmlp", range(KD), lambda f: ("drained", items[len(items) - 4 + f][0]))
                for g in range(3):
                    for t in range(4 if g == 2 else nt):
                        key = ((L, "qkv", g), t)
                        w_ = 512 if g < 2 else 256
                        act.wait_ge(*at(("full", key)))
                        A(scr[:, t % 2, 0:w_], ps[:, B(key), 0:w_], ACT.Square).then_inc(*mark("squares_ready", ("sq", key)))
                        if g == 2:
                            A(vb[:, t, :], ps[:, B(key), 256:512], ACT.Identity).then_inc(*mark("values_ready", ("vcopied", key)))
                        root(key, 4 if g < 2 else 2)
                    for t in range(nt if g else 0):
                        act.wait_ge(*at(("full", (L, "q", g - 1, t))))
                        A(uT[:, 4 * g - 4:4 * g, t * P:(t + 1) * P],
                               ps[:, B((L, "q", g - 1, t)), :].rearrange("p (h q) -> p h q", h=4), ACT.Identity).then_inc(*mark("turned_copied", ("drained", (L, "q", g - 1, t))))
                units = units_of[l]
                for n in range(len(units) + 2):
                    if n < len(units):
                        h, seg = units[n]
                        key = (L, h, seg)
                        nk = 4 if seg == 0 else 2
                        for t in range(TT):
                            act.wait_ge(*at((key, "nm", t)))
                            if n >= 2:
                                act.wait_ge(*at(((L,) + units[n - 2], "p", t)))
                            A(tmp[:, 4 + 2 * (n % 2) + t, 0:nk * P], ps[:, B((key, "s", t)), 0:nk * P], ACT.Exp,
                                   bias=stat(("nm", n % 2, t)), accum_out=stat(("den", n % 2, t))).then_inc(*mark("exps_ready", ("drained", (key, "s", t))))
                    if 1 <= n <= len(units):
                        h, seg = units[n - 1]
                        key = (L, h, seg)
                        nk = 4 if seg == 0 else 2
                        for t in range(TT):
                            act.wait_ge(*at(("full", (key, "pt", t))))
                            if n >= 3:
                                act.wait_ge(*at(("full", ((L,) + units[n - 3], "o"))))
                            A(ptb[(n - 1) % 2][:, 0:nk, t * P:(t + 1) * P],
                                   ps[:, B((key, "pt", t)), 0:nk * P].rearrange("p (j q) -> p j q", j=nk), ACT.Identity).then_inc(*mark("turned_copied", ("drained", (key, "pt", t))))
                    if n >= 2:
                        h, seg = units[n - 2]
                        key = (L, h, seg)
                        act.wait_ge(*at(("full", (key, "o"))))
                        A(uT[:, h, seg * SEQ:(seg + 1) * SEQ], ps[:, B((key, "o")), 0:SEQ], ACT.Identity).then_inc(*mark("heads_read", ("drained", (key, "o"))))
                gates("attn", range(4), lambda f: ("full", ((L,) + units[len(units) - 2 + f // 2], "pt", f % 2)))
                for k in range(KD):
                    act.wait_ge(*at((L, "cvc", k)))
                    A(glsq[:, k, 0:N], cv[:, k, 0:N], ACT.Square).then_inc(*mark("squares_ready", (L, "cvsq", k)))
                gates("attn", range(4, KD), None)
                act.wait_ge(*at(("ms", (L, "cvn"))))
                A(scr[:, 1, 0:N], scr[:, 1, 0:N], ACT.Sqrt).then_inc(*mark("roots_ready", ("root", (L, "cvn"))))
                for k in range(KD):
                    act.wait_ge(*at((L, "cvz", k)))
                    if k >= 2:
                        act.wait_ge(*at((L, "cvn", k - 2)))
                    A(scr[:, 2 + k % 2, 0:N], cv[:, k, 0:N], ACT.Sigmoid).then_inc(*mark("sigmoids", (L, "cvs", k)))
                gates("conv", range(4), lambda f: ("drained", ((L, "out", "attn"), f + 4)))

                def spread(which):
                    for s in range(ns):
                        for g in range(2):
                            act.wait_ge(*at(("full", (L, "bc", which, s, g))))
                            A(bcv[:, s, 512 * g:512 * g + 512], ps[:, B((L, "bc", which, s, g)), :], ACT.Identity).then_inc(*mark("spread_copied", ("drained", (L, "bc", which, s, g))))
                spread(0)
                gates("conv", range(4, KD), None)
                for g in range(2):
                    for t in range(nt):
                        key = ((L, "wo", g), t)
                        act.wait_ge(*at(("full", key)))
                        A(yb[:, t, 512 * g:512 * g + 512], ps[:, B(key), :], ACT.Identity).then_inc(*mark("products_copied", ("drained", key)))
                        if g == 1:
                            act.wait_ge(*last("products_copied"))
                            sumsq(((L, "y", 0), t), [yb[:, t, :]], junkb)
                            sumsq(((L, "n2"), t), rowsx[t:t + 1], junkb, [(L, "x1", t)])
                for hf in range(2):
                    for j in range(16):
                        key = ((L, "ff1", hf), j)
                        act.wait_ge(*at(("full", key)))
                        if j >= 8:
                            act.wait_ge(*at((L, "hid", hf, j - 8)))
                        elif hf:
                            act.wait_ge(*at((L, "hid", 0, j + 8)))
                        A(tmp[:, j % 8, 0:N], ps[:, B(key), 0:N], ACT.Relu).then_inc(*mark("relus_ready", ("drained", key)))
                    if hf == 0:
                        spread(1)
                        for g in range(2):
                            for t in range(nt):
                                key = ((L, "ff2", 0, g), t)
                                act.wait_ge(*at(("full", key)))
                                A(yb[:, t, 512 * g:512 * g + 512], ps[:, B(key), :], ACT.Identity).then_inc(*mark("products_copied", ("drained", key)))
                for t in range(nt):
                    sumsq(((L, "y", 1), t), [yb[:, t, :]], junkb, [("drained", ((L, "ff2", 1, 1), t))])
                    if l + 1 < LAYERS:
                        sumsq(((f"L{l + 1}", "n1"), t), rowsx[t:t + 1], junkb, [(L, "x2", t)])

        @block.gpsimd
        def _(pool):
            for l in range(LAYERS):
                nt = 4 if l == 0 else 2
                N = nt * P
                L = f"L{l}"
                for br in ("attn", "conv"):
                    for f in range(KD):
                        pool.wait_ge(*at(("drained", ((L, "out", br), f))))
                        if br == "conv":
                            pool.wait_ge(*at((L, "added", "attn", f)))
                        nc.gpsimd.tensor_tensor(merged[:, f, 0:N], merged[:, f, 0:N], tmp[:, 4 + f % 4, 0:N], ALU.add).then_inc(*mark("branches_added", (L, "added", br, f), *([(L, "merged", f)] if br == "conv" else [])))

        @block.sync
        def _(sp):
            used = K.sem("weights_used")

            def load(c, slot_, sem):
                sp.dma_start(ring[:, slot_], stream[c].rearrange("p (k n) -> p k n", k=4)).then_inc(sem, 16)

            def one(c):
                if c >= RING:
                    sp.wait_ge(used, c - RING + 1)
                load(c, c % RING, landed[c % RING])

            def load_mod(g):
                if g >= 2:
                    sp.wait_ge(*at(("part", g - 2)))
                sp.dma_start(mods[:, g % 2], mods_d[g]).then_inc(mods_landed[g % 2], 16)

            end, cut = CH["total"], CH["after_moe"]
            for g in range(EARLY):
                load_mod(g)
            for c in range(CH["moe"]):
                one(c)
                for g in {6: (6, 7), 7: (8,), 8: (9, 10), 9: (11,), 10: (12,), 11: (13,), 12: (14,), 13: (15,)}.get(c, ()):
                    load_mod(g)
            if end > CH["moe"]:
                parts = K.sem("shared_parts")
                sp.wait_ge(*at(("part", MOD1 - 1)))
                def expert(e, first):
                    for ci in range(CPE):
                        if ci == CPE // 2:
                            if not first:
                                sp.wait_ge(parts, e * (2 * KD))
                            sp.dma_start(mods[:, 0], mods_d[e + MOD1]).then_inc(mods_landed[0], 16)
                        sp.wait_ge(used, e * CPE + (CH["moe"] + ci - RING + 1))
                        load(e * CPE + (CH["moe"] + ci), (CH["moe"] + ci) % RING, landed[(CH["moe"] + ci) % RING])
                expert(0, True)
                with sp.Fori(1, NE) as e:
                    expert(e, False)
            if end > cut:
                sp.wait_ge(*at("flag"))
                over = nc.sync.value_load(flag[0:1, 0:1], min_val=0, max_val=1)
                with nc.sync.If(over > 0):
                    sp.wait_ge(used, CH["after_moe"])
                    again = K.sem("spill_weights_used")
                    for ci in range(CPE):
                        if ci >= RING:
                            sp.wait_ge(again, ci - RING + 1)
                        s = (CH["moe"] + ci) % RING
                        load(CH["moe"] + ci, s, spill_landed[s])
                    for p in range(NPASS - 1):
                        with sp.Fori(0 if p else 1, NE) as e:
                            for ci in range(CPE):
                                sp.wait_ge(again, e * CPE + (CPE * NE * p + ci - RING + 1))
                                s = (CH["moe"] + ci) % RING
                                load(e * CPE + (CH["moe"] + ci), s, spill_landed[s])
                    sp.wait_ge(again, CPE * NE * (NPASS - 1))
            nxt_c = cut
            while nxt_c < end and nxt_c % RING:
                one(nxt_c)
                nxt_c += 1
            if nxt_c < end:
                full_ = end // RING
                with sp.Fori(nxt_c // RING, full_) as r:
                    for s in range(RING):
                        sp.wait_ge(used, r * RING + (s - RING + 1))
                        load(r * RING + s, s, landed[s])
                for c in range(full_ * RING, end):
                    one(c)
            for name in ("ws", "wr", "bdn", "ctx"):
                sp.wait_ge(*at(name))
            sp.wait_ge(*at(("L1", "x2", TT - 1)))
            sp.dma_start(out_d, x[:, :, :]).then_inc(*mark("stored", "out", inc=16))
            sp.wait_ge(K.sem("stored"), 16)
    return K


def _constants():
    c = np.zeros((P, CST["total"]), np.float32)
    p = np.arange(P)
    c[:, CST["ident"]:CST["ident"] + P] = np.eye(P)
    c[:, CST["ones"]:CST["ones"] + P] = 1
    c[:, CST["tri"]:CST["tri"] + P] = p[:, None] < p[None, :]
    c[:, CST["iota"]:CST["iota"] + CAP] = np.arange(CAP)
    c[:, CST["iotae"]:CST["iotae"] + NE] = np.arange(NE)
    freqs = HD2 // 4
    inv = np.float32(10000.0) ** (-np.arange(freqs, dtype=np.float32) / np.float32(freqs))
    tok = np.arange(SEQ)
    ang = np.concatenate([(tok // 64).astype(np.float32)[:, None] * inv, (tok % 64).astype(np.float32)[:, None] * inv], -1)
    cos, sin = np.cos(ang).astype(np.float32), np.sin(ang).astype(np.float32)
    for t in range(TT):
        c[:, CST["cos"] + 64 * t:CST["cos"] + 64 * t + 64] = cos[t * P:(t + 1) * P]
        c[:, CST["sin"] + 128 * t:CST["sin"] + 128 * t + 64] = -sin[t * P:(t + 1) * P]
        c[:, CST["sin"] + 128 * t + 64:CST["sin"] + 128 * t + 128] = sin[t * P:(t + 1) * P]
        d = (t * P + p)[:, None] - np.arange(P * (t + 1))[None, :]
        cnt = (((d >= 0) & (d <= 128)).astype(int) + ((d >= 0) & (d % 4 == 0)) + ((d >= 0) & (d % 16 == 0)))
        at = P * t
        c[:, CST["cnt"] + at:CST["cnt"] + at + d.shape[1]] = cnt
        c[:, CST["distA"] + at:CST["distA"] + at + d.shape[1]] = np.where(cnt > 0, d, 1e30)
        c[:, CST["distB"] + at:CST["distB"] + at + d.shape[1]] = np.where(d >= 0, d, 1e30)
    return c


def _chunks(w):
    k, n = w.shape
    return w.reshape(k // 512, 4, P, n // 512, 512).transpose(3, 0, 2, 1, 4).reshape(-1, P, 2048)


def kernel(**inputs):
    import concourse.bacc as bacc
    from concourse.bass_utils import run_bass_kernel_spmd as run

    a = {n: np.asarray(w) for n, w in inputs.items()}
    stream = np.empty((CH["total"], P, 2048), np.float32)

    def put(name, w):
        c = _chunks(w)
        at = name if isinstance(name, int) else CH[name]
        stream[at:at + len(c)] = c

    mods = np.concatenate([w.reshape(KD, P, 6 * D // MODW, MODW).transpose(2, 1, 0, 3).reshape(-1, P, KD * MODW)
                           for w in (a["w_ada"][0], a["ada_w_2"][0], a["ada_w_2"][1])])
    put("w_in", a["w_in"][0])
    put("w_out", a["w_out"][0])
    for e in range(NE):
        gu = a["w_gate_up"][0, e].reshape(D, 2, 2, 512).transpose(0, 2, 1, 3).reshape(D, 2 * D)
        put(CH["moe"] + CPE * e, gu)
        put(CH["moe"] + CPE * e + 8, a["w_down"][0, e])
    for l in range(LAYERS):
        w = a["w_in_2"][l]
        cg = w[:, 3584:5632].reshape(D, 2, KD, P).transpose(0, 2, 1, 3).reshape(D, 2 * D)
        put(("cg", l), cg)
        put(("gu", l), w[:, 1536:2560])
        put(("gv", l), w[:, 2560:3584])
        put(("qkv", l), w[:, 0:1536])
        for br, off, out in (("attn", 0, "w_attn_o_2"), ("gmlp", 1024, "w_gmlp_o_2"), ("conv", 2048, "w_conv_o_2")):
            for n in range(2):
                put(("gate", br, l, n), w[:, 5632 + off + 512 * n:5632 + off + 512 * n + 512])
                put(("out", br, l, n), a[out][l][:, 512 * n:512 * n + 512])
        put(("w_out", l), a["w_out_2"][l])
        for h in range(2):
            put(("ff1", l, h), a["w_ff1_2"][l][:, 2048 * h:2048 * h + 2048])
            put(("ff2", l, h), a["w_ff2_2"][l][2048 * h:2048 * h + 2048])

    column = {}

    def features(name, w):
        w = np.ascontiguousarray(w).reshape(-1, P).T
        columns[:, COL[name]:COL[name] + w.shape[1]] = w

    columns = np.zeros((P, COL["total"]), np.float32)
    features("cond", np.concatenate([a["c"].ravel(), a["c_2"].ravel(), a["c_ctx_2"].ravel()]))
    features("b_ada", a["b_ada"])
    features("norm1", a["norm1_g"])
    features("norm2", a["norm2_g"])
    features("qk_a", np.concatenate([a["a_q_norm_g"], a["a_q_norm_g"], a["a_k_norm_g"], a["a_k_norm_g"]], 0))
    features("qk_b", np.concatenate([a["b_q_norm_g"], a["b_q_norm_g"], a["b_k_norm_g"], a["b_k_norm_g"]], 0))
    features("diff", a["diff_norm_g"])
    features("b_gu", a["b_gate_up"][0])
    for l in range(LAYERS):
        for n, w in (("ada_b", "ada_b_2"), ("mix_pre", "mix_pre_g_2"), ("mix_post", "mix_post_g_2"),
                     ("gmlp_norm", "gmlp_norm_g_2"), ("conv_b", "conv_b_2"), ("conv_g", "conv_norm_g_2"),
                     ("conv_nb", "conv_norm_b_2"), ("ffn_pre", "ffn_pre_g_2"), ("ffn_post", "ffn_post_g_2"),
                     ("conv_w", "conv_w_2")):
            features((n, l), a[w][l])
    row = np.concatenate([a["lambda_q1"].ravel(), a["lambda_k1"].ravel(), a["lambda_q2"].ravel(), a["lambda_k2"].ravel()]
                         + [a[n][l].ravel() for l in range(LAYERS) for n in ("q_norm_g_2", "k_norm_g_2")]
                         + [a["gmlp_bs_2"].ravel(), a["b_router"].ravel()])
    arrays = {
        "stream": stream,
        "modulation": mods,
        "columns": columns,
        "row_vectors": row,
        "constants": _constants(),
        "x_tiles": np.ascontiguousarray(a["x"][0].reshape(TT, P, D).transpose(1, 0, 2)),
        "ctx_tiles": np.ascontiguousarray(a["ctx_2"][0].reshape(TT, P, D).transpose(1, 0, 2)),
        "spatial": np.ascontiguousarray(a["gmlp_ws_2"].transpose(3, 0, 1, 2)),
        "router": np.ascontiguousarray(a["w_router"][0].reshape(KD, P, NE).transpose(1, 0, 2)),
        "down_bias": np.ascontiguousarray(a["b_down"][0]),
    }

    def program(known, per):
        nc = bacc.Bacc("TRN2", target_bir_lowering=False, num_devices=1)
        args = [nc.dram_tensor(n, w.shape, F32, kind="ExternalInput").ap() for n, w in arrays.items()]
        args.append(nc.dram_tensor("out", (P, TT, D), F32, kind="ExternalOutput").ap())
        return nc, build(nc, args, known, per)

    _, first = program({}, {})
    nc, _ = program(first.marks, first.newper)
    got = run(nc, [arrays], core_ids=[0]).results[0]["out"]
    return got.transpose(1, 0, 2).reshape(1, SEQ, D)
```
